# Optimizing a Trainium2 kernel written in Bass

```python
import jax, jax.numpy as jnp
from jax import lax
import numpy as np

D_MODEL = 2048
BATCH = 1
SEQ = 256
DEPTH = 1

PLE_DIM = 256
EPS = 1e-6

SSM_HEAD_DIM = 64
SSM_INNER = D_MODEL
SSM_HEADS = SSM_INNER // SSM_HEAD_DIM
SSM_GROUPS = 4
SSM_STATE = 128
SSM_CONV = 4
SSM_CHUNK = 128
SSM_HPG = SSM_HEADS // SSM_GROUPS
SSM_CONV_CH = SSM_INNER + 2 * SSM_GROUPS * SSM_STATE

ATT_HEAD_DIM = 64
ATT_HEADS = D_MODEL // ATT_HEAD_DIM
ATT_KV_HEADS = ATT_HEADS // 4
ATT_REP = ATT_HEADS // ATT_KV_HEADS
ATT_INNER = ATT_HEADS * ATT_HEAD_DIM
ATT_KV_DIM = ATT_KV_HEADS * ATT_HEAD_DIM
WINDOW = 128
ROPE_THETA = 500000.0
ROPE_DIM = ATT_HEAD_DIM // 4

MIX_WIDTH = SSM_INNER + ATT_INNER
IN_WIDTH = SSM_INNER + SSM_CONV_CH + SSM_HEADS + ATT_INNER + 2 * ATT_KV_DIM

D_FF = 256 * ((8 * D_MODEL // 3 + 255) // 256)
FFN_CONV = 3


def _rmsnorm(x, g):
    xf = x.astype(jnp.float32)
    y = xf * lax.rsqrt(jnp.mean(xf * xf, axis=-1, keepdims=True) + EPS)
    return (y * g.astype(jnp.float32)).astype(x.dtype)

def _causal_dwconv(x, w, b):
    k = w.shape[0]
    y = lax.conv_general_dilated(x, w[:, None, :].astype(x.dtype), window_strides=(1,),
                                 padding=[(k - 1, 0)],
                                 dimension_numbers=('NWC', 'WIO', 'NWC'),
                                 feature_group_count=x.shape[-1])
    return y + b.astype(x.dtype)

def _ssd(xs, dt, a, bm, cm):
    b, s = xs.shape[0], xs.shape[1]
    nc, L = s // SSM_CHUNK, SSM_CHUNK
    G, E, P, N = SSM_GROUPS, SSM_HPG, SSM_HEAD_DIM, SSM_STATE
    X = (xs.astype(jnp.float32) * dt[..., None]).reshape(b, nc, L, G, E, P)
    a_dt = (dt * a).reshape(b, nc, L, G, E).transpose(0, 3, 4, 1, 2)
    Bc = bm.astype(jnp.float32).reshape(b, nc, L, G, N)
    Cc = cm.astype(jnp.float32).reshape(b, nc, L, G, N)
    a_cs = jnp.cumsum(a_dt, axis=-1)
    tril = jnp.tril(jnp.ones((L, L), dtype=bool))
    seg = a_cs[..., :, None] - a_cs[..., None, :]
    decay_in = jnp.exp(jnp.where(tril, seg, -jnp.inf))
    cb = jnp.einsum('bclgn,bcsgn->bgcls', Cc, Bc)
    y_diag = jnp.einsum('bgecls,bcsgep->bclgep', cb[:, :, None] * decay_in, X)
    decay_states = jnp.exp(a_cs[..., -1:] - a_cs)
    states = jnp.einsum('bclgn,bgecl,bclgep->bcgepn', Bc, decay_states, X)
    chunk_decay = jnp.exp(a_cs[..., -1])

    def step(h, inp):
        st, d = inp
        return h * d[..., None, None] + st, h

    h0 = jnp.zeros((b, G, E, P, N), jnp.float32)
    _, prev = lax.scan(step, h0, (jnp.moveaxis(states, 1, 0), jnp.moveaxis(chunk_decay, -1, 0)))
    prev = jnp.moveaxis(prev, 0, 1)
    y_off = jnp.einsum('bclgn,bcgepn,bgecl->bclgep', Cc, prev, jnp.exp(a_cs))
    return (y_diag + y_off).reshape(b, s, SSM_HEADS, P)

def _partial_rope(t, cos, sin):
    half = ROPE_DIM // 2
    t1, t2 = t[..., :half], t[..., half:ROPE_DIM]
    return jnp.concatenate([t1 * cos - t2 * sin, t2 * cos + t1 * sin, t[..., ROPE_DIM:]], axis=-1)

def _swa_sinks(q, k, v, sinks):
    b, s = q.shape[0], q.shape[1]
    blk = WINDOW
    nb = s // blk
    scale = ATT_HEAD_DIM ** -0.5
    qb = q.astype(jnp.float32).reshape(b, nb, blk, ATT_KV_HEADS, ATT_REP, ATT_HEAD_DIM)

    def band(t):
        tp = jnp.pad(t.astype(jnp.float32), ((0, 0), (blk, 0), (0, 0), (0, 0)))
        tp = tp.reshape(b, nb + 1, blk, ATT_KV_HEADS, ATT_HEAD_DIM)
        return jnp.concatenate([tp[:, :-1], tp[:, 1:]], axis=2)

    kb, vb = band(k), band(v)
    sc = jnp.einsum('bnqhrd,bnkhd->bnhrqk', qb, kb) * scale
    qi = jnp.arange(blk)[:, None]
    kj = jnp.arange(2 * blk)[None, :]
    diff = qi + blk - kj
    in_band = (diff >= 0) & (diff < WINDOW)
    valid = (jnp.arange(nb)[:, None] * blk + kj - blk) >= 0
    mask = in_band[None] & valid[:, None, :]
    sc = jnp.where(mask[None, :, None, None], sc, -jnp.inf)
    sink = sinks.astype(jnp.float32).reshape(ATT_KV_HEADS, ATT_REP)[None, None, :, :, None, None]
    m = jnp.maximum(jnp.max(sc, axis=-1, keepdims=True), sink)
    e = jnp.exp(sc - m)
    pr = e / (jnp.sum(e, axis=-1, keepdims=True) + jnp.exp(sink - m))
    o = jnp.einsum('bnhrqk,bnkhd->bnqhrd', pr, vb)
    return o.reshape(b, s, ATT_INNER).astype(q.dtype)

def first_inputs(seed: int = 0) -> dict:
    key = jax.random.key(seed)
    ks = jax.random.split(key, 24)
    f32 = jnp.float32
    nrm = lambda k, shape, sc: jax.random.normal(k, shape, f32) * sc
    gain = lambda k, shape: 1.0 + 0.02 * jax.random.normal(k, shape, f32)
    dt0 = jnp.exp(jax.random.uniform(ks[5], (DEPTH, SSM_HEADS), f32) * (np.log(0.1) - np.log(0.001)) + np.log(0.001))
    return {
        'x': nrm(ks[0], (BATCH, SEQ, D_MODEL), 1.0),
        'p': nrm(ks[1], (DEPTH, BATCH, SEQ, PLE_DIM), 1.0),
        'positions': jnp.broadcast_to(jnp.arange(SEQ, dtype=jnp.int32)[None, :], (BATCH, SEQ)),
        'attn_norm_g': gain(ks[2], (DEPTH, D_MODEL)),
        'w_in': nrm(ks[3], (DEPTH, D_MODEL, IN_WIDTH), D_MODEL ** -0.5),
        'conv_w': nrm(ks[4], (DEPTH, SSM_CONV, SSM_CONV_CH), SSM_CONV ** -0.5),
        'conv_b': nrm(ks[6], (DEPTH, SSM_CONV_CH), 0.02),
        'dt_bias': dt0 + jnp.log(-jnp.expm1(-dt0)),
        'a_log': jnp.log(jax.random.uniform(ks[7], (DEPTH, SSM_HEADS), f32, 1.0, 16.0)),
        'd_skip': gain(ks[8], (DEPTH, SSM_HEADS)),
        'ssm_norm_g': gain(ks[9], (DEPTH, SSM_INNER)),
        'q_norm_g': gain(ks[10], (DEPTH, ATT_HEAD_DIM)),
        'k_norm_g': gain(ks[11], (DEPTH, ATT_HEAD_DIM)),
        'sinks': nrm(ks[12], (DEPTH, ATT_HEADS), 0.5),
        'w_out': nrm(ks[13], (DEPTH, MIX_WIDTH, D_MODEL), MIX_WIDTH ** -0.5),
        'ffn_norm_g': gain(ks[14], (DEPTH, D_MODEL)),
        'w_up': nrm(ks[15], (DEPTH, D_MODEL, 2 * D_FF), D_MODEL ** -0.5),
        'ffn_conv_w': nrm(ks[16], (DEPTH, FFN_CONV, 2 * D_FF), FFN_CONV ** -0.5),
        'ffn_conv_b': nrm(ks[17], (DEPTH, 2 * D_FF), 0.02),
        'w_down': nrm(ks[18], (DEPTH, D_FF, D_MODEL), D_FF ** -0.5),
        'ple_norm_g': gain(ks[19], (DEPTH, D_MODEL)),
        'w_ple_gate': nrm(ks[20], (DEPTH, D_MODEL, D_MODEL), D_MODEL ** -0.5),
        'w_ple_proj': nrm(ks[21], (DEPTH, PLE_DIM, D_MODEL), PLE_DIM ** -0.5),
        'ple_post_g': gain(ks[22], (DEPTH, D_MODEL)),
    }

def first_block(x, p, positions, attn_norm_g, w_in, conv_w, conv_b, dt_bias, a_log, d_skip,
              ssm_norm_g, q_norm_g, k_norm_g, sinks, w_out, ffn_norm_g, w_up, ffn_conv_w,
              ffn_conv_b, w_down, ple_norm_g, w_ple_gate, w_ple_proj, ple_post_g):
    b, s = x.shape[0], x.shape[1]
    inv_freq = ROPE_THETA ** (-jnp.arange(0, ROPE_DIM, 2, dtype=jnp.float32) / ROPE_DIM)
    ang = positions.astype(jnp.float32)[..., None] * inv_freq
    cos = jnp.cos(ang)[:, :, None, :].astype(x.dtype)
    sin = jnp.sin(ang)[:, :, None, :].astype(x.dtype)
    o1 = SSM_INNER
    o2 = o1 + SSM_CONV_CH
    o3 = o2 + SSM_HEADS
    o4 = o3 + ATT_INNER
    o5 = o4 + ATT_KV_DIM
    h = x
    for i in range(DEPTH):
        a_in = _rmsnorm(h, attn_norm_g[i])
        proj = a_in @ w_in[i]
        z, xbc, dt_raw, q, k, v = jnp.split(proj, [o1, o2, o3, o4, o5], axis=-1)
        xbc = jax.nn.silu(_causal_dwconv(xbc, conv_w[i], conv_b[i]))
        xs, bm, cm = jnp.split(xbc, [SSM_INNER, SSM_INNER + SSM_GROUPS * SSM_STATE], axis=-1)
        dt = jax.nn.softplus(dt_raw.astype(jnp.float32) + dt_bias[i].astype(jnp.float32))
        a_neg = -jnp.exp(a_log[i].astype(jnp.float32))
        xs_h = xs.reshape(b, s, SSM_HEADS, SSM_HEAD_DIM)
        y = _ssd(xs_h, dt, a_neg, bm.reshape(b, s, SSM_GROUPS, SSM_STATE),
                 cm.reshape(b, s, SSM_GROUPS, SSM_STATE))
        y = y + d_skip[i].astype(jnp.float32)[:, None] * xs_h.astype(jnp.float32)
        y = y.reshape(b, s, SSM_INNER) * jax.nn.silu(z.astype(jnp.float32))
        y_ssm = _rmsnorm(y.reshape(b, s, SSM_GROUPS, SSM_INNER // SSM_GROUPS),
                         ssm_norm_g[i].reshape(SSM_GROUPS, SSM_INNER // SSM_GROUPS))
        y_ssm = y_ssm.reshape(b, s, SSM_INNER).astype(h.dtype)
        qh = _rmsnorm(q.reshape(b, s, ATT_HEADS, ATT_HEAD_DIM), q_norm_g[i])
        kh = _rmsnorm(k.reshape(b, s, ATT_KV_HEADS, ATT_HEAD_DIM), k_norm_g[i])
        qh = _partial_rope(qh, cos, sin)
        kh = _partial_rope(kh, cos, sin)
        vh = v.reshape(b, s, ATT_KV_HEADS, ATT_HEAD_DIM)
        y_att = _swa_sinks(qh, kh, vh, sinks[i])
        h = h + jnp.concatenate([y_ssm, y_att], axis=-1) @ w_out[i]
        u = _rmsnorm(h, ffn_norm_g[i]) @ w_up[i]
        u = _causal_dwconv(u, ffn_conv_w[i], ffn_conv_b[i])
        g_ff, u_ff = jnp.split(u, [D_FF], axis=-1)
        h = h + (jax.nn.silu(g_ff) * u_ff) @ w_down[i]
        gate = jax.nn.sigmoid(_rmsnorm(h, ple_norm_g[i]) @ w_ple_gate[i])
        pe = _rmsnorm(p[i] @ w_ple_proj[i], ple_post_g[i])
        h = h + gate * pe
    return h


N_DN_HEADS = 8
DN_HEAD_DIM = 128
DN_WIDTH = N_DN_HEADS * DN_HEAD_DIM
N_FOURIER_GROUPS = 8
FOURIER_GROUP_DIM = 128
FOURIER_WIDTH = N_FOURIER_GROUPS * FOURIER_GROUP_DIM
CONV_WIDTH = 5
CHUNK = 64
D_FF_2 = 4 * D_MODEL
N_BRANCHES = 2

SPLIT_SIZES = (DN_WIDTH, DN_WIDTH, DN_WIDTH, DN_WIDTH, FOURIER_WIDTH, 4 * N_DN_HEADS, N_BRANCHES * D_MODEL)
IN_WIDTH_2 = int(sum(SPLIT_SIZES))
SPLIT_POINTS = tuple(int(s) for s in np.cumsum(SPLIT_SIZES)[:-1])


def rms_norm(x, g):
    xf = x.astype(jnp.float32)
    y = xf * lax.rsqrt(jnp.mean(xf * xf, axis=-1, keepdims=True) + EPS)
    return (y * g.astype(jnp.float32)).astype(x.dtype)

def l2_norm(x):
    return x * lax.rsqrt(jnp.sum(x * x, axis=-1, keepdims=True) + EPS)

def centred_short_conv(u, w):
    c = u.shape[-1]
    pad = (CONV_WIDTH - 1) // 2
    return lax.conv_general_dilated(u, w[:, None, :].astype(u.dtype), window_strides=(1,),
                                    padding=[(pad, pad)], dimension_numbers=("NWC", "WIO", "NWC"),
                                    feature_group_count=c)

def gated_delta_rule_chunked(q, k, v, g, beta):
    b, h, t, dk = q.shape
    dv = v.shape[-1]
    n = t // CHUNK
    q = q.reshape(b, h, n, CHUNK, dk)
    k = k.reshape(b, h, n, CHUNK, dk)
    v = v.reshape(b, h, n, CHUNK, dv)
    gc = jnp.cumsum(g.reshape(b, h, n, CHUNK), axis=-1)
    beta = beta.reshape(b, h, n, CHUNK, 1)
    idx = jnp.arange(CHUNK)
    incl = idx[:, None] >= idx[None, :]
    strict = idx[:, None] > idx[None, :]
    diff = gc[..., :, None] - gc[..., None, :]
    decay = jnp.where(incl, jnp.exp(jnp.where(incl, diff, 0.0)), 0.0)
    kb = k * beta
    m = jnp.where(strict, jnp.einsum("bhnid,bhnjd->bhnij", kb, k) * decay, 0.0)
    a_mat = m + jnp.eye(CHUNK, dtype=m.dtype)
    rhs = jnp.concatenate([v * beta, kb * jnp.exp(gc)[..., None]], axis=-1)
    sol = lax.linalg.triangular_solve(a_mat, rhs, left_side=True, lower=True, unit_diagonal=True)
    u, w = sol[..., :dv], sol[..., dv:]
    qk = jnp.where(incl, jnp.einsum("bhnid,bhnjd->bhnij", q, k) * decay, 0.0)
    q_dec = q * jnp.exp(gc)[..., None]
    k_dec = k * jnp.exp(gc[..., -1:] - gc)[..., None]
    g_last = jnp.exp(gc[..., -1])
    xs = tuple(jnp.moveaxis(a, 2, 0) for a in (q_dec, k_dec, u, w, qk, g_last))

    def step(s, inp):
        qd, kd, uc, wc, qkc, gl = inp
        v_new = uc - jnp.einsum("bhck,bhkv->bhcv", wc, s)
        o = jnp.einsum("bhck,bhkv->bhcv", qd, s) + jnp.einsum("bhij,bhjv->bhiv", qkc, v_new)
        s = s * gl[..., None, None] + jnp.einsum("bhck,bhcv->bhkv", kd, v_new)
        return s, o

    s0 = jnp.zeros((b, h, dk, dv), jnp.float32)
    _, o = lax.scan(step, s0, xs)
    return jnp.moveaxis(o, 0, 2).reshape(b, h, t, dv)

def gated_deltanet_branch(q, k, v, z, scal, conv_w, a_log_f, a_log_b, dt_b_f, dt_b_b, g_head, w_up):
    b, t, _ = q.shape
    dtype = q.dtype
    qkv = jax.nn.silu(centred_short_conv(jnp.concatenate([q, k, v], axis=-1), conv_w)).astype(jnp.float32)
    q, k, v = jnp.split(qkv, 3, axis=-1)
    heads = lambda a: a.reshape(b, t, N_DN_HEADS, DN_HEAD_DIM).transpose(0, 2, 1, 3)
    q = l2_norm(heads(q)) * (DN_HEAD_DIM ** -0.5)
    k = l2_norm(heads(k))
    v = heads(v)
    scal = scal.astype(jnp.float32).transpose(0, 2, 1)
    beta_f, beta_b, a_f, a_b = jnp.split(scal, 4, axis=1)
    beta_f, beta_b = jax.nn.sigmoid(beta_f), jax.nn.sigmoid(beta_b)
    g_f = -jnp.exp(a_log_f.astype(jnp.float32))[:, None] * jax.nn.softplus(a_f + dt_b_f.astype(jnp.float32)[:, None])
    g_b = -jnp.exp(a_log_b.astype(jnp.float32))[:, None] * jax.nn.softplus(a_b + dt_b_b.astype(jnp.float32)[:, None])
    o_f = gated_delta_rule_chunked(q, k, v, g_f, beta_f)
    flip = lambda a: jnp.flip(a, axis=2)
    o_b = flip(gated_delta_rule_chunked(flip(q), flip(k), flip(v), flip(g_b), flip(beta_b)))
    o = (o_f + o_b).transpose(0, 2, 1, 3)
    o = o * lax.rsqrt(jnp.mean(o * o, axis=-1, keepdims=True) + EPS) * g_head.astype(jnp.float32)
    o = o * jax.nn.silu(z.astype(jnp.float32).reshape(b, t, N_DN_HEADS, DN_HEAD_DIM))
    return o.reshape(b, t, DN_WIDTH).astype(dtype) @ w_up

def fourier_branch(f, w_lin):
    b, t, _ = f.shape
    fg = f.astype(jnp.float32).reshape(b, t, N_FOURIER_GROUPS, FOURIER_GROUP_DIM)
    fr = jnp.real(jnp.fft.fft2(fg, axes=(1, 3), norm="ortho"))
    return fr.reshape(b, t, FOURIER_WIDTH).astype(f.dtype) @ w_lin

def second_inputs(seed: int = 0) -> dict:
    key = jax.random.key(seed)
    ks = jax.random.split(key, 20)
    nrm = lambda k, shape, fan_in: jax.random.normal(k, shape, jnp.float32) * (fan_in ** -0.5)
    gain = lambda k, shape: 1.0 + 0.02 * jax.random.normal(k, shape, jnp.float32)
    a_log = lambda k: jnp.log(jax.random.uniform(k, (DEPTH, N_DN_HEADS), jnp.float32, 1.0, 16.0))

    def dt_bias(k):
        dt = jnp.exp(jax.random.uniform(k, (DEPTH, N_DN_HEADS), jnp.float32, np.log(1e-3), np.log(1e-1)))
        return dt + jnp.log(-jnp.expm1(-dt))

    return {
        "x": jax.random.normal(ks[0], (BATCH, SEQ, D_MODEL), jnp.float32),
        "g_mix": gain(ks[1], (DEPTH, D_MODEL)),
        "w_in": nrm(ks[2], (DEPTH, D_MODEL, IN_WIDTH_2), D_MODEL),
        "conv_w": nrm(ks[3], (DEPTH, CONV_WIDTH, 3 * DN_WIDTH), CONV_WIDTH),
        "a_log_fwd": a_log(ks[4]),
        "a_log_bwd": a_log(ks[5]),
        "dt_bias_fwd": dt_bias(ks[6]),
        "dt_bias_bwd": dt_bias(ks[7]),
        "g_dn_head": gain(ks[8], (DEPTH, DN_HEAD_DIM)),
        "w_dn_up": nrm(ks[9], (DEPTH, DN_WIDTH, D_MODEL), DN_WIDTH),
        "w_fourier": nrm(ks[10], (DEPTH, FOURIER_WIDTH, D_MODEL), FOURIER_WIDTH),
        "w_o": nrm(ks[11], (DEPTH, D_MODEL, D_MODEL), D_MODEL),
        "g_mlp": gain(ks[12], (DEPTH, D_MODEL)),
        "w_mlp_up": nrm(ks[13], (DEPTH, D_MODEL, D_FF_2), D_MODEL),
        "w_mlp_down": nrm(ks[14], (DEPTH, D_FF_2, D_MODEL), D_FF_2),
        "g_final": gain(ks[15], (D_MODEL,)),
    }

def second_block(x, g_mix, w_in, conv_w, a_log_fwd, a_log_bwd, dt_bias_fwd, dt_bias_bwd, g_dn_head,
              w_dn_up, w_fourier, w_o, g_mlp, w_mlp_up, w_mlp_down, g_final):
    for l in range(DEPTH):
        h = rms_norm(x, g_mix[l])
        proj = h @ w_in[l]
        q, k, v, z, f, scal, gates = jnp.split(proj, SPLIT_POINTS, axis=-1)
        y_a = gated_deltanet_branch(q, k, v, z, scal, conv_w[l], a_log_fwd[l], a_log_bwd[l],
                                    dt_bias_fwd[l], dt_bias_bwd[l], g_dn_head[l], w_dn_up[l])
        y_f = fourier_branch(f, w_fourier[l])
        gate_a, gate_f = jnp.split(jax.nn.sigmoid(gates), N_BRANCHES, axis=-1)
        x = x + (gate_a * y_a + gate_f * y_f) @ w_o[l]
        h = rms_norm(x, g_mlp[l])
        x = x + jnp.square(jax.nn.relu(h @ w_mlp_up[l])) @ w_mlp_down[l]
    return rms_norm(x, g_final)


def setup_inputs(seed=0):
    out = dict(first_inputs(seed))
    for name, value in second_inputs(seed + 1).items():
        if name != "x":
            out[name + "_2"] = value
    return out


def reference(
    x, p, positions, attn_norm_g, w_in, conv_w, conv_b, dt_bias, a_log, d_skip, ssm_norm_g,
    q_norm_g, k_norm_g, sinks, w_out, ffn_norm_g, w_up, ffn_conv_w, ffn_conv_b, w_down,
    ple_norm_g, w_ple_gate, w_ple_proj, ple_post_g, g_mix_2, w_in_2, conv_w_2, a_log_fwd_2,
    a_log_bwd_2, dt_bias_fwd_2, dt_bias_bwd_2, g_dn_head_2, w_dn_up_2, w_fourier_2, w_o_2,
    g_mlp_2, w_mlp_up_2, w_mlp_down_2, g_final_2,
):
    x = first_block(
        x, p, positions, attn_norm_g, w_in, conv_w, conv_b, dt_bias, a_log, d_skip, ssm_norm_g,
        q_norm_g, k_norm_g, sinks, w_out, ffn_norm_g, w_up, ffn_conv_w, ffn_conv_b, w_down,
        ple_norm_g, w_ple_gate, w_ple_proj, ple_post_g,
    )
    return second_block(
        x, g_mix_2, w_in_2, conv_w_2, a_log_fwd_2, a_log_bwd_2, dt_bias_fwd_2, dt_bias_bwd_2,
        g_dn_head_2, w_dn_up_2, w_fourier_2, w_o_2, g_mlp_2, w_mlp_up_2, w_mlp_down_2,
        g_final_2,
    )


_drawn_inputs = setup_inputs


def setup_inputs(seed=0):
    import zlib

    import numpy as np

    out = dict(_drawn_inputs(seed))
    spreads = {}
    factors = {'attn_norm_g': 2.709,
     'conv_b': 3.012,
     'd_skip': 55.464,
     'ssm_norm_g': 4.452,
     'q_norm_g': 8.0,
     'k_norm_g': 8.0,
     'sinks': 8.0,
     'ffn_norm_g': 4.191,
     'ffn_conv_b': 4.408,
     'ple_norm_g': 34.243,
     'ple_post_g': 31.524,
     'g_mix_2': 6.161,
     'g_dn_head_2': 26.07,
     'g_mlp_2': 16.229,
     'g_final_2': 8.437}
    for name, (base, spread) in spreads.items():
        noise = np.random.default_rng([zlib.crc32(name.encode()), seed]).standard_normal(out[name].shape)
        drawn = base * np.exp(spread * noise) if base else spread * noise
        out[name] = __import__('jax').numpy.asarray(drawn.astype(out[name].dtype))
    for name, factor in factors.items():
        out[name] = (out[name] * factor).astype(out[name].dtype)
    return out
```

```python
from contextlib import ExitStack

import numpy as np
import concourse.bass as bass
import concourse.mybir as mybir

F32 = mybir.dt.float32
F32R = mybir.dt.float32r
I32 = mybir.dt.int32
ACT = mybir.ActivationFunctionType
ALU = mybir.AluOpType
AX = mybir.AxisListType

P = 128
SEQ, D = 256, 2048
TT = SEQ // P
KT = D // P
NC = 512
EPS = 1e-6
SLAB_KT, QUAD = 2, 4

HEADS, HD = 32, 64
GROUPS, HPG = 4, 8
KVH, REP = 8, 4
QKV_W = (HEADS + 2 * KVH) * HD
CONV1, XBC_W = 4, 3072
ROPE = 16
PLE = 256
D_FF = 5632
FFB = NC
N_FF = D_FF // FFB
CONV_FF = 3
DNH, DND = 8, 128
DNW = DNH * DND
CHUNK = 64
CONV2 = 5
D_FF2 = 4 * D
N_FF2 = D_FF2 // NC

Q_QKV = 0
Q_XBC = Q_QKV + 2 * (QKV_W // NC)
Q_Z = Q_XBC + 2 * (XBC_W // NC)
Q_WOA = Q_Z + 2 * (D // NC)
Q_WOS = Q_WOA + 2 * (D // NC)
Q_FF = Q_WOS + 2 * (D // NC)
Q_GATE = Q_FF + 6 * N_FF
Q_QKV2 = Q_GATE + 2 * (D // NC)
Q_F = Q_QKV2 + 2 * (3 * DNW // NC)
Q_Z2 = Q_F + 2 * (DNW // NC)
Q_MIX = Q_Z2 + 2 * (DNW // NC)
Q_WO2 = Q_MIX + 6 * (D // NC)
Q_MLP = Q_WO2 + 2 * (D // NC)
N_QUADS = Q_MLP + 4 * N_FF2

ROW = {}
_at = 0
for _name, _n in (("q_norm_g", HD), ("k_norm_g", HD), ("sinks", HEADS), ("dt_bias", HEADS),
                  ("a_log", HEADS), ("d_skip", HEADS), ("g_dn_head_2", DND),
                  ("a_log_fwd_2", DNH), ("a_log_bwd_2", DNH),
                  ("dt_bias_fwd_2", DNH), ("dt_bias_bwd_2", DNH)):
    ROW[_name] = (_at, _at + _n)
    _at += _n
N_ROW = _at
GAINS = ("attn_norm_g", "ssm_norm_g", "ffn_norm_g", "ple_post_g", "ple_norm_g",
         "g_mix_2", "g_mlp_2", "g_final_2")
NEG = -1e30

def _constants():
    i, j = np.arange(P)[:, None], np.arange(P)[None, :]
    same = (i // CHUNK) == (j // CHUNK)
    out = {"ident": i == j, "ones": np.ones((P, P)), "before": i <= j}
    mask = np.zeros((P, 3, P))
    mask[:, 0] = np.where(j <= i, 0.0, NEG)
    mask[:, 1] = np.where(j > i, 0.0, NEG)
    mask[:, 2] = mask[:, 0]
    out["att_mask"] = mask
    out["cum"] = np.stack([same & (i <= j), same & (i >= j)], 1)
    out["rest"] = np.stack([same & (i > j), same & (i < j)], 1)
    out["chunk_ones"] = np.stack([(i // CHUNK == c) & (j >= 0) for c in range(P // CHUNK)], 1)
    level = []
    for k in range(LEVELS):
        block = (i >> (k + 1)) == (j >> (k + 1))
        later, earlier = (i >> k) & 1, (j >> k) & 1
        fwd = block & (later == 1) & (earlier == 0)
        level.append(np.stack([fwd, fwd.T], 1))
    out["level"] = np.stack(level, 1)
    t, c = np.arange(SEQ), np.arange(DND)
    norm = 1.0 / np.sqrt(SEQ * DND)
    at = 2 * np.pi * np.outer(t, t) / SEQ
    ad = 2 * np.pi * np.outer(c, c) / DND
    dft_t = np.stack([np.cos(at), np.sin(at)], 0) * norm
    out["dft_t"] = dft_t.reshape(2, TT, P, SEQ).transpose(2, 0, 1, 3)
    out["dft_d"] = np.stack([np.cos(ad), -np.sin(ad)], 1)
    freq = ROPE_THETA ** (-np.arange(0, ROPE, 2, dtype=np.float32) / np.float32(ROPE))
    out["inv_freq"] = np.broadcast_to(freq, (P, ROPE // 2))
    return {k: np.ascontiguousarray(v, dtype=np.float32) for k, v in out.items()}


LEVELS = CHUNK.bit_length() - 1
ROPE_THETA = np.float32(500000.0)
TWO_PI = (6.28125, 0.0019350051879882812, float(2 * np.pi - 6.28125 - 0.0019350051879882812))
PI_BELOW = 3.1415925
ROUND = 1.5 * 2.0 ** 23
CONSTS = _constants()

SMALL = {
    "x_tok": (P, TT, D), "positions_tok": (P, TT), "p_T": (P, PLE // P, SEQ),
    "w_dt": (P, KT, HEADS), "w_scal": (P, KT, 4 * DNH), "w_proj": (P, PLE // P, D),
    "conv_col": (P, XBC_W // P, CONV1 + 1), "ff_col": (P, N_FF, 2 * FFB // P, CONV_FF + 1),
    "conv2_col": (P, 3 * DNW // P, CONV2), "gains": (len(GAINS), D), "row": (1, N_ROW),
}

U_QKV = 0
U_XBC = U_QKV + QKV_W // NC // 2
U_Z = U_XBC + XBC_W // NC // 2
U_WOA = U_Z + D // NC // 2
U_WOS = U_WOA + D // NC // 2
U_FF = U_WOS + D // NC // 2
U_GATE = U_FF + 3 * N_FF
U_QKV2 = U_GATE
U_F = U_QKV2 + 3 * DNW // NC // 2
U_Z2 = U_F + DNW // NC // 2
U_MIX = U_Z2 + DNW // NC // 2
U_WO2 = U_MIX + D // NC
U_MLP = U_WO2 + D // NC // 2
V_PLE, V_MIX = 0, D // NC // 2
V_MLP = V_MIX + D // NC
TR_ATTN, TR_YATT, TR_YSSM, TR_FFN, TR_PLE, TR_MIX2, TR_WO2, TR_MLP = range(8)
NORM_ATTN, NORM_FFN, NORM_PLE, NORM_MIX2, NORM_MLP, NORM_OUT = range(6)
(G_ATTN, G_SSM, G_FFN, G_POST, G_PLE, G_MIX2, G_MLP, G_OUT) = range(8)


class Chain:

    def __init__(self, eng, sem):
        self.eng, self.sem, self.base, self.n = eng, sem, 0, 0

    def __call__(self, instruction):
        instruction.then_inc(self.sem, 1)
        self.n += 1
        self.eng.wait_ge(self.sem, self.base + self.n)

    def enter(self, turn, steps):
        self.before, self.steps = self.base + self.n, steps
        self.base, self.n = self.before + turn * steps, 0

    def leave(self, turns):
        assert self.n == self.steps, (self.n, self.steps)
        self.base, self.n = self.before + turns * self.steps, 0


NORMED = np.cumsum([TT, TT * GROUPS, TT, TT, TT, TT, TT, TT]).tolist()


def program(nc, wstream, small, const, out):
    ctx = ExitStack()
    with ctx:
        def sb(name, shape, dt=F32, scope=ctx):
            return scope.enter_context(nc.sbuf_tensor(name, list(shape), dt))

        sems = {}

        def sem(name):
            sems[name] = ctx.enter_context(nc.semaphore(name))
            return sems[name]

        w_raw = sb("w_raw", [P, QUAD, SLAB_KT * NC])
        w_hi = sb("w_hi", [P, QUAD, SLAB_KT * NC], F32R)
        w_lo = sb("w_lo", [P, QUAD, SLAB_KT * NC], F32R)
        a_hi = sb("a_hi", [P, KT, SEQ], F32R)
        a_lo = sb("a_lo", [P, KT, SEQ], F32R)
        h = sb("h", [P, TT, D])
        gain = sb("gain", [P, D])
        ident = sb("ident_sb", [P, P])
        ones = sb("ones_sb", [P, P])
        row = sb("row_sb", [P, N_ROW])
        neg_half = sb("neg_half", [P, 88])
        stat = sb("stat", [P, 4])
        rstd = sb("rstd", [P, 4])

        with ExitStack() as part:
            def at1(name, shape, dt=F32):
                return sb(name, shape, dt, part)
            qkv = at1("qkv", [P, TT, QKV_W])
            xs = at1("xs", [P, TT, D])
            with ExitStack() as first:
                def at1f(name, shape, dt=F32):
                    return sb(name, shape, dt, first)
                w32_raw = at1f("w32_raw", [P, KT, HEADS])
                w32_hi = at1f("w32_hi", [P, KT, HEADS], F32R)
                w32_lo = at1f("w32_lo", [P, KT, HEADS], F32R)
                rope_t = at1f("rope_t", [P, 4, HEADS + KVH, ROPE // 2])
            z = at1("z", [P, TT, D])
            bT = at1("bT", [P, GROUPS, SEQ])
            cT = at1("cT", [P, GROUPS, SEQ])
            b_tok = at1("b_tok", [P, GROUPS, P])
            stage = at1("stage", [P, 2, TT, NC])
            cv = at1("cv", [P, 4, SEQ])
            cv_act = at1("cv_act", [P, 4, SEQ])
            work = at1("work", [P, 2 * 1536])
            before = at1("before_sb", [P, P])
            att_mask = at1("att_mask_sb", [P, 3, P])
            inv_freq = at1("inv_freq_sb", [P, ROPE // 2])
            conv_col = at1("conv_col_sb", [P, XBC_W // P, CONV1 + 1])
            pos_i = at1("pos_i", [P, TT], I32)
            pos_f = at1("pos_f", [P, TT])
            ang = at1("ang", [P, 6, TT, ROPE // 2])
            sin = at1("sin", [P, TT, ROPE // 2])
            cos = at1("cos", [P, TT, ROPE // 2])
            qk_ss = at1("qk_ss", [P, TT, 40])
            qk_rs = at1("qk_rs", [P, TT, 40])
            sp = at1("sp", [P, 6, TT * HEADS])
            dt = at1("dt", [P, TT, HEADS])
            adt = at1("adt", [P, TT, HEADS])
            acs = at1("acs", [P, TT, HEADS])
            aneg = at1("aneg", [P, HEADS])
            ds = at1("ds", [P, HEADS])
            ea = at1("ea", [P, HEADS])
            att_s = at1("att_s", [P, 8, 8])
            ssm_ss = at1("ssm_ss", [P, TT, GROUPS])
            ssm_rs = at1("ssm_rs", [P, TT, GROUPS])
        with ExitStack() as part:
            def at2(name, shape, dt=F32):
                return sb(name, shape, dt, part)
            xn_f = at2("xn_f", [P, TT, D])
            f_hi = at2("f_hi", [P, FFB // P, SEQ], F32R)
            f_lo = at2("f_lo", [P, FFB // P, SEQ], F32R)
            f_stage = at2("f_stage", [P, TT, 2 * FFB])
            f_cv = at2("f_cv", [P, 2 * FFB // P, SEQ])
            f_silu = at2("f_silu", [P, FFB // P, SEQ])
            f_act = at2("f_act", [P, FFB // P, SEQ])
            ff_col = at2("ff_col_sb", [P, N_FF, 2 * FFB // P, CONV_FF + 1])
            pe_tok = at2("pe_tok", [P, TT, D])
            w_proj = at2("w_proj_sb", [P, PLE // P, D])
            p_T = at2("p_T_sb", [P, PLE // P, SEQ])
            sig = at2("sig", [P, TT, NC])
        with ExitStack() as part:
            def at3(name, shape, dt=F32):
                return sb(name, shape, dt, part)
            qkv2 = at3("qkv2", [P, TT, 3 * DNW])
            qk_T = at3("qk_T", [P, 2, DNH, SEQ])
            z2 = at3("z2", [P, TT, DNW])
            fr = at3("fr", [P, TT, DNW])
            conv2_col = at3("conv2_col_sb", [P, 3 * DNW // P, CONV2])
            sc = at3("sc", [P, TT, 4 * DNH])
            sp2 = at3("sp2", [P, 6, TT * 2 * DNH])
            g2 = at3("g2", [P, TT, 2, DNH])
            aneg2 = at3("aneg2", [P, 2 * DNH])
            beta = at3("beta", [P, TT, 2, DNH])
            gc = at3("gc", [P, TT, 2, DNH])
            be = at3("be", [P, TT, 2, DNH])
            kd = at3("kd", [P, TT, 2, DNH])
            gl = at3("gl", [P, SEQ // CHUNK, 2, DNH])
            dn_ss = at3("dn_ss", [P, TT, 2 * DNH])
            dn_rs = at3("dn_rs", [P, TT, 2 * DNH])
            with ExitStack() as inner:
                def at3a(name, shape, dt_=F32):
                    return sb(name, shape, dt_, inner)
                cum = at3a("cum_sb", [P, 2, P])
                rest = at3a("rest_sb", [P, 2, P])
                chunk_ones = at3a("chunk_ones_sb", [P, P // CHUNK, P])
                level = at3a("level_sb", [P, LEVELS, 2, P])
                with ExitStack() as first:
                    def at3p(name, shape, dt_=F32):
                        return sb(name, shape, dt_, first)
                    s_stage = at3p("s_stage", [P, 2, TT, NC])
                    s_cv = at3p("s_cv", [P, 4, SEQ])
                    s_act = at3p("s_act", [P, 4, SEQ])
                    s_raw = at3p("s_raw", [P, KT, 4 * DNH])
                    s_hi = at3p("s_hi", [P, KT, 4 * DNH], F32R)
                    s_lo = at3p("s_lo", [P, KT, 4 * DNH], F32R)
                d_qk = at3a("d_qk", [P, 2, SEQ])
                d_gs, d_eT, d_eN, d_m, d_mk, d_t, d_r, d_zz, d_vb, d_kb, d_kd, d_u, d_wT, d_qd = (
                    at3a(f"d_{n}", [P, TT, 2, P]) for n in
                    ("gs", "eT", "eN", "m", "mk", "t", "r", "zz", "vb", "kb", "kd", "u", "wT", "qd"))
                d_vn = at3a("d_vn", [P, 2, P])
                d_s = at3a("d_s", [P, 2, P])
            with ExitStack() as inner:
                def at3b(name, shape, dt_=F32):
                    return sb(name, shape, dt_, inner)
                dft_t = at3b("dft_t_sb", [P, 2, TT, SEQ])
                dft_d = at3b("dft_d_sb", [P, 2, DND])
                f_half = at3b("f_half", [P, 2, 2, SEQ])
                fr_hi = at3b("fr_hi", [P, DNH, SEQ], F32R)
                fr_lo = at3b("fr_lo", [P, DNH, SEQ], F32R)
                y_hi = at3b("y_hi", [P, DNH, SEQ], F32R)
                y_lo = at3b("y_lo", [P, DNH, SEQ], F32R)
        with ExitStack() as part:
            def at4(name, shape, dt_=F32):
                return sb(name, shape, dt_, part)
            xn_m = at4("xn_m", [P, TT, D])
            m_hi = at4("m_hi", [P, FFB // P, SEQ], F32R)
            m_lo = at4("m_lo", [P, FFB // P, SEQ], F32R)
            m_stage = at4("m_stage", [P, TT, NC])
            m_relu = at4("m_relu", [P, FFB // P, SEQ])
            m_act = at4("m_act", [P, FFB // P, SEQ])
        bank = [ctx.enter_context(nc.psum_tensor(f"bank{i}", [P, NC], F32)) for i in range(8)]
        pair = [bank[2 * i:2 * i + 2] for i in range(4)]

        att_q = stage[:, 0].rearrange("p t (a b d) -> p t a b d", a=REP, b=2)
        att_k = stage[:, 1, 0, 0:SEQ].rearrange("p (t d) -> p t d", t=TT)
        att_qT = cv[:].rearrange("p a s -> p (a s)").rearrange("p (t a s) -> p t a s", t=TT, a=REP)
        att_kT = cv_act[:, 0]
        att_p, att_pTs = work[:, 0:1536], work[:, 1536:3072]
        ssm_cb = cv_act[:].rearrange("p g (t s) -> p g t s", t=TT)
        ssm_rows = cv[:].rearrange("p a s -> p (a s)").rearrange("p (a s) -> p a s", a=HPG)
        ssm_w = work[:, 0:HPG * P].rearrange("p (a s) -> p a s", a=HPG)
        ssm_xd = work[:, 1024:2048].rearrange("p (t n) -> p t n", t=TT)
        ssm_xds, ssm_state = work[:, 2048:2560], work[:, 2560:3072]
        ssm_dx = stage[:, 0]
        ssm_y, ssm_junk = stage[:, 1, 0], stage[:, 1, 1]
        ssm_off = qkv[:, 0, 0:NC]

        def att_cols(n):
            s0 = n * P if n < REP else REP * P + (n - REP) * 2 * P
            return s0, s0 + (P if n < REP else 2 * P)

        qk_flat = qk_T[:].rearrange("p a h s -> p (a h s)")
        mix = qk_flat.rearrange("p (t n) -> p t n", t=TT)
        qkh = qk_T[:].rearrange("p a h s -> p (a h) s")

        def rows_of(n, d):
            c = n if d == 0 else SEQ // CHUNK - 1 - n
            r = c % (P // CHUNK) * CHUNK
            return c, c // (P // CHUNK), slice(r, r + CHUNK)

        raw_loaded = [sem(f"raw_loaded{s}") for s in range(QUAD)]
        hi_ready, lo_ready = sem("hi_ready"), sem("lo_ready")
        slab_done = sem("slab_done")
        pair_free = [sem(f"pair_free{p}") for p in range(4)]
        x_loaded, small1_loaded = sem("x_loaded"), sem("small1_loaded")
        w32_loaded, w32_hi_ready, w32_lo_ready = sem("w32_loaded"), sem("w32_hi_ready"), sem("w32_lo_ready")
        gain_loaded = sem("gain_loaded")
        stat_ready, rstd_ready = sem("stat_ready"), sem("rstd_ready")
        normed = sem("normed")
        tr_ready, a_hi_ready, a_lo_ready = sem("tr_ready"), sem("a_hi_ready"), sem("a_lo_ready")
        dve_step, pool_step = sem("dve_step"), sem("pool_step")
        dt_mm = sem("dt_mm")
        sp_abs, sp_exp, sp_sum, sp_ln = sem("sp_abs"), sem("sp_exp"), sem("sp_sum"), sem("sp_ln")
        rope_arg, rope_ready = sem("rope_arg"), sem("rope_ready")
        qk_sq, qk_summed, qk_rstd, qk_ready = sem("qk_sq"), sem("qk_summed"), sem("qk_rstd"), sem("qk_ready")
        xbc_t, conv_done, silu_done, xbc_back = sem("xbc_t"), sem("conv_done"), sem("silu_done"), sem("xbc_back")
        back0_evac, back1_evac = sem("back0_evac"), sem("back1_evac")
        att_staged, att_qkT, att_qkT_evac = sem("att_staged"), sem("att_qkT"), sem("att_qkT_evac")
        att_scored, att_max, att_exp = sem("att_scored"), sem("att_max"), sem("att_exp")
        att_pT, att_pT_evac, att_pv, att_done = sem("att_pT"), sem("att_pT_evac"), sem("att_pv"), sem("att_done")
        adt_ready, acs_mm, acs_ready, sdecay = sem("adt_ready"), sem("acs_mm"), sem("acs_ready"), sem("sdecay")
        aneg_ready = sem("aneg_ready")
        cb_mm, cb_ready = sem("cb_mm"), sem("cb_ready")
        row_scaled, row_mm, seg_ready, seg_exp, seg_w = (sem(n) for n in (
            "row_scaled", "row_mm", "seg_ready", "seg_exp", "seg_w"))
        xd_ready, xds_ready, state_mm, state_evac = sem("xd_ready"), sem("xds_ready"), sem("state_mm"), sem("state_evac")
        ydiag_mm, yoff_mm, dskip_ready, y_gated, y_squared, ssm_rstd = (sem(n) for n in (
            "ydiag_mm", "yoff_mm", "dskip_ready", "y_gated", "y_squared", "ssm_rstd"))
        small2_loaded, ple_mm = sem("small2_loaded"), sem("ple_mm")
        ff_t, ff_conv, ff_silu, ff_mul, ff_hi, ff_lo = (sem(n) for n in (
            "ff_t", "ff_conv", "ff_silu", "ff_mul", "ff_hi", "ff_lo"))
        sig_ready, gated = sem("sig_ready"), sem("gated")
        small3_loaded, small4_loaded = sem("small3_loaded"), sem("small4_loaded")
        s_hi_ready, s_lo_ready, sc_mm = sem("s_hi_ready"), sem("s_lo_ready"), sem("sc_mm")
        qkv2_t, conv2_done, silu2_done, qkv2_back = sem("qkv2_t"), sem("conv2_done"), sem("silu2_done"), sem("qkv2_back")
        back2_evac0, back2_evac1 = sem("back2_evac0"), sem("back2_evac1")
        beta_ready, g2_ready, gc_mm, gc_exp, dn_pre = (sem(n) for n in (
            "beta_ready", "g2_ready", "gc_mm", "gc_exp", "dn_pre"))
        dn_sq, dn_summed, dn_qk_normed, dn_qkT, dn_qkT_evac0, dn_qkT_evac1 = (sem(n) for n in (
            "dn_sq", "dn_summed", "dn_qk_normed", "dn_qkT", "dn_qkT_evac0", "dn_qkT_evac1"))
        z2_scaled, fr_ready = sem("z2_scaled"), sem("fr_ready")
        (dn_free, dn_qk, dn_rows, dn_in, dn_gcb, dn_kk, dn_diff, dn_eT, dn_eN, dn_egb, dn_eTm, dn_qd, dn_m, dn_mk,
         dn_t, dn_rT, dn_r, dn_z, dn_zz, dn_rz, dn_tz, dn_uw, dn_u, dn_wT, dn_qkm, dn_ws, dn_vn, dn_so, dn_s) = (
            sem("dn_" + n) for n in (
                "free", "qk", "rows", "in", "gcb", "kk", "diff", "eT", "eN", "egb", "eTm", "qd", "m", "mk", "t", "rT",
                "r", "z", "zz", "rz", "tz", "uw", "u", "wT", "qkm", "ws", "vn", "so", "s"))
        o_sq, o_summed, o_rstd, y_ready, y_t, y_hi_ready, y_lo_ready = (sem(n) for n in (
            "o_sq", "o_summed", "o_rstd", "y_ready", "y_t", "y_hi_ready", "y_lo_ready"))
        f_mm, f_half_ready, f_out, fr_hi_ready, fr_lo_ready = (sem(n) for n in (
            "f_mm", "f_half_ready", "f_out", "fr_hi_ready", "fr_lo_ready"))
        mix_ready = sem("mix_ready")
        mlp_relu = sem("mlp_relu")
        stored = sem("stored")

        block = ctx.enter_context(nc.Block())

        @block.sync
        def _(sp_):
            sp_.dma_start(h[:], small["x_tok"]).then_inc(x_loaded, 16)
            for dst, src in ((ident, const["ident"]), (ones, const["ones"]),
                             (row, small["row"].to_broadcast([P, N_ROW]))):
                sp_.dma_start(dst[:], src).then_inc(x_loaded, 16)
            for s in range(QUAD):
                sp_.dma_start(w_raw[:, s, :], wstream[0, s]).then_inc(raw_loaded[s], 16)
            sp_.dma_start(w32_raw[:], small["w_dt"]).then_inc(w32_loaded, 16)
            for dst, src in ((before, const["before"]), (att_mask, const["att_mask"]),
                             (inv_freq, const["inv_freq"]), (conv_col, small["conv_col"]),
                             (pos_i, small["positions_tok"])):
                sp_.dma_start(dst[:], src).then_inc(small1_loaded, 16)
            with sp_.Fori(1, N_QUADS) as q:
                for s in range(QUAD):
                    sp_.wait_ge(lo_ready, QUAD * (q - 1) + s + 1)
                    sp_.dma_start(w_raw[:, s, :], wstream[q, s]).then_inc(raw_loaded[s], 16)

            for t in range(TT):
                sp_.wait_ge(normed, NORMED[G_MLP] + t + 1)
                sp_.dma_start(out[t], xn_m[:, t]).then_inc(stored, 16)
            sp_.wait_ge(stored, TT * 16)

        @block.gpsimd
        def _(pool):
            step = Chain(pool, pool_step)

            def load_gain(n):
                if n:
                    pool.wait_ge(normed, NORMED[n - 1])
                pool.dma_start(gain[:], small["gains"][n:n + 1, :].to_broadcast([P, D])).then_inc(gain_loaded, 16)

            def inverse_root(dst, src, width, scale, eps, done):
                step(nc.gpsimd.tensor_scalar(dst, src, scale, eps, ALU.mult, ALU.add))
                nc.gpsimd.tensor_tensor(dst, dst, neg_half[:, 0:width], ALU.pow).then_inc(done, 1)

            def norm_root(n):
                pool.wait_ge(stat_ready, TT * (n + 1))
                inverse_root(rstd[:, 0:TT], stat[:, 0:TT], TT, 1.0 / D, EPS, rstd_ready)

            load_gain(G_ATTN)
            for p in range(4):
                nc.gpsimd.memset(neg_half[:, 20 * p:20 * p + 20], -0.5).then_inc(pair_free[p], 2)
            nc.gpsimd.memset(neg_half[:, 80:81], -0.5).then_inc(att_qkT_evac, 3)
            nc.gpsimd.memset(neg_half[:, 81:82], -0.5).then_inc(back0_evac, 1)
            nc.gpsimd.memset(neg_half[:, 82:83], -0.5).then_inc(back1_evac, 1)
            for k, s in enumerate((back2_evac0, back2_evac1, dn_free)):
                nc.gpsimd.memset(neg_half[:, 83 + k:84 + k], -0.5).then_inc(s, 1)
            for s, n in [(pair_free[p], 2) for p in range(4)] + [(att_qkT_evac, 3), (back0_evac, 1), (back1_evac, 1),
                                                                 (back2_evac0, 1), (back2_evac1, 1), (dn_free, 1)]:
                pool.wait_ge(s, n)
            norm_root(0)
            load_gain(G_SSM)

            pool.wait_ge(small1_loaded, 5 * 16)
            pool.wait_ge(rope_ready, 1)
            for t in range(TT):
                pool.wait_ge(qk_summed, t + 1)
                inverse_root(qk_rs[:, t, :], qk_ss[:, t, :], 40, 1.0 / HD, EPS, qk_rstd)
                pool.wait_ge(qk_rstd, t + 1)
                qk = qkv[:, t, 0:40 * HD].rearrange("p (a d) -> p a d", d=HD)
                step(nc.gpsimd.tensor_tensor(qk, qk, qk_rs[:, t, :].unsqueeze(2).to_broadcast([P, 40, HD]), ALU.mult))
                for name, a0, a1 in (("q_norm_g", 0, HEADS), ("k_norm_g", HEADS, HEADS + KVH)):
                    g = row[:, ROW[name][0]:ROW[name][1]].unsqueeze(1).to_broadcast([P, a1 - a0, HD])
                    step(nc.gpsimd.tensor_tensor(qk[:, a0:a1], qk[:, a0:a1], g, ALU.mult))
                half = ROPE // 2
                t1, t2 = qk[:, :, 0:half], qk[:, :, half:ROPE]
                c = cos[:, t, :].unsqueeze(1).to_broadcast([P, 40, half])
                s = sin[:, t, :].unsqueeze(1).to_broadcast([P, 40, half])
                for m, (x, y) in enumerate(((t1, c), (t2, s), (t2, c), (t1, s))):
                    step(nc.gpsimd.tensor_tensor(rope_t[:, m], x, y, ALU.mult))
                step(nc.gpsimd.tensor_tensor(t1, rope_t[:, 0], rope_t[:, 1], ALU.subtract))
                nc.gpsimd.tensor_tensor(t2, rope_t[:, 2], rope_t[:, 3], ALU.add).then_inc(qk_ready, 1)

            pool.wait_ge(qk_ready, TT)

            pool.wait_ge(slab_done, QUAD * Q_WOA)
            with pool.Fori(0, KVH // 2) as i:
                pool.wait_ge(att_qkT_evac, 3 * i + 3)
                for t in range(TT):
                    for par in range(2):
                        src = qkv[:, t, bass.ds(i * (2 * REP * HD) + par * REP * HD, REP * HD)]
                        nc.gpsimd.tensor_copy(att_q[:, t, :, par, :], src.rearrange("p (a d) -> p a d", d=HD))
                nc.gpsimd.tensor_copy(att_k, qkv[:, :, bass.ds(i * (2 * HD) + HEADS * HD, 2 * HD)]).then_inc(att_staged, 1)

            pool.wait_ge(att_done, KVH)
            pool.wait_ge(sdecay, 1)
            for g in range(GROUPS):
                cols = slice(g * NC, (g + 1) * NC)
                hs = slice(g * HPG, (g + 1) * HPG)

                def by_head(x, hd=HD):
                    return x.rearrange("p (a d) -> p a d", d=hd)
                if g:
                    pool.wait_ge(ydiag_mm, TT * g)
                    pool.wait_ge(y_gated, TT * g)
                for t in range(TT):
                    w = dt[:, t, hs].unsqueeze(2).to_broadcast([P, HPG, HD])
                    last = nc.gpsimd.tensor_tensor(by_head(ssm_xd[:, t]), by_head(xs[:, t, cols]), w, ALU.mult)
                last.then_inc(xd_ready, 1)
                pool.wait_ge(xd_ready, g + 1)
                w = ds[:, hs].unsqueeze(2).to_broadcast([P, HPG, HD])
                nc.gpsimd.tensor_tensor(by_head(ssm_xds), by_head(ssm_xd[:, 0]), w, ALU.mult).then_inc(xds_ready, 1)
                for t in range(TT):
                    n = TT * g + t
                    if n:
                        pool.wait_ge(row_mm, n)
                    w = adt[:, t, hs].unsqueeze(2).to_broadcast([P, HPG, P])
                    nc.gpsimd.tensor_tensor(ssm_rows, before[:].unsqueeze(1).to_broadcast([P, HPG, P]), w,
                                            ALU.mult).then_inc(row_scaled, 1)
                    if t == 0:
                        for tt in range(TT):
                            w = row[:, ROW["d_skip"][0] + g * HPG:ROW["d_skip"][0] + (g + 1) * HPG]
                            last = nc.gpsimd.tensor_tensor(by_head(ssm_dx[:, tt]), by_head(xs[:, tt, cols]),
                                                           w.unsqueeze(2).to_broadcast([P, HPG, HD]), ALU.mult)
                        last.then_inc(dskip_ready, 1)
                    pool.wait_ge(seg_exp, n + 1)
                    cb = ssm_cb[:, g, t, :].unsqueeze(1).to_broadcast([P, HPG, P])
                    nc.gpsimd.tensor_tensor(ssm_w, ssm_w, cb, ALU.mult).then_inc(seg_w, 1)
            pool.wait_ge(y_squared, TT * GROUPS)
            inverse_root(ssm_rs[:].rearrange("p t g -> p (t g)"), ssm_ss[:].rearrange("p t g -> p (t g)"),
                         TT * GROUPS, 1.0 / NC, EPS, ssm_rstd)
            load_gain(G_FFN)

            pool.wait_ge(pair_free[0], 2 * (U_FF + 1))
            pool.wait_ge(pair_free[1], 2 * (U_FF + 1))
            for dst, src in ((ff_col, "ff_col"), (w_proj, "w_proj"), (p_T, "p_T")):
                pool.dma_start(dst[:], small[src]).then_inc(small2_loaded, 16)
            norm_root(1)
            load_gain(G_POST)
            norm_root(2)
            load_gain(G_PLE)
            norm_root(3)
            load_gain(G_MIX2)

            pool.wait_ge(gated, TT * (D // NC))
            for dst, src in ((s_raw, small["w_scal"]), (conv2_col, small["conv2_col"]), (cum, const["cum"]),
                             (rest, const["rest"]), (chunk_ones, const["chunk_ones"]), (level, const["level"])):
                pool.dma_start(dst[:], src).then_inc(small3_loaded, 16)
            norm_root(4)
            load_gain(G_MLP)
            pool.wait_ge(pair_free[0], 2 * (U_F + 1) + 2)
            nc.gpsimd.tensor_copy(fr[:, :, 0:NC], s_stage[:, 0]).then_inc(fr_ready, 1)
            for p in range(2):
                pool.wait_ge(pair_free[p], 2 * (U_MIX + 1))
            g_head = row[:, ROW["g_dn_head_2"][0]:ROW["g_dn_head_2"][1]].unsqueeze(1).to_broadcast([P, DNH, DND])
            for t in range(TT):
                zt = z2[:, t].rearrange("p (a d) -> p a d", d=DND)
                nc.gpsimd.tensor_tensor(zt, zt, g_head, ALU.mult).then_inc(z2_scaled, 1)
            for t in range(TT):
                pool.wait_ge(dn_summed, t + 1)
                step(nc.gpsimd.tensor_scalar(dn_rs[:, t, 0:DNH], dn_ss[:, t, 0:DNH], float(DND), DND * EPS, ALU.mult, ALU.add))
                step(nc.gpsimd.tensor_scalar(dn_rs[:, t, DNH:], dn_ss[:, t, DNH:], EPS, None, ALU.add))
                step(nc.gpsimd.tensor_tensor(dn_rs[:, t], dn_rs[:, t], neg_half[:, 0:2 * DNH], ALU.pow))
                qk = qkv2[:, t, 0:2 * DNW].rearrange("p (a d) -> p a d", d=DND)
                nc.gpsimd.tensor_tensor(qk, qk, dn_rs[:, t].unsqueeze(2).to_broadcast([P, 2 * DNH, DND]),
                                        ALU.mult).then_inc(dn_qk_normed, 1)

            pool.wait_ge(dn_pre, 1)
            pool.wait_ge(dn_qkT_evac0, 4)
            pool.wait_ge(dn_qkT_evac1, 4)
            shape = [P, TT, 2, P]
            with pool.Fori(0, DNH) as i:
                pool.wait_ge(dn_free, i + 1)

                def of_head(x):
                    return x[:, :, :, bass.ds(i, 1)].to_broadcast(shape)

                def tokens(col0):
                    return qkv2[:, :, bass.ds(i * DND + col0, DND)].unsqueeze(2).to_broadcast(shape)
                cums = cum[:].unsqueeze(1).to_broadcast(shape)
                nc.gpsimd.tensor_tensor(d_gs[:], cums, of_head(g2), ALU.mult).then_inc(dn_rows, 1)
                nc.gpsimd.tensor_copy(d_qk[:].unsqueeze(2), qk_T[:, :, bass.ds(i, 1), :]).then_inc(dn_qk, 1)
                nc.gpsimd.tensor_tensor(d_vb[:], tokens(2 * DNW), of_head(beta), ALU.mult)
                nc.gpsimd.tensor_tensor(d_kb[:], tokens(DNW), of_head(be), ALU.mult)
                nc.gpsimd.tensor_tensor(d_kd[:], tokens(DNW), of_head(kd), ALU.mult).then_inc(dn_in, 1)
                for k in range(LEVELS):
                    if k == 0:
                        pool.wait_ge(dn_m, i + 1)
                    elif k == 1:
                        pool.wait_ge(dn_t, (LEVELS - 1) * i + 1)
                    else:
                        pool.wait_ge(dn_z, (LEVELS - 1) * i + k - 1)
                    nc.gpsimd.tensor_tensor(d_mk[:], d_m[:], level[:, k].unsqueeze(1).to_broadcast(shape),
                                            ALU.mult).then_inc(dn_mk, 1)
                    if k == 1:
                        pool.wait_ge(dn_eT, i + 1)
                        nc.gpsimd.tensor_tensor(d_eT[:], d_eT[:], cums, ALU.mult).then_inc(dn_eTm, 1)
                        pool.wait_ge(dn_egb, i + 1)
                        q_rows = d_qk[:, 0].rearrange("p (t s) -> p t s", t=TT).unsqueeze(2).to_broadcast(shape)
                        nc.gpsimd.tensor_tensor(d_qd[:], d_qd[:], q_rows, ALU.mult).then_inc(dn_qd, 1)

            pool.wait_ge(dn_free, DNH + 1)
            for dst, src in ((dft_t, const["dft_t"]), (dft_d, const["dft_d"])):
                pool.dma_start(dst[:], src).then_inc(small4_loaded, 16)
            for t in range(TT):
                pool.wait_ge(o_summed, t + 1)
                inverse_root(dn_rs[:, t, 0:DNH], dn_ss[:, t, 0:DNH], DNH, 1.0 / DND, EPS, o_rstd)
            norm_root(5)
            load_gain(G_OUT)
            with pool.Fori(0, N_FF2) as j:
                pool.wait_ge(mlp_relu, 2 * j + 2)
                nc.gpsimd.tensor_tensor(m_act[:], m_relu[:], m_relu[:], ALU.mult).then_inc(ff_mul, 1)
            norm_root(6)
        @block.scalar
        def _(act):
            def split(q, s0=0, s1=QUAD, first=False):
                for s in range(s0, s1):
                    act.wait_ge(raw_loaded[s], 16 * (q + 1))
                    if not first:
                        act.wait_ge(slab_done, QUAD * (q - 1) + s + 1)
                    nc.scalar.copy(w_hi[:, s, :], w_raw[:, s, :]).then_inc(hi_ready, 1)

            def sum_squares(src, junk):
                for t in range(TT):
                    nc.scalar.activation(junk(t), src[:, t], ACT.Square, accum_out=stat[:, t:t + 1]).then_inc(stat_ready, 1)

            def rounded_operand(n):
                for i in range(KT // 2):
                    act.wait_ge(tr_ready, KT // 2 * n + i + 1)
                    nc.scalar.copy(a_hi[:, 2 * i:2 * i + 2, :].rearrange("p k s -> p (k s)"), bank[4 + i % 4][:]).then_inc(a_hi_ready, 1)

            def softplus_parts(n, buf):
                act.wait_ge(sp_abs, n)
                nc.scalar.activation(buf[:, 2], buf[:, 1], ACT.Exp, scale=-1.0).then_inc(sp_exp, 1)
                act.wait_ge(sp_sum, n)
                nc.scalar.activation(buf[:, 4], buf[:, 3], ACT.Ln).then_inc(sp_ln, 1)

            def pairs_empty(uses):
                act.wait_ge(pair_free[0], 2 * (uses + 1))
                act.wait_ge(pair_free[1], 2 * (uses + 1))

            act.wait_ge(x_loaded, 4 * 16)
            sum_squares(h, lambda t: xs[:, t])
            act.wait_ge(w32_loaded, 16)
            nc.scalar.copy(w32_hi[:], w32_raw[:]).then_inc(w32_hi_ready, 1)
            split(0, first=True)
            rounded_operand(TR_ATTN)
            with act.Fori(0, QKV_W // NC // 2) as i:
                for par in range(2):
                    q = Q_QKV + 4 * i + 2 * par
                    split(q + 1)
                    split(q + 2)
                    act.wait_ge(slab_done, QUAD * (q + 2))
                    nc.scalar.copy(qkv[:, 0, bass.ds(i * (2 * NC) + par * NC, NC)], pair[par][0][:]).then_inc(pair_free[par], 1)
            act.wait_ge(rope_arg, 1)
            nc.scalar.activation(sin[:], ang[:, 3], ACT.Sin)
            nc.scalar.activation(cos[:], ang[:, 5], ACT.Sin).then_inc(rope_ready, 1)
            softplus_parts(1, sp)
            a0, a1 = ROW["a_log"]
            nc.scalar.activation(aneg[:], row[:, a0:a1], ACT.Exp).then_inc(aneg_ready, 1)
            pairs_empty(U_XBC)
            for t in range(TT):
                if t:
                    act.wait_ge(qk_summed, t)
                nc.scalar.activation(work[:, 0:40 * HD], qkv[:, t, 0:40 * HD], ACT.Square).then_inc(qk_sq, 1)

            q = Q_XBC
            split(q + 1)
            split(q + 2)
            act.wait_ge(slab_done, QUAD * (q + 2))
            nc.scalar.copy(stage[:, 0, 0, :], pair[0][0][:]).then_inc(pair_free[0], 1)
            with act.Fori(0, 2) as i:
                for k in range(2):
                    c, par = 2 * i + k, (1 + k) % 2
                    q = Q_XBC + 2 * (2 * i + 1 + k)
                    split(q + 1)
                    act.wait_ge(conv_done, c + 1)
                    nc.scalar.activation(cv_act[:], cv[:], ACT.Silu).then_inc(silu_done, 1)
                    split(q + 2)
                    act.wait_ge(slab_done, QUAD * (q + 2))
                    nc.scalar.copy(stage[:, par, 0, :], pair[par][0][:]).then_inc(pair_free[par], 1)
                    act.wait_ge(xbc_back, c + 1)
                    nc.scalar.copy(xs[:, 0, bass.ds(c * NC, NC)], bank[6][:]).then_inc(back0_evac, 1)
            q = Q_XBC + 10
            split(q + 1)
            act.wait_ge(conv_done, 5)
            nc.scalar.activation(bT[:], cv[:], ACT.Silu).then_inc(silu_done, 1)
            split(q + 2)
            act.wait_ge(slab_done, QUAD * (q + 2))
            nc.scalar.copy(stage[:, 1, 0, :], pair[1][0][:]).then_inc(pair_free[1], 1)
            act.wait_ge(xbc_back, 5)
            nc.scalar.copy(b_tok[:].rearrange("p g n -> p (g n)"), bank[6][:]).then_inc(back0_evac, 1)
            act.wait_ge(conv_done, 6)
            nc.scalar.activation(cT[:], cv[:], ACT.Silu).then_inc(silu_done, 1)

            act.wait_ge(qk_ready, TT)
            with act.Fori(0, D // NC // 2) as i:
                for par in range(2):
                    q = Q_Z + 4 * i + 2 * par
                    split(q + 1)
                    split(q + 2)
                    act.wait_ge(slab_done, QUAD * (q + 2))
                    for t in range(TT):
                        nc.scalar.activation(z[:, t, bass.ds(i * (2 * NC) + par * NC, NC)], pair[par][t][:], ACT.Silu).then_inc(pair_free[par], 1)

            with act.Fori(0, KVH // 2) as i:
                act.wait_ge(att_qkT, i + 1)
                nc.scalar.copy(att_qT[:, 0].rearrange("p a s -> p (a s)"), bank[4][:]).then_inc(att_qkT_evac, 1)
                nc.scalar.copy(att_kT, bank[6][:, 0:SEQ]).then_inc(att_qkT_evac, 1)
                for par in range(2):
                    u = 2 * i + par
                    act.wait_ge(att_max, u + 1)
                    for n in range(TT * REP):
                        s0, s1 = att_cols(n)
                        nc.scalar.activation(att_p[:, s0:s1], att_p[:, s0:s1], ACT.Exp, bias=att_s[:, 2, n:n + 1],
                                             accum_out=att_s[:, 4, n:n + 1])
                    nc.scalar.activation(att_s[:, 5, :], att_s[:, 3, :], ACT.Exp).then_inc(att_exp, 1)
                    act.wait_ge(att_pT, u + 1)
                    nc.scalar.copy(att_pTs[:, 0:NC], bank[4][:]).then_inc(att_pT_evac, 1)
            rounded_operand(TR_YATT)
            with act.Fori(0, D // NC) as i:
                split(Q_WOA + 2 * i + 1)
                split(Q_WOA + 2 * i + 2)

            act.wait_ge(acs_ready, 1)
            nc.scalar.activation(ds[:], sp[:, 0, 0:HEADS], ACT.Exp)
            nc.scalar.activation(ea[:], acs[:, 1, :], ACT.Exp).then_inc(sdecay, 1)
            for g in range(GROUPS):
                for t in range(TT):
                    n = TT * g + t
                    act.wait_ge(seg_ready, n + 1)
                    nc.scalar.activation(ssm_w, ssm_w, ACT.Exp).then_inc(seg_exp, 1)
                    if t == 0:
                        act.wait_ge(state_mm, g + 1)
                        nc.scalar.copy(ssm_state, bank[6][:]).then_inc(state_evac, 1)
                    act.wait_ge(y_gated, n + 1)
                    nc.scalar.activation(ssm_junk, z[:, t, g * NC:(g + 1) * NC], ACT.Square,
                                         accum_out=ssm_ss[:, t, g:g + 1]).then_inc(y_squared, 1)
            rounded_operand(TR_YSSM)
            with act.Fori(0, D // NC) as i:
                split(Q_WOS + 2 * i + 1)
                split(Q_WOS + 2 * i + 2)

            pairs_empty(U_FF)
            sum_squares(h, lambda t: xn_f[:, t])
            rounded_operand(TR_FFN)
            for n in range(D // NC):
                act.wait_ge(ple_mm, n + 1)
                for t in range(TT):
                    nc.scalar.copy(pe_tok[:, t, n * NC:(n + 1) * NC], pair[2 + n % 2][t][:]).then_inc(pair_free[2 + n % 2], 1)
            act.wait_ge(pair_free[2], 2 * (V_MIX + 1))
            act.wait_ge(pair_free[3], 2 * (V_MIX + 1))
            sum_squares(pe_tok, lambda t: (f_cv, f_stage)[t][:].rearrange("p k s -> p (k s)"))

            def ff_evac(par, q):
                act.wait_ge(slab_done, QUAD * (q + 2))
                nc.scalar.copy(f_stage[:, 0, par * FFB:(par + 1) * FFB], pair[par][0][:]).then_inc(pair_free[par], 1)

            def ff_gated(j):
                act.wait_ge(ff_conv, j + 1)
                nc.scalar.activation(f_silu[:], f_cv[:, 0:4], ACT.Silu).then_inc(ff_silu, 1)
                act.wait_ge(ff_mul, j + 1)
                nc.scalar.copy(f_hi[:], f_act[:]).then_inc(ff_hi, 1)

            q = Q_FF
            split(q + 1)
            split(q + 2)
            ff_evac(0, q)
            split(q + 3)
            split(q + 4)
            ff_evac(1, q + 2)
            with act.Fori(0, N_FF - 1) as j:
                q = Q_FF + 4 + 6 * j
                split(q + 1)
                ff_gated(j)
                split(q + 2)
                ff_evac(0, q)
                split(q + 3)
                split(q + 4)
                ff_evac(1, q + 2)
                split(q + 5)
                split(q + 6)
            q = Q_FF + 4 + 6 * (N_FF - 1)
            ff_gated(N_FF - 1)
            split(q + 1)
            split(q + 2)

            pairs_empty(U_GATE)
            sum_squares(h, lambda t: xn_f[:, t])
            rounded_operand(TR_PLE)
            for n in range(D // NC):
                q = Q_GATE + 2 * n
                split(q + 1)
                split(q + 2)
                act.wait_ge(slab_done, QUAD * (q + 2))
                if n:
                    act.wait_ge(gated, TT * n)
                for t in range(TT):
                    nc.scalar.activation(sig[:, t], pair[n % 2][t][:], ACT.Sigmoid).then_inc(sig_ready, 1)

            act.wait_ge(gated, TT * (D // NC))
            sum_squares(h, lambda t: qkv2[:, t, 0:D])
            act.wait_ge(small3_loaded, 6 * 16)
            nc.scalar.copy(s_hi[:], s_raw[:]).then_inc(s_hi_ready, 1)
            rounded_operand(TR_MIX2)
            q = Q_QKV2
            split(q + 1)
            split(q + 2)
            act.wait_ge(slab_done, QUAD * (q + 2))
            nc.scalar.copy(s_stage[:, 0, 0, :], pair[0][0][:]).then_inc(pair_free[0], 1)
            with act.Fori(0, 3) as i:
                for k in range(2):
                    c, par = 2 * i + k, (1 + k) % 2
                    q = Q_QKV2 + 2 * (2 * i + 1 + k)
                    split(q + 1)
                    act.wait_ge(conv2_done, c + 1)
                    nc.scalar.activation(s_act[:], s_cv[:], ACT.Silu).then_inc(silu2_done, 1)
                    split(q + 2)
                    act.wait_ge(slab_done, QUAD * (q + 2))
                    nc.scalar.copy(s_stage[:, par, 0, :], pair[par][0][:]).then_inc(pair_free[par], 1)
                    act.wait_ge(qkv2_back, c + 1)
                    nc.scalar.copy(qkv2[:, 0, bass.ds(c * NC, NC)], bank[6][:]).then_inc(back2_evac0, 1)
            q = Q_F + 2
            split(q + 1)
            split(q + 2)
            act.wait_ge(slab_done, QUAD * (q + 2))
            nc.scalar.copy(fr[:, 0, NC:], pair[1][0][:]).then_inc(pair_free[1], 1)
            for par in range(2):
                q = Q_Z2 + 2 * par
                split(q + 1)
                split(q + 2)
                act.wait_ge(slab_done, QUAD * (q + 2))
                for t in range(TT):
                    nc.scalar.activation(z2[:, t, par * NC:(par + 1) * NC], pair[par][t][:], ACT.Silu).then_inc(pair_free[par], 1)

            act.wait_ge(sc_mm, 1)
            act.wait_ge(sp_abs, 2)
            sc_view = bank[4][:, 0:TT * 4 * DNH].rearrange("p (t a) -> p t a", t=TT)
            nc.scalar.activation(beta[:].rearrange("p t d a -> p t (d a)"), sc_view[:, :, 0:2 * DNH], ACT.Sigmoid).then_inc(beta_ready, 1)
            nc.scalar.activation(aneg2[:], row[:, ROW["a_log_fwd_2"][0]:ROW["a_log_bwd_2"][1]], ACT.Exp).then_inc(aneg_ready, 1)
            softplus_parts(2, sp2)
            act.wait_ge(gc_mm, 1)
            flat = [x[:].rearrange("p a d h -> p (a d h)") for x in (be, kd, gl)]
            for x, c0 in zip(flat, (0, 32, 64)):
                last = nc.scalar.activation(x, bank[4][:, c0:c0 + x.shape[1]], ACT.Exp)
            last.then_inc(gc_exp, 1)
            for t in range(TT):
                nc.scalar.activation(mix[:, t], qkv2[:, t, 0:2 * DNW], ACT.Square).then_inc(dn_sq, 1)
            for n in range(0, 8, 2):
                act.wait_ge(dn_qkT, n + 1)
                nc.scalar.copy(qkh[:, 2 * n:2 * n + 2].rearrange("p a s -> p (a s)"), bank[4 + n % 4][:]).then_inc(dn_qkT_evac0, 1)

            with act.Fori(0, DNH) as i:
                act.wait_ge(dn_diff, 2 * i + 1)
                nc.scalar.activation(d_eN[:], d_eN[:], ACT.Exp, scale=-1.0).then_inc(dn_eN, 1)
                act.wait_ge(dn_diff, 2 * i + 2)
                nc.scalar.activation(d_eT[:], d_eT[:], ACT.Exp).then_inc(dn_eT, 1)
                nc.scalar.activation(d_qd[:].rearrange("p t d s -> p (t d s)"), bank[4][:], ACT.Exp).then_inc(dn_egb, 1)
                act.wait_ge(dn_rT, i + 1)
                nc.scalar.copy(d_r[:].rearrange("p t d s -> p (t d s)"), bank[6][:]).then_inc(dn_r, 1)
                for k in range(1, LEVELS):
                    act.wait_ge(dn_z, (LEVELS - 1) * i + k)
                    nc.scalar.copy(d_zz[:].rearrange("p t d s -> p (t d s)"), bank[7][:]).then_inc(dn_zz, 1)
                act.wait_ge(dn_uw, i + 1)
                nc.scalar.copy(d_wT[:].rearrange("p t d s -> p (t d s)"), bank[6][:]).then_inc(dn_wT, 1)
            for t in range(TT):
                act.wait_ge(dn_free, DNH + 1)
                nc.scalar.activation(mix[:, t, 0:DNW], qkv2[:, t, 0:DNW], ACT.Square).then_inc(o_sq, 1)
            for n in range(4):
                act.wait_ge(y_t, n + 1)
                nc.scalar.copy(y_hi[:, 2 * n:2 * n + 2].rearrange("p k s -> p (k s)"), bank[4 + n][:]).then_inc(y_hi_ready, 1)

            for g in range(DNH):
                act.wait_ge(f_mm, g + 1)
                nc.scalar.copy(f_half[:, g % 2].rearrange("p c s -> p (c s)"), bank[4 + g % 2][:]).then_inc(f_half_ready, 1)
                act.wait_ge(f_out, g + 1)
                nc.scalar.copy(fr_hi[:, g], bank[6 + g % 2][:, 0:SEQ]).then_inc(fr_hi_ready, 1)

            with act.Fori(0, D // NC) as n:
                q = Q_MIX + 6 * n
                for k, p in enumerate((0, 1)):
                    split(q + 2 * k + 1)
                    split(q + 2 * k + 2)
                    act.wait_ge(slab_done, QUAD * (q + 2 * k + 2))
                    act.wait_ge(pair_free[2 + p], 2 * (V_MIX + n + 1))
                    for t in range(TT):
                        nc.scalar.activation(z2[:, t, p * NC:(p + 1) * NC], pair[p][t][:], ACT.Sigmoid).then_inc(pair_free[p], 1)
                split(q + 5)
                split(q + 6)
            rounded_operand(TR_WO2)
            with act.Fori(0, D // NC) as i:
                split(Q_WO2 + 2 * i + 1)
                split(Q_WO2 + 2 * i + 2)

            pairs_empty(U_MLP)
            sum_squares(h, lambda t: xn_m[:, t])
            rounded_operand(TR_MLP)

            def mlp_evac(q):
                act.wait_ge(slab_done, QUAD * (q + 2))
                nc.scalar.copy(m_stage[:, 0], pair[2][0][:]).then_inc(pair_free[2], 1)

            def mlp_gated(j):
                act.wait_ge(ff_t, N_FF + j + 1)
                for b in range(2):
                    nc.scalar.activation(m_relu[:, 2 * b:2 * b + 2].rearrange("p k s -> p (k s)"), bank[6 + b][:], ACT.Relu).then_inc(mlp_relu, 1)
                act.wait_ge(ff_mul, N_FF + j + 1)
                nc.scalar.copy(m_hi[:], m_act[:]).then_inc(ff_hi, 1)

            q = Q_MLP
            split(q + 1)
            split(q + 2)
            mlp_evac(q)
            with act.Fori(0, N_FF2 - 1) as j:
                q = Q_MLP + 2 + 4 * j
                split(q + 1)
                mlp_gated(j)
                split(q + 2)
                mlp_evac(q)
                split(q + 3)
                split(q + 4)
            mlp_gated(N_FF2 - 1)
            split(N_QUADS - 1)
            pairs_empty(U_MLP + 2 * N_FF2)
            sum_squares(h, lambda t: xn_m[:, t])
        @block.vector
        def _(dve):
            step = Chain(dve, dve_step)
            V = nc.vector

            def split(q, s0=0, s1=QUAD):
                for s in range(s0, s1):
                    dve.wait_ge(hi_ready, QUAD * q + s + 1)
                    V.tensor_tensor(w_lo[:, s, :], w_raw[:, s, :], w_hi[:, s, :].bitcast(F32), ALU.subtract).then_inc(lo_ready, 1)

            def rest_of_operand(n):
                for i in range(KT // 2):
                    dve.wait_ge(a_hi_ready, KT // 2 * n + i + 1)
                    V.tensor_tensor(a_lo[:, 2 * i:2 * i + 2, :].rearrange("p k s -> p (k s)"), bank[4 + i % 4][:],
                                    a_hi[:, 2 * i:2 * i + 2, :].rearrange("p k s -> p (k s)").bitcast(F32),
                                    ALU.subtract).then_inc(a_lo_ready, 1)

            def normalize(dst, src, n, g):
                dve.wait_ge(rstd_ready, n + 1)
                dve.wait_ge(gain_loaded, 16 * (g + 1))
                for t in range(TT):
                    V.scalar_tensor_tensor(dst[:, t], src[:, t], rstd[:, t:t + 1], gain[:], ALU.mult, ALU.mult).then_inc(normed, 1)

            def softplus(n, buf, out):
                V.scalar_tensor_tensor(buf[:, 1], buf[:, 0], -1.0, buf[:, 0], ALU.mult, ALU.max).then_inc(sp_abs, 1)
                dve.wait_ge(sp_exp, n)
                V.tensor_scalar(buf[:, 3], buf[:, 2], 1.0, None, ALU.add).then_inc(sp_sum, 1)
                dve.wait_ge(sp_sum, n)
                step(V.tensor_scalar(buf[:, 5], buf[:, 3], -1.0, None, ALU.add))
                step(V.tensor_tensor(buf[:, 5], buf[:, 2], buf[:, 5], ALU.subtract))
                step(V.reciprocal(buf[:, 1], buf[:, 3]))
                step(V.tensor_tensor(buf[:, 5], buf[:, 5], buf[:, 1], ALU.mult))
                dve.wait_ge(sp_ln, n)
                step(V.tensor_tensor(buf[:, 5], buf[:, 5], buf[:, 4], ALU.add))
                step(V.scalar_tensor_tensor(out, buf[:, 0], 0.0, buf[:, 5], ALU.max, ALU.add))

            def add_to_h(p, col):
                for t in range(TT):
                    V.tensor_tensor(h[:, t, col], h[:, t, col], pair[p][t][:], ALU.add).then_inc(pair_free[p], 1)

            def project_into_h(q0):
                with dve.Fori(0, D // NC // 2) as i:
                    for par in range(2):
                        q = q0 + 4 * i + 2 * par
                        split(q + 1)
                        split(q + 2)
                        dve.wait_ge(slab_done, QUAD * (q + 2))
                        add_to_h(par, bass.ds(i * (2 * NC) + par * NC, NC))

            def convolve(dst, src, col, taps, back, done, bias):
                tiles = dst.shape[1]
                for n, j in enumerate([back] + [j for j in range(taps) if j != back]):
                    d = j - back
                    for ct in range(tiles):
                        w = col(ct, j)
                        if n == 0 and bias:
                            last = V.tensor_scalar(dst[:, ct], src(ct), w, col(ct, taps), ALU.mult, ALU.add)
                        elif n == 0:
                            last = V.tensor_scalar(dst[:, ct], src(ct), w, None, ALU.mult)
                        else:
                            o = slice(max(0, -d), SEQ - max(0, d))
                            s = slice(max(0, d), SEQ - max(0, -d))
                            last = V.scalar_tensor_tensor(dst[:, ct, o], src(ct)[:, s], w, dst[:, ct, o], ALU.mult, ALU.add)
                    if n < taps - 1:
                        step(last)
                last.then_inc(done, 1)

            def tile_in_bank(first):
                return lambda ct: bank[first + ct // 2][:, (ct % 2) * SEQ:(ct % 2 + 1) * SEQ]

            dve.wait_ge(w32_hi_ready, 1)
            V.tensor_tensor(w32_lo[:], w32_raw[:], w32_hi[:].bitcast(F32), ALU.subtract).then_inc(w32_lo_ready, 1)
            normalize(xs, h, 0, G_ATTN)
            split(0)
            rest_of_operand(TR_ATTN)
            dve.wait_ge(small1_loaded, 5 * 16)
            step(V.tensor_copy(pos_f[:], pos_i[:]))
            for t in range(TT):
                last = V.tensor_scalar(ang[:, 0, t], inv_freq[:], pos_f[:, t:t + 1], None, ALU.mult)
            step(last)
            step(V.tensor_scalar(ang[:, 1], ang[:, 0], float(1 / (2 * np.pi)), ROUND, ALU.mult, ALU.add))
            step(V.tensor_scalar(ang[:, 1], ang[:, 1], -ROUND, None, ALU.add))
            src = ang[:, 0]
            for part_2pi in TWO_PI:
                step(V.scalar_tensor_tensor(ang[:, 2], ang[:, 1], -part_2pi, src, ALU.mult, ALU.add))
                src = ang[:, 2]
            step(V.tensor_scalar(ang[:, 3], ang[:, 2], PI_BELOW, -PI_BELOW, ALU.min, ALU.max))
            step(V.scalar_tensor_tensor(ang[:, 4], ang[:, 3], -1.0, ang[:, 3], ALU.mult, ALU.max))
            V.tensor_scalar(ang[:, 5], ang[:, 4], -1.0, float(np.pi / 2), ALU.mult, ALU.add).then_inc(rope_arg, 1)
            with dve.Fori(0, QKV_W // NC // 2) as i:
                for par in range(2):
                    q = Q_QKV + 4 * i + 2 * par
                    split(q + 1)
                    split(q + 2)
                    dve.wait_ge(slab_done, QUAD * (q + 2))
                    V.tensor_copy(qkv[:, 1, bass.ds(i * (2 * NC) + par * NC, NC)], pair[par][1][:]).then_inc(pair_free[par], 1)
            dve.wait_ge(dt_mm, 1)
            for t in range(TT):
                last = V.tensor_tensor(sp[:, 0, t * HEADS:(t + 1) * HEADS], bank[4][:, t * HEADS:(t + 1) * HEADS],
                                       row[:, ROW["dt_bias"][0]:ROW["dt_bias"][1]], ALU.add)
            step(last)
            softplus(1, sp, dt[:].rearrange("p t a -> p (t a)"))
            dve.wait_ge(aneg_ready, 1)
            for t in range(TT):
                last = V.scalar_tensor_tensor(adt[:, t], dt[:, t], -1.0, aneg[:], ALU.mult, ALU.mult)
            last.then_inc(adt_ready, 1)
            for t in range(TT):
                dve.wait_ge(qk_sq, t + 1)
                V.tensor_reduce(qk_ss[:, t, :], work[:, 0:40 * HD].rearrange("p (a d) -> p a d", d=HD), AX.X, ALU.add).then_inc(qk_summed, 1)

            def xbc_convolve(c):
                dve.wait_ge(xbc_t, c + 1)
                convolve(cv, tile_in_bank(4), lambda ct, j: conv_col[:, bass.ds(c * 4 + ct, 1), j], CONV1, CONV1 - 1, conv_done, True)

            q = Q_XBC
            split(q + 1)
            split(q + 2)
            dve.wait_ge(slab_done, QUAD * (q + 2))
            V.tensor_copy(stage[:, 0, 1, :], pair[0][1][:]).then_inc(pair_free[0], 1)
            with dve.Fori(0, 2) as i:
                step.enter(i, 2 * (CONV1 - 1))
                for k in range(2):
                    c, par = 2 * i + k, (1 + k) % 2
                    q = Q_XBC + 2 * (2 * i + 1 + k)
                    split(q + 1)
                    xbc_convolve(c)
                    split(q + 2)
                    dve.wait_ge(slab_done, QUAD * (q + 2))
                    V.tensor_copy(stage[:, par, 1, :], pair[par][1][:]).then_inc(pair_free[par], 1)
                    dve.wait_ge(xbc_back, c + 1)
                    V.tensor_copy(xs[:, 1, bass.ds(c * NC, NC)], bank[7][:]).then_inc(back1_evac, 1)
                step.leave(2)
            q = Q_XBC + 10
            split(q + 1)
            xbc_convolve(4)
            split(q + 2)
            dve.wait_ge(slab_done, QUAD * (q + 2))
            V.tensor_copy(stage[:, 1, 1, :], pair[1][1][:]).then_inc(pair_free[1], 1)
            dve.wait_ge(silu_done, 5)
            xbc_convolve(5)

            with dve.Fori(0, D // NC) as i:
                split(Q_Z + 2 * i + 1)
                split(Q_Z + 2 * i + 2)

            scale = float(HD ** -0.5)
            s_max, s_m, s_neg, s_sink, s_sum, s_esink, s_tot, s_inv = range(8)
            with dve.Fori(0, KVH // 2) as i:
                step.enter(i, 2 * 6)
                dve.wait_ge(att_qkT, i + 1)
                V.tensor_copy(att_qT[:, 1].rearrange("p a s -> p (a s)"), bank[5][:]).then_inc(att_qkT_evac, 1)
                for par in range(2):
                    u = 2 * i + par
                    dve.wait_ge(att_scored, u + 1)
                    V.scalar_tensor_tensor(att_p[:, 0:NC].rearrange("p (a k) -> p a k", a=REP),
                                           bank[4][:].rearrange("p (a k) -> p a k", a=REP), scale,
                                           att_mask[:, 0].unsqueeze(1).to_broadcast([P, REP, P]), ALU.mult, ALU.add)
                    for b in range(2):
                        last = V.scalar_tensor_tensor(
                            att_p[:, (b + 1) * NC:(b + 2) * NC].rearrange("p (a k) -> p a k", a=2),
                            bank[5 + b][:].rearrange("p (a k) -> p a k", a=2), scale,
                            att_mask[:, 1:3].rearrange("p b k -> p (b k)").unsqueeze(1).to_broadcast([P, 2, 2 * P]),
                            ALU.mult, ALU.add)
                    step(last)
                    V.tensor_reduce(att_s[:, s_max, 0:REP], att_p[:, 0:NC].rearrange("p (a k) -> p a k", a=REP), AX.X, ALU.max)
                    step(V.tensor_reduce(att_s[:, s_max, REP:2 * REP], att_p[:, NC:3 * NC].rearrange("p (a k) -> p a k", a=REP), AX.X, ALU.max))
                    sink = row[:, bass.ds(i * (2 * REP) + ROW["sinks"][0] + par * REP, REP)].unsqueeze(1).to_broadcast([P, TT, REP])

                    def by_tile(k):
                        return att_s[:, k, :].rearrange("p (t a) -> p t a", t=TT)
                    step(V.tensor_tensor(by_tile(s_m), by_tile(s_max), sink, ALU.max))
                    step(V.tensor_scalar(att_s[:, s_neg], att_s[:, s_m], -1.0, None, ALU.mult))
                    V.tensor_tensor(by_tile(s_sink), by_tile(s_neg), sink, ALU.add).then_inc(att_max, 1)
                    dve.wait_ge(att_exp, u + 1)
                    step(V.tensor_tensor(att_s[:, s_tot], att_s[:, s_sum], att_s[:, s_esink], ALU.add))
                    step(V.reciprocal(att_s[:, s_inv], att_s[:, s_tot]))
                    dve.wait_ge(att_pT, u + 1)
                    for b in range(2):
                        V.tensor_copy(att_pTs[:, (b + 1) * NC:(b + 2) * NC], bank[5 + b][:]).then_inc(att_pT_evac, 1)
                    dve.wait_ge(att_pv, u + 1)
                    for t in range(TT):
                        inv = att_s[:, s_inv, t * REP:(t + 1) * REP].unsqueeze(2).to_broadcast([P, REP, HD])
                        last = V.tensor_tensor(
                            qkv[:, t, bass.ds(i * (2 * REP * HD) + par * REP * HD, REP * HD)].rearrange("p (a d) -> p a d", d=HD),
                            bank[7][:, t * REP * HD:(t + 1) * REP * HD].rearrange("p (a d) -> p a d", d=HD), inv, ALU.mult)
                    last.then_inc(att_done, 1)
                step.leave(KVH // 2)
            rest_of_operand(TR_YATT)
            project_into_h(Q_WOA)

            dve.wait_ge(acs_mm, 1)
            step(V.tensor_copy(acs[:].rearrange("p t a -> p (t a)"), bank[4][:, 0:TT * HEADS]))
            V.tensor_tensor(sp[:, 0, 0:HEADS], bank[4][:, TT * HEADS:(TT + 1) * HEADS], acs[:, 0], ALU.subtract).then_inc(acs_ready, 1)
            dve.wait_ge(cb_mm, 1)
            for b in range(2):
                last = V.tensor_tensor(ssm_cb[:, 2 * b:2 * b + 2].rearrange("p g t s -> p (g t) s"),
                                       bank[5 + b][:].rearrange("p (g s) -> p g s", s=P),
                                       before[:].unsqueeze(1).to_broadcast([P, 4, P]), ALU.mult)
            last.then_inc(cb_ready, 1)
            for g in range(GROUPS):
                cols = slice(g * NC, (g + 1) * NC)
                for t in range(TT):
                    n = TT * g + t
                    dve.wait_ge(row_mm, n + 1)
                    if n:
                        dve.wait_ge(ydiag_mm, n)
                    for a in range(HPG):
                        last = V.tensor_scalar(ssm_w[:, a], bank[4 + a // 4][:, (a % 4) * P:(a % 4 + 1) * P],
                                               acs[:, t, g * HPG + a:g * HPG + a + 1], 0.0, ALU.subtract, ALU.min)
                    last.then_inc(seg_ready, 1)
                    dve.wait_ge(ydiag_mm, n + 1)
                    dve.wait_ge(dskip_ready, g + 1)
                    step(V.tensor_tensor(ssm_y, bank[7][:], ssm_dx[:, t], ALU.add))
                    if t == 1:
                        dve.wait_ge(yoff_mm, g + 1)
                        w = ea[:, g * HPG:(g + 1) * HPG].unsqueeze(2).to_broadcast([P, HPG, HD])
                        step(V.tensor_tensor(ssm_off.rearrange("p (a d) -> p a d", d=HD),
                                             bank[6][:].rearrange("p (a d) -> p a d", d=HD), w, ALU.mult))
                        step(V.tensor_tensor(ssm_y, ssm_y, ssm_off, ALU.add))
                    V.tensor_tensor(z[:, t, cols], z[:, t, cols], ssm_y, ALU.mult).then_inc(y_gated, 1)
            dve.wait_ge(ssm_rstd, 1)
            dve.wait_ge(gain_loaded, 16 * (G_SSM + 1))
            for g in range(GROUPS):
                cols = slice(g * NC, (g + 1) * NC)
                for t in range(TT):
                    V.scalar_tensor_tensor(z[:, t, cols], z[:, t, cols], ssm_rs[:, t, g:g + 1], gain[:, cols],
                                           ALU.mult, ALU.mult).then_inc(normed, 1)
            rest_of_operand(TR_YSSM)
            project_into_h(Q_WOS)

            normalize(xn_f, h, 1, G_FFN)
            rest_of_operand(TR_FFN)
            normalize(pe_tok, pe_tok, 2, G_POST)

            def ff_evac(par, q):
                dve.wait_ge(slab_done, QUAD * (q + 2))
                V.tensor_copy(f_stage[:, 1, par * FFB:(par + 1) * FFB], pair[par][1][:]).then_inc(pair_free[par], 1)

            def ff_gated(j):
                dve.wait_ge(ff_t, j + 1)
                convolve(f_cv, tile_in_bank(4), lambda ct, k: ff_col[:, bass.ds(j, 1), ct, k], CONV_FF, CONV_FF - 1, ff_conv, True)
                dve.wait_ge(ff_conv, j + 1)
                dve.wait_ge(ff_silu, j + 1)
                V.tensor_tensor(f_act[:], f_silu[:], f_cv[:, 4:8], ALU.mult).then_inc(ff_mul, 1)
                dve.wait_ge(ff_hi, j + 1)
                V.tensor_tensor(f_lo[:], f_act[:], f_hi[:].bitcast(F32), ALU.subtract).then_inc(ff_lo, 1)

            def ff_down(q):
                for n in range(D // NC):
                    split(q + 1 + n // 2, 2 * (n % 2), 2 * (n % 2) + 2)
                    dve.wait_ge(slab_done, QUAD * q + 2 * (n + 1))
                    add_to_h(n % 2, slice(n * NC, (n + 1) * NC))

            q = Q_FF
            split(q + 1)
            split(q + 2)
            ff_evac(0, q)
            split(q + 3)
            split(q + 4)
            ff_evac(1, q + 2)
            dve.wait_ge(small2_loaded, 3 * 16)
            with dve.Fori(0, N_FF - 1) as j:
                step.enter(j, CONV_FF - 1)
                q = Q_FF + 4 + 6 * j
                split(q + 1)
                ff_gated(j)
                split(q + 2)
                ff_evac(0, q)
                split(q + 3)
                split(q + 4)
                ff_evac(1, q + 2)
                ff_down(q + 4)
                step.leave(N_FF - 1)
            ff_gated(N_FF - 1)
            ff_down(Q_GATE - 2)

            normalize(xn_f, h, 3, G_PLE)
            rest_of_operand(TR_PLE)
            for n in range(D // NC):
                q = Q_GATE + 2 * n
                split(q + 1)
                split(q + 2)
                dve.wait_ge(sig_ready, TT * (n + 1))
                cols = slice(n * NC, (n + 1) * NC)
                for t in range(TT):
                    last = V.tensor_tensor(sig[:, t], sig[:, t], pe_tok[:, t, cols], ALU.mult)
                step(last)
                for t in range(TT):
                    V.tensor_tensor(h[:, t, cols], h[:, t, cols], sig[:, t], ALU.add).then_inc(gated, 1)

            xn2 = qkv2[:, :, 0:D]
            normalize(xn2, h, 4, G_MIX2)
            dve.wait_ge(s_hi_ready, 1)
            V.tensor_tensor(s_lo[:], s_raw[:], s_hi[:].bitcast(F32), ALU.subtract).then_inc(s_lo_ready, 1)
            rest_of_operand(TR_MIX2)
            q = Q_QKV2
            split(q + 1)
            split(q + 2)
            dve.wait_ge(slab_done, QUAD * (q + 2))
            V.tensor_copy(s_stage[:, 0, 1, :], pair[0][1][:]).then_inc(pair_free[0], 1)
            dve.wait_ge(small3_loaded, 6 * 16)
            with dve.Fori(0, 3) as i:
                step.enter(i, 2 * (CONV2 - 1))
                for k in range(2):
                    c, par = 2 * i + k, (1 + k) % 2
                    q = Q_QKV2 + 2 * (2 * i + 1 + k)
                    split(q + 1)
                    dve.wait_ge(qkv2_t, c + 1)
                    convolve(s_cv, tile_in_bank(4), lambda ct, j: conv2_col[:, bass.ds(c * 4 + ct, 1), j], CONV2, CONV2 // 2, conv2_done, False)
                    split(q + 2)
                    dve.wait_ge(slab_done, QUAD * (q + 2))
                    V.tensor_copy(s_stage[:, par, 1, :], pair[par][1][:]).then_inc(pair_free[par], 1)
                    dve.wait_ge(qkv2_back, c + 1)
                    V.tensor_copy(qkv2[:, 1, bass.ds(c * NC, NC)], bank[7][:]).then_inc(back2_evac1, 1)
                step.leave(3)
            q = Q_F + 2
            split(q + 1)
            split(q + 2)
            dve.wait_ge(slab_done, QUAD * (q + 2))
            V.tensor_copy(fr[:, 1, NC:], pair[1][1][:]).then_inc(pair_free[1], 1)
            for par in range(2):
                q = Q_Z2 + 2 * par
                split(q + 1)
                split(q + 2)

            dve.wait_ge(sc_mm, 1)
            sc_view = bank[4][:, 0:TT * 4 * DNH].rearrange("p (t a) -> p t a", t=TT)
            bias = row[:, ROW["dt_bias_fwd_2"][0]:ROW["dt_bias_bwd_2"][1]].unsqueeze(1).to_broadcast([P, TT, 2 * DNH])
            step(V.tensor_tensor(sp2[:, 0].rearrange("p (t a) -> p t a", t=TT), sc_view[:, :, 2 * DNH:], bias, ALU.add))
            g2_tok = g2[:].rearrange("p t d a -> p t (d a)")
            softplus(2, sp2, g2[:].rearrange("p t d a -> p (t d a)"))
            dve.wait_ge(aneg_ready, 2)
            dve.wait_ge(beta_ready, 1)
            V.scalar_tensor_tensor(g2_tok, g2_tok, -1.0, aneg2[:].unsqueeze(1).to_broadcast([P, TT, 2 * DNH]),
                                   ALU.mult, ALU.mult).then_inc(g2_ready, 1)
            dve.wait_ge(gc_exp, 1)
            V.tensor_copy(gc[:].rearrange("p t d a -> p (t d a)"), bank[4][:, 0:32])
            V.tensor_tensor(be[:].rearrange("p t d a -> p (t d a)"), be[:].rearrange("p t d a -> p (t d a)"),
                            beta[:].rearrange("p t d a -> p (t d a)"), ALU.mult).then_inc(dn_pre, 1)
            for t in range(TT):
                dve.wait_ge(dn_sq, t + 1)
                V.tensor_reduce(dn_ss[:, t], mix[:, t].rearrange("p (a d) -> p a d", d=DND), AX.X, ALU.add).then_inc(dn_summed, 1)
            for n in range(1, 8, 2):
                dve.wait_ge(dn_qkT, n + 1)
                V.tensor_copy(qkh[:, 2 * n:2 * n + 2].rearrange("p a s -> p (a s)"), bank[4 + n % 4][:]).then_inc(dn_qkT_evac1, 1)

            shape = [P, TT, 2, P]

            def units(b):
                return bank[b][:].rearrange("p (t d s) -> p t d s", t=TT, d=2)
            with dve.Fori(0, DNH) as i:
                dve.wait_ge(dn_gcb, i + 1)
                for t in range(TT):
                    for d in range(2):
                        last = V.tensor_scalar(d_eN[:, t, d], units(4)[:, t, d], gc[:, t, d, bass.ds(i, 1)], 0.0, ALU.subtract, ALU.max)
                last.then_inc(dn_diff, 1)
                for t in range(TT):
                    for d in range(2):
                        last = V.tensor_scalar(d_eT[:, t, d], units(4)[:, t, d], gc[:, t, d, bass.ds(i, 1)], 0.0, ALU.subtract, ALU.min)
                last.then_inc(dn_diff, 1)
                dve.wait_ge(dn_kk, i + 1)
                dve.wait_ge(dn_eN, i + 1)
                for t in range(TT):
                    for d in range(2):
                        last = V.scalar_tensor_tensor(d_m[:, t, d], bank[5][:, t * P:(t + 1) * P], beta[:, t, d, bass.ds(i, 1)],
                                                      d_eN[:, t, d], ALU.mult, ALU.mult)
                last.then_inc(dn_m, 1)
                dve.wait_ge(dn_mk, LEVELS * i + 1)
                V.tensor_tensor(d_t[:].rearrange("p t d s -> p (t d) s"), ident[:].unsqueeze(1).to_broadcast([P, 2 * TT, P]),
                                d_mk[:].rearrange("p t d s -> p (t d) s"), ALU.subtract).then_inc(dn_t, 1)
                dve.wait_ge(dn_eTm, i + 1)
                for t in range(TT):
                    qk = bank[5][:, (TT + t) * P:(TT + t + 1) * P].unsqueeze(1).to_broadcast([P, 2, P])
                    last = V.tensor_tensor(d_eT[:, t], qk, d_eT[:, t], ALU.mult)
                last.then_inc(dn_qkm, 1)
                for k in range(1, LEVELS):
                    dve.wait_ge(dn_rz, (LEVELS - 1) * i + k)
                    V.tensor_tensor(d_r[:], d_r[:], units(6), ALU.subtract).then_inc(dn_r, 1)
                    if k < LEVELS - 1:
                        dve.wait_ge(dn_tz, (LEVELS - 2) * i + k)
                        V.tensor_tensor(d_t[:], d_t[:], units(4), ALU.subtract).then_inc(dn_t, 1)
                dve.wait_ge(dn_uw, i + 1)
                V.tensor_copy(d_u[:].rearrange("p t d s -> p (t d s)"), bank[7][:]).then_inc(dn_u, 1)
                steps = SEQ // CHUNK
                for n in range(steps):
                    if n:
                        dve.wait_ge(dn_ws, (steps - 1) * i + n)
                        for d in range(2):
                            c, t, r = rows_of(n, d)
                            last = V.tensor_tensor(d_vn[r, d], d_u[r, t, d], bank[4][r, d * P:(d + 1) * P], ALU.subtract)
                        last.then_inc(dn_vn, 1)
                    dve.wait_ge(dn_so, steps * i + n + 1)
                    if n == 0:
                        for d in range(2):
                            last = V.tensor_copy(d_s[:, d], bank[6 + d][:, 0:P])
                        last.then_inc(dn_s, 1)
                    elif n < steps - 1:
                        for d in range(2):
                            c, t, r = rows_of(n, d)
                            last = V.scalar_tensor_tensor(d_s[:, d], d_s[:, d], gl[:, c, d, bass.ds(i, 1)],
                                                          bank[6 + d][:, 0:P], ALU.mult, ALU.add)
                        last.then_inc(dn_s, 1)
                    for d in range(2):
                        c, t, r = rows_of(n, d)
                        o = qkv2[r, t, bass.ds(i * DND, DND)]
                        b = bank[5][r, d * P:(d + 1) * P]
                        if n < steps // 2:
                            last = V.tensor_copy(o, b)
                        else:
                            last = V.tensor_tensor(o, o, b, ALU.add)
                    if n == steps - 1:
                        last.then_inc(dn_free, 1)

            for t in range(TT):
                dve.wait_ge(o_sq, t + 1)
                V.tensor_reduce(dn_ss[:, t, 0:DNH], mix[:, t, 0:DNW].rearrange("p (a d) -> p a d", d=DND), AX.X, ALU.add).then_inc(o_summed, 1)
            for t in range(TT):
                dve.wait_ge(o_rstd, t + 1)
                o = qkv2[:, t, 0:DNW].rearrange("p (a d) -> p a d", d=DND)
                step(V.tensor_tensor(o, o, dn_rs[:, t, 0:DNH].unsqueeze(2).to_broadcast([P, DNH, DND]), ALU.mult))
                dve.wait_ge(z2_scaled, t + 1)
                V.tensor_tensor(qkv2[:, t, 0:DNW], qkv2[:, t, 0:DNW], z2[:, t], ALU.mult).then_inc(y_ready, 1)
            for n in range(4):
                dve.wait_ge(y_hi_ready, n + 1)
                V.tensor_tensor(y_lo[:, 2 * n:2 * n + 2].rearrange("p k s -> p (k s)"), bank[4 + n][:],
                                y_hi[:, 2 * n:2 * n + 2].rearrange("p k s -> p (k s)").bitcast(F32), ALU.subtract).then_inc(y_lo_ready, 1)
            for g in range(DNH):
                dve.wait_ge(fr_hi_ready, g + 1)
                V.tensor_tensor(fr_lo[:, g], bank[6 + g % 2][:, 0:SEQ], fr_hi[:, g].bitcast(F32), ALU.subtract).then_inc(fr_lo_ready, 1)

            with dve.Fori(0, D // NC) as n:
                step.enter(n, 1)
                q = Q_MIX + 6 * n
                for k in range(1, 5):
                    split(q + k)
                for k, p in enumerate((2, 3)):
                    split(q + 5 + k)
                    dve.wait_ge(slab_done, QUAD * (q + 5 + k))
                    dve.wait_ge(pair_free[p - 2], 2 * (U_MIX + n + 1) + 2)
                    for t in range(TT):
                        last = V.tensor_tensor(fr[:, t, k * NC:(k + 1) * NC], z2[:, t, k * NC:(k + 1) * NC], pair[p][t][:],
                                               ALU.mult).then_inc(pair_free[p], 1)
                dve.wait_ge(pair_free[3], 2 * (V_MIX + n + 1) + 2)
                dve.wait_ge(pair_free[2], 2 * (V_MIX + n + 1) + 2)
                step(V.tensor_tensor(mix[:, 0, bass.ds(n * NC, NC)], fr[:, 0, 0:NC], fr[:, 0, NC:], ALU.add))
                V.tensor_tensor(mix[:, 1, bass.ds(n * NC, NC)], fr[:, 1, 0:NC], fr[:, 1, NC:], ALU.add).then_inc(mix_ready, 1)
                step.leave(D // NC)
            rest_of_operand(TR_WO2)
            project_into_h(Q_WO2)

            normalize(xn_m, h, 5, G_MLP)
            rest_of_operand(TR_MLP)

            def mlp_evac(q):
                dve.wait_ge(slab_done, QUAD * (q + 2))
                V.tensor_copy(m_stage[:, 1], pair[2][1][:]).then_inc(pair_free[2], 1)

            def mlp_gated(j):
                dve.wait_ge(ff_hi, N_FF + j + 1)
                V.tensor_tensor(m_lo[:], m_act[:], m_hi[:].bitcast(F32), ALU.subtract).then_inc(ff_lo, 1)

            def mlp_down(q, quads):
                for n in range(D // NC):
                    if n // 2 < quads:
                        split(q + 1 + n // 2, 2 * (n % 2), 2 * (n % 2) + 2)
                    dve.wait_ge(slab_done, QUAD * q + 2 * (n + 1))
                    add_to_h(n % 2, slice(n * NC, (n + 1) * NC))

            q = Q_MLP
            split(q + 1)
            split(q + 2)
            mlp_evac(q)
            with dve.Fori(0, N_FF2 - 1) as j:
                q = Q_MLP + 2 + 4 * j
                split(q + 1)
                mlp_gated(j)
                split(q + 2)
                mlp_evac(q)
                mlp_down(q + 2, 2)
            mlp_gated(N_FF2 - 1)
            mlp_down(N_QUADS - 2, 1)
            normalize(xn_m, h, 6, G_OUT)
        @block.tensor
        def _(pe):
            T = nc.tensor

            def slab(q, s, products, psum, start, stop):
                pe.wait_ge(lo_ready, QUAD * q + s + 1)
                for j, (left_hi, left_lo) in enumerate(products):
                    wh = w_hi[:, s, j * NC:(j + 1) * NC]
                    wl = w_lo[:, s, j * NC:(j + 1) * NC]
                    for t in range(TT):
                        ts = slice(t * P, (t + 1) * P)
                        first = start and j == 0
                        final = stop and j == SLAB_KT - 1
                        T.matmul(psum[t][:], left_hi[:, ts], wh, start=first, stop=False)
                        T.matmul(psum[t][:], left_hi[:, ts], wl, start=False, stop=False)
                        last = T.matmul(psum[t][:], left_lo[:, ts], wh, start=False, stop=final)
                last.then_inc(slab_done, 1)

            def chunk(q, p, use, left_hi, left_lo, k_tiles=KT, between=None):
                pe.wait_ge(pair_free[p], 2 * (use + 1))
                for n in range(k_tiles // SLAB_KT):
                    if between and n and n % QUAD == 0:
                        between()
                    k = n * SLAB_KT
                    slab(q + n // QUAD, n % QUAD, [(left_hi[:, k + j], left_lo[:, k + j]) for j in range(SLAB_KT)],
                         pair[p], n == 0, n == k_tiles // SLAB_KT - 1)

            def transpose_operand(n, src):
                for i in range(KT // 2):
                    if i >= 4:
                        pe.wait_ge(a_lo_ready, KT // 2 * n + i - 3)
                    for k in range(2):
                        for t in range(TT):
                            last = T.transpose(bank[4 + i % 4][:, k * SEQ + t * P:k * SEQ + (t + 1) * P],
                                               src[:, t, (2 * i + k) * P:(2 * i + k + 1) * P], ident[:])
                    last.then_inc(tr_ready, 1)
                pe.wait_ge(a_lo_ready, KT // 2 * (n + 1))

            def narrow(psum, hi, lo, width):
                for t in range(TT):
                    ts = slice(t * P, (t + 1) * P)
                    o = psum[:, t * width:(t + 1) * width]
                    for k in range(KT):
                        T.matmul(o, a_hi[:, k, ts], hi[:, k], start=k == 0, stop=False)
                        T.matmul(o, a_hi[:, k, ts], lo[:, k], start=False, stop=False)
                        last = T.matmul(o, a_lo[:, k, ts], hi[:, k], start=False, stop=k == KT - 1)
                return last

            def project(q0, use, chunks):
                with pe.Fori(0, chunks // 2) as i:
                    for par in range(2):
                        chunk(q0 + 4 * i + 2 * par, par, use + i, a_hi, a_lo)

            def to_channels(src, col0, first):
                for ct in range(4):
                    for t in range(TT):
                        last = T.transpose(bank[first + ct // 2][:, (ct % 2) * SEQ + t * P:(ct % 2) * SEQ + (t + 1) * P],
                                           src[:, t, col0 + ct * P:col0 + (ct + 1) * P], ident[:])
                return last

            def to_tokens(src, tiles):
                for t in range(tiles):
                    for ct in range(4):
                        last = T.transpose(bank[6 + t][:, ct * P:(ct + 1) * P], src[:, ct, t * P:(t + 1) * P], ident[:])
                return last

            pe.wait_ge(normed, NORMED[G_ATTN])
            transpose_operand(TR_ATTN, xs)
            project(Q_QKV, U_QKV, QKV_W // NC)
            pe.wait_ge(w32_lo_ready, 1)
            narrow(bank[4], w32_hi, w32_lo, HEADS).then_inc(dt_mm, 1)

            chunk(Q_XBC, 0, U_XBC, a_hi, a_lo)
            pe.wait_ge(adt_ready, 1)
            with pe.Fori(0, 2) as i:
                for k in range(2):
                    c, par = 2 * i + k, (1 + k) % 2

                    def channels():
                        pe.wait_ge(pair_free[1 - par], 2 * (U_XBC + i + 1) + 2)
                        to_channels(stage[:, 1 - par], 0, 4).then_inc(xbc_t, 1)
                    chunk(Q_XBC + 2 * (2 * i + 1 + k), par, U_XBC + i + k, a_hi, a_lo, between=channels)
                    pe.wait_ge(silu_done, c + 1)
                    pe.wait_ge(back0_evac, c + 1)
                    pe.wait_ge(back1_evac, c + 1)
                    to_tokens(cv_act, TT).then_inc(xbc_back, 1)

            def channels_of_b():
                pe.wait_ge(pair_free[0], 2 * (U_Z) + 2)
                to_channels(stage[:, 0], 0, 4).then_inc(xbc_t, 1)
            chunk(Q_XBC + 10, 1, U_XBC + 2, a_hi, a_lo, between=channels_of_b)
            pe.wait_ge(silu_done, 5)
            pe.wait_ge(back0_evac, 4 + 1)
            pe.wait_ge(back1_evac, 4 + 1)
            to_tokens(bT, 1).then_inc(xbc_back, 1)
            pe.wait_ge(pair_free[1], 2 * (U_Z) + 2)
            to_channels(stage[:, 1], 0, 4).then_inc(xbc_t, 1)

            project(Q_Z, U_Z, D // NC)

            pe.wait_ge(silu_done, 6)
            with pe.Fori(0, KVH // 2) as i:
                pe.wait_ge(att_staged, i + 1)
                for t in range(TT):
                    for a in range(REP):
                        T.transpose(bank[4 + t][:, a * P:(a + 1) * P], att_q[:, t, a].rearrange("p b d -> p (b d)"), ident[:])
                for t in range(TT):
                    last = T.transpose(bank[6][:, t * P:(t + 1) * P], att_k[:, t], ident[:])
                last.then_inc(att_qkT, 1)
                pe.wait_ge(att_qkT_evac, 3 * i + 6)
                for par in range(2):
                    u = 2 * i + par
                    rows = slice(par * HD, (par + 1) * HD)
                    for a in range(REP):
                        T.matmul(bank[4][:, a * P:(a + 1) * P], att_qT[rows, 0, a], att_kT[rows, 0:P], start=True, stop=True)
                    for a in range(REP):
                        last = T.matmul(bank[5 + a // 2][:, (a % 2) * SEQ:(a % 2 + 1) * SEQ], att_qT[rows, 1, a],
                                        att_kT[rows, 0:SEQ], start=True, stop=True)
                    last.then_inc(att_scored, 1)
                    pe.wait_ge(att_exp, u + 1)
                    for a in range(REP):
                        T.transpose(bank[4][:, a * P:(a + 1) * P], att_p[:, a * P:(a + 1) * P], ident[:])
                    for a in range(REP):
                        for b in range(2):
                            c = (2 * a + b) * P
                            last = T.transpose(bank[5 + c // NC][:, c % NC:c % NC + P], att_p[:, NC + c:NC + c + P], ident[:])
                    last.then_inc(att_pT, 1)
                    pe.wait_ge(att_pT_evac, 3 * u + 3)
                    for a in range(REP):
                        v = [qkv[:, t, bass.ds(i * (2 * HD) + (HEADS + KVH) * HD + par * HD, HD)] for t in range(TT)]
                        T.matmul(bank[7][:, a * HD:(a + 1) * HD], att_pTs[:, a * P:(a + 1) * P], v[0], start=True, stop=True)
                        o = bank[7][:, (REP + a) * HD:(REP + a + 1) * HD]
                        for b in range(TT):
                            c = NC + (2 * a + b) * P
                            last = T.matmul(o, att_pTs[:, c:c + P], v[b], start=b == 0, stop=b == TT - 1)
                    last.then_inc(att_pv, 1)
            pe.wait_ge(att_done, KVH)
            transpose_operand(TR_YATT, qkv)
            project(Q_WOA, U_WOA, D // NC)

            pe.wait_ge(adt_ready, 1)
            for t in range(TT):
                T.matmul(bank[4][:, t * HEADS:(t + 1) * HEADS], before[:], adt[:, t], start=True, stop=True)
            T.matmul(bank[4][:, TT * HEADS:(TT + 1) * HEADS], ones[:], adt[:, 0], start=True, stop=True).then_inc(acs_mm, 1)
            for g in range(GROUPS):
                for t in range(TT):
                    ts = slice(t * P, (t + 1) * P)
                    c = (TT * g + t) * P
                    last = T.matmul(bank[5 + c // NC][:, c % NC:c % NC + P], bT[:, g, ts], cT[:, g, ts], start=True, stop=True)
            last.then_inc(cb_mm, 1)
            pe.wait_ge(cb_ready, 1)
            for g in range(GROUPS):
                for t in range(TT):
                    n = TT * g + t
                    pe.wait_ge(row_scaled, n + 1)
                    if n:
                        pe.wait_ge(y_gated, n)
                    for b in range(2):
                        last = T.matmul(bank[4 + b][:], ones[:], ssm_rows[:, 4 * b:4 * b + 4].rearrange("p a s -> p (a s)"),
                                        start=True, stop=True)
                    last.then_inc(row_mm, 1)
                    if t == 0:
                        pe.wait_ge(xds_ready, g + 1)
                        T.matmul(bank[6][:], b_tok[:, g], ssm_xds, start=True, stop=True).then_inc(state_mm, 1)
                    else:
                        pe.wait_ge(state_evac, g + 1)
                        T.matmul(bank[6][:], cT[:, g, P:2 * P], ssm_state, start=True, stop=True).then_inc(yoff_mm, 1)
                    pe.wait_ge(seg_w, n + 1)
                    for a in range(HPG):
                        cols = slice(a * HD, (a + 1) * HD)
                        last = T.matmul(bank[7][:, cols], ssm_w[:, a], ssm_xd[:, t, cols], start=True, stop=True)
                    last.then_inc(ydiag_mm, 1)
            pe.wait_ge(normed, NORMED[G_SSM])
            transpose_operand(TR_YSSM, z)
            project(Q_WOS, U_WOS, D // NC)

            pe.wait_ge(normed, NORMED[G_FFN])
            transpose_operand(TR_FFN, xn_f)
            pe.wait_ge(small2_loaded, 3 * 16)
            for n in range(D // NC):
                pe.wait_ge(pair_free[2 + n % 2], 2 * (V_PLE + n // 2 + 1))
                for t in range(TT):
                    for k in range(PLE // P):
                        last = T.matmul(pair[2 + n % 2][t][:], p_T[:, k, t * P:(t + 1) * P], w_proj[:, k, n * NC:(n + 1) * NC],
                                        start=k == 0, stop=k == PLE // P - 1)
                last.then_inc(ple_mm, 1)

            def ff_down(q, use):
                for n in range(D // NC):
                    pe.wait_ge(pair_free[n % 2], 2 * (use + n // 2 + 1))
                    for s in range(2):
                        slab(q + n // 2, 2 * (n % 2) + s, [(f_hi[:, 2 * s + k], f_lo[:, 2 * s + k]) for k in range(SLAB_KT)],
                             pair[n % 2], s == 0, s == 1)

            def ff_channels(use):
                for p in range(2):
                    pe.wait_ge(pair_free[p], 2 * (use + 1))
                to_channels(f_stage, 0, 4)
                to_channels(f_stage, FFB, 6).then_inc(ff_t, 1)

            chunk(Q_FF, 0, U_FF, a_hi, a_lo)
            chunk(Q_FF + 2, 1, U_FF, a_hi, a_lo)
            pe.wait_ge(pair_free[2], 2 * (V_MIX + 1))
            pe.wait_ge(pair_free[3], 2 * (V_MIX + 1))
            ff_channels(U_FF + 1)
            with pe.Fori(0, N_FF - 1) as j:
                q, use = Q_FF + 4 + 6 * j, U_FF + 1 + 3 * j
                chunk(q, 0, use, a_hi, a_lo)
                chunk(q + 2, 1, use, a_hi, a_lo)
                pe.wait_ge(ff_lo, j + 1)
                ff_down(q + 4, use + 1)
                ff_channels(use + 3)
            pe.wait_ge(ff_lo, N_FF)
            ff_down(Q_GATE - 2, U_GATE - 2)

            pe.wait_ge(normed, NORMED[G_PLE])
            transpose_operand(TR_PLE, xn_f)
            for n in range(D // NC):
                if n >= 2:
                    pe.wait_ge(sig_ready, TT * (n - 1))
                chunk(Q_GATE + 2 * n, n % 2, U_GATE, a_hi, a_lo)

            pe.wait_ge(normed, NORMED[G_MIX2])
            transpose_operand(TR_MIX2, qkv2)
            chunk(Q_QKV2, 0, U_QKV2, a_hi, a_lo)
            with pe.Fori(0, 3) as i:
                for k in range(2):
                    c, par = 2 * i + k, (1 + k) % 2

                    def channels2():
                        pe.wait_ge(pair_free[1 - par], 2 * (U_QKV2 + i + 1) + 2)
                        to_channels(s_stage[:, 1 - par], 0, 4).then_inc(qkv2_t, 1)
                    chunk(Q_QKV2 + 2 * (2 * i + 1 + k), par, U_QKV2 + i + k, a_hi, a_lo, between=channels2)
                    pe.wait_ge(silu2_done, c + 1)
                    pe.wait_ge(back2_evac0, c + 1)
                    pe.wait_ge(back2_evac1, c + 1)
                    to_tokens(s_act, TT).then_inc(qkv2_back, 1)
            chunk(Q_F + 2, 1, U_F, a_hi, a_lo)
            for par in range(2):
                chunk(Q_Z2 + 2 * par, par, U_Z2, a_hi, a_lo)
            pe.wait_ge(s_lo_ready, 1)
            narrow(bank[4], s_hi, s_lo, 4 * DNH).then_inc(sc_mm, 1)
            pe.wait_ge(g2_ready, 1)
            for t in range(TT):
                for d in range(2):
                    c = (2 * t + d) * DNH
                    T.matmul(bank[4][:, c:c + DNH], cum[:, d], g2[:, t, d], start=True, stop=True)
                    T.matmul(bank[4][:, 32 + c:32 + c + DNH], rest[:, d], g2[:, t, d], start=True, stop=True)
                for b in range(P // CHUNK):
                    c = 64 + (2 * t + b) * 2 * DNH
                    last = T.matmul(bank[4][:, c:c + 2 * DNH], chunk_ones[:, b], g2[:, t].rearrange("p d a -> p (d a)"),
                                    start=True, stop=True)
            last.then_inc(gc_mm, 1)
            pe.wait_ge(dn_qk_normed, TT)
            pe.wait_ge(dn_pre, 1)
            for n in range(8):
                if n >= 4:
                    pe.wait_ge((dn_qkT_evac0, dn_qkT_evac1)[n % 2], n // 2 - 1)
                for a in range(2):
                    for t in range(TT):
                        last = T.transpose(bank[4 + n % 4][:, a * SEQ + t * P:a * SEQ + (t + 1) * P],
                                           qkv2[:, t, (2 * n + a) * P:(2 * n + a + 1) * P], ident[:])
                last.then_inc(dn_qkT, 1)

            steps = SEQ // CHUNK
            unit = [(t, d) for t in range(TT) for d in range(2)]

            def at(b, n):
                return bank[b][:, n * P:(n + 1) * P]
            pe.wait_ge(dn_qkT_evac0, 4)
            pe.wait_ge(dn_qkT_evac1, 4)
            with pe.Fori(0, DNH) as i:
                pe.wait_ge(dn_rows, i + 1)
                T.matmul(bank[4][:], ones[:], d_gs[:].rearrange("p t d s -> p (t d s)"), start=True, stop=True).then_inc(dn_gcb, 1)
                pe.wait_ge(dn_qk, i + 1)
                for a in (1, 0):
                    for t in range(TT):
                        ts = slice(t * P, (t + 1) * P)
                        last = T.matmul(at(5, TT * (1 - a) + t), d_qk[:, 1, ts], d_qk[:, a, ts], start=True, stop=True)
                last.then_inc(dn_kk, 1)
                pe.wait_ge(dn_t, (LEVELS - 1) * i + 1)
                for n, (t, d) in enumerate(unit):
                    last = T.transpose(at(6, n), d_t[:, t, d], ident[:])
                last.then_inc(dn_rT, 1)
                for k in range(1, LEVELS):
                    pe.wait_ge(dn_mk, LEVELS * i + k + 1)
                    pe.wait_ge(dn_r, LEVELS * i + k)
                    for n, (t, d) in enumerate(unit):
                        last = T.matmul(at(7, n), d_mk[:, t, d], d_r[:, t, d], start=True, stop=True)
                    last.then_inc(dn_z, 1)
                    pe.wait_ge(dn_zz, (LEVELS - 1) * i + k)
                    pe.wait_ge(dn_t, (LEVELS - 1) * i + k)
                    for n, (t, d) in enumerate(unit):
                        last = T.matmul(at(6, n), d_t[:, t, d], d_zz[:, t, d], start=True, stop=True)
                    last.then_inc(dn_rz, 1)
                    if k == 1:
                        pe.wait_ge(dn_egb, i + 1)
                    if k < LEVELS - 1:
                        for n, (t, d) in enumerate(unit):
                            last = T.matmul(at(4, n), d_zz[:, t, d], d_t[:, t, d], start=True, stop=True)
                        last.then_inc(dn_tz, 1)
                pe.wait_ge(dn_in, i + 1)
                pe.wait_ge(dn_r, LEVELS * (i + 1))
                for n, (t, d) in enumerate(unit):
                    T.matmul(at(7, n), d_r[:, t, d], d_vb[:, t, d], start=True, stop=True)
                    last = T.matmul(at(6, n), d_kb[:, t, d], d_r[:, t, d], start=True, stop=True)
                last.then_inc(dn_uw, 1)
                pe.wait_ge(dn_u, i + 1)
                pe.wait_ge(dn_wT, i + 1)
                pe.wait_ge(dn_qkm, i + 1)
                pe.wait_ge(dn_qd, i + 1)
                for n in range(steps):
                    if n:
                        pe.wait_ge(dn_s, (steps - 1) * i + n)
                        for d in range(2):
                            c, t, r = rows_of(n, d)
                            last = T.matmul(bank[4][r, d * P:(d + 1) * P], d_wT[:, t, d, r], d_s[:, d], start=True, stop=True)
                        last.then_inc(dn_ws, 1)
                        pe.wait_ge(dn_vn, (steps - 1) * i + n)
                    for d in range(2):
                        c, t, r = rows_of(n, d)
                        v = d_vn[r, d] if n else d_u[r, t, d]
                        if n < steps - 1:
                            T.matmul(at(6 + d, 0), d_kd[r, t, d], v, start=True, stop=True)
                        o = bank[5][r, d * P:(d + 1) * P]
                        if n:
                            T.matmul(o, d_qd[:, t, d, r], d_s[:, d], start=True, stop=False)
                        last = T.matmul(o, d_eT[r, t, d, r], v, start=n == 0, stop=True)
                    last.then_inc(dn_so, 1)
            pe.wait_ge(y_ready, TT)
            for n in range(4):
                for a in range(2):
                    for t in range(TT):
                        last = T.transpose(bank[4 + n][:, a * SEQ + t * P:a * SEQ + (t + 1) * P],
                                           qkv2[:, t, (2 * n + a) * P:(2 * n + a + 1) * P], ident[:])
                last.then_inc(y_t, 1)

            pe.wait_ge(small4_loaded, 2 * 16)
            pe.wait_ge(fr_ready, 1)
            pe.wait_ge(y_lo_ready, 4)
            for g in range(DNH + 1):
                if g < DNH:
                    for c in range(2):
                        for t in range(TT):
                            last = T.matmul(bank[4 + g % 2][:, c * SEQ:(c + 1) * SEQ], fr[:, t, g * P:(g + 1) * P], dft_t[:, c, t],
                                            start=t == 0, stop=t == TT - 1)
                    last.then_inc(f_mm, 1)
                if g:
                    pe.wait_ge(f_half_ready, g)
                    if g >= 3:
                        pe.wait_ge(fr_lo_ready, g - 2)
                    for c in range(2):
                        last = T.matmul(bank[6 + (g - 1) % 2][:, 0:SEQ], dft_d[:, c], f_half[:, (g - 1) % 2, c], start=c == 0, stop=c == 1)
                    last.then_inc(f_out, 1)

            pe.wait_ge(fr_lo_ready, DNH)
            with pe.Fori(0, D // NC) as n:
                q = Q_MIX + 6 * n
                chunk(q, 0, U_MIX + n, a_hi, a_lo)
                chunk(q + 2, 1, U_MIX + n, a_hi, a_lo)
                chunk(q + 4, 2, V_MIX + n, fr_hi, fr_lo, DNH)
                chunk(q + 5, 3, V_MIX + n, y_hi, y_lo, DNH)
            pe.wait_ge(mix_ready, D // NC)
            transpose_operand(TR_WO2, mix)
            project(Q_WO2, U_WO2, D // NC)

            pe.wait_ge(normed, NORMED[G_MLP])
            transpose_operand(TR_MLP, xn_m)

            def mlp_down(q, use):
                for n in range(D // NC):
                    pe.wait_ge(pair_free[n % 2], 2 * (use + n // 2 + 1))
                    for s in range(2):
                        slab(q + n // 2, 2 * (n % 2) + s, [(m_hi[:, 2 * s + k], m_lo[:, 2 * s + k]) for k in range(SLAB_KT)],
                             pair[n % 2], s == 0, s == 1)

            def mlp_channels(use):
                pe.wait_ge(pair_free[2], 2 * (use + 1))
                to_channels(m_stage, 0, 6).then_inc(ff_t, 1)

            chunk(Q_MLP, 2, V_MLP, a_hi, a_lo)
            mlp_channels(V_MLP + 1)
            with pe.Fori(0, N_FF2 - 1) as j:
                q = Q_MLP + 2 + 4 * j
                chunk(q, 2, V_MLP + 1 + j, a_hi, a_lo)
                pe.wait_ge(ff_lo, N_FF + j + 1)
                mlp_down(q + 2, U_MLP + 2 * j)
                mlp_channels(V_MLP + 2 + j)
            pe.wait_ge(ff_lo, N_FF + N_FF2)
            mlp_down(N_QUADS - 2, U_MLP + 2 * (N_FF2 - 1))


def _slabs(w, k_major=False):
    k, n = w.shape
    s = w.reshape(k // (SLAB_KT * P), SLAB_KT, P, n // NC, NC).transpose(3, 0, 2, 1, 4)
    return s.reshape(-1, P, SLAB_KT * NC)


def _stream(a):
    w_in, w_out, w_up, w_down = a["w_in"][0], a["w_out"][0], a["w_up"][0], a["w_down"][0]
    w_in2, up2, down2 = a["w_in_2"][0], a["w_mlp_up_2"][0], a["w_mlp_down_2"][0]
    o_xbc, o_dt = D, D + XBC_W
    o_q = o_dt + HEADS
    parts = [_slabs(w_in[:, o_q:]), _slabs(w_in[:, o_xbc:o_dt]), _slabs(w_in[:, :D]),
             _slabs(w_out[D:]), _slabs(w_out[:D])]
    for j in range(N_FF + 1):
        if j < N_FF:
            parts += [_slabs(w_up[:, j * FFB:(j + 1) * FFB]), _slabs(w_up[:, D_FF + j * FFB:D_FF + (j + 1) * FFB])]
        if j:
            parts.append(_slabs(w_down[(j - 1) * FFB:j * FFB]))
    parts.append(_slabs(a["w_ple_gate"][0]))
    o_z, o_f = 3 * DNW, 4 * DNW
    o_sc = o_f + DNW
    o_ga = o_sc + 4 * DNH
    o_gf = o_ga + D
    parts += [_slabs(w_in2[:, :o_z]), _slabs(w_in2[:, o_f:o_sc]), _slabs(w_in2[:, o_z:o_f])]
    for n in range(D // NC):
        c = slice(n * NC, (n + 1) * NC)
        parts += [_slabs(w_in2[:, o_gf:][:, c]), _slabs(w_in2[:, o_ga:o_gf][:, c]),
                  _slabs(a["w_fourier_2"][0][:, c]), _slabs(a["w_dn_up_2"][0][:, c])]
    parts.append(_slabs(a["w_o_2"][0]))
    for j in range(N_FF2 + 1):
        if j < N_FF2:
            parts.append(_slabs(up2[:, j * NC:(j + 1) * NC]))
        if j:
            parts.append(_slabs(down2[(j - 1) * NC:j * NC]))
    return np.concatenate(parts).reshape(N_QUADS, QUAD, P, SLAB_KT * NC)


def _small(a):
    def tiles(x):
        return np.ascontiguousarray(x.reshape(-1, P, x.shape[-1]).transpose(1, 0, 2))

    def columns(*rows):
        return tiles(np.concatenate(rows, 0).T)
    o_dt = D + XBC_W
    o_sc = 5 * DNW
    ff = columns(a["ffn_conv_w"][0], a["ffn_conv_b"])
    ff = ff.reshape(P, 2, N_FF, FFB // P, CONV_FF + 1).transpose(0, 2, 1, 3, 4).reshape(P, N_FF, -1, CONV_FF + 1)
    out = {
        "x_tok": tiles(a["x"][0]), "positions_tok": a["positions"].reshape(TT, P).T,
        "p_T": tiles(a["p"][0, 0].T), "w_dt": tiles(a["w_in"][0][:, o_dt:o_dt + HEADS]),
        "w_scal": tiles(a["w_in_2"][0][:, o_sc:o_sc + 4 * DNH]), "w_proj": tiles(a["w_ple_proj"][0]),
        "conv_col": columns(a["conv_w"][0], a["conv_b"]), "ff_col": ff, "conv2_col": columns(a["conv_w_2"][0]),
        "gains": np.stack([np.asarray(a[g]).reshape(D) for g in GAINS]),
        "row": np.concatenate([a[n].reshape(1, -1) for n in ROW], 1),
    }
    return {k: np.ascontiguousarray(v) for k, v in out.items()}


def build(nc):
    def dram(name, shape, dt=F32, kind="ExternalInput"):
        return nc.dram_tensor(name, tuple(shape), dt, kind=kind).ap()
    wstream = dram("weights", (N_QUADS, QUAD, P, SLAB_KT * NC))
    small = {n: dram(n, s, I32 if n == "positions_tok" else F32) for n, s in SMALL.items()}
    const = {n: dram("c_" + n, v.shape) for n, v in CONSTS.items()}
    out = dram("out", (TT, P, D), kind="ExternalOutput")
    program(nc, wstream, small, const, out)


def kernel(**inputs):
    import concourse.bacc as bacc
    from concourse.bass_utils import run_bass_kernel_spmd

    a = {k: np.asarray(v) for k, v in inputs.items()}
    nc = bacc.Bacc("TRN2", target_bir_lowering=False, num_devices=1)
    build(nc)
    arrays = {"weights": _stream(a), **_small(a), **{"c_" + n: v for n, v in CONSTS.items()}}
    r = run_bass_kernel_spmd(nc, [arrays], core_ids=[0])
    return r.results[0]["out"].reshape(1, SEQ, D)
```

```python
from contextlib import ExitStack

import numpy as np
import concourse.bass as bass
import concourse.mybir as mybir

F32 = mybir.dt.float32
F32R = mybir.dt.float32r
I32 = mybir.dt.int32
ACT = mybir.ActivationFunctionType
ALU = mybir.AluOpType
AX = mybir.AxisListType

P = 128
SEQ, D = 256, 2048
TT = SEQ // P
KT = D // P
NC = 512
DC = D // NC
EPS = 1e-6
SLAB_KT, QUAD = 2, 4

HEADS, HD = 32, 64
GROUPS, HPG = 4, 8
KVH, REP = 8, 4
QKV_W = (HEADS + 2 * KVH) * HD
CONV1, XBC_W = 4, 3072
ROPE = 16
PLE = 256
D_FF = 5632
FFB = NC
N_FF = D_FF // FFB
CONV_FF = 3
DNH, DND = 8, 128
DNW = DNH * DND
CHUNK = 64
CONV2 = 5
D_FF2 = 4 * D
N_FF2 = D_FF2 // NC

Q_XBC = 0
Q_Z = Q_XBC + 2 * (XBC_W // NC)
Q_QKV = Q_Z + 2 * (D // NC)
Q_WOS = Q_QKV + 2 * (QKV_W // NC)
Q_WOA = Q_WOS + 2 * (D // NC)
Q_FF = Q_WOA + 2 * (D // NC)
Q_GATE = Q_FF + 6 * N_FF
Q_QKV2 = Q_GATE + 2 * (D // NC)
Q_F = Q_QKV2 + 2 * (3 * DNW // NC)
Q_Z2 = Q_F + 2 * (DNW // NC)
Q_MIX = Q_Z2 + 2 * (DNW // NC)
Q_WO2 = Q_MIX + 6 * (D // NC)
Q_MLP = Q_WO2 + 2 * (D // NC)
N_QUADS = Q_MLP + 4 * N_FF2

ROW = {}
_at = 0
for _name, _n in (("q_norm_g", HD), ("k_norm_g", HD), ("sinks", HEADS), ("dt_bias", HEADS),
                  ("a_log", HEADS), ("d_skip", HEADS), ("g_dn_head_2", DND),
                  ("a_log_fwd_2", DNH), ("a_log_bwd_2", DNH),
                  ("dt_bias_fwd_2", DNH), ("dt_bias_bwd_2", DNH)):
    ROW[_name] = (_at, _at + _n)
    _at += _n
N_ROW = _at
GAINS = ("attn_norm_g", "ssm_norm_g", "ffn_norm_g", "ple_post_g", "ple_norm_g",
         "g_mix_2", "g_mlp_2", "g_final_2")
NEG = -1e30

def _constants():
    i, j = np.arange(P)[:, None], np.arange(P)[None, :]
    same = (i // CHUNK) == (j // CHUNK)
    out = {"ident": i == j, "ones": np.ones((P, P)), "before": i <= j}
    mask = np.zeros((P, 3, P))
    mask[:, 0] = np.where(j <= i, 0.0, NEG)
    mask[:, 1] = np.where(j > i, 0.0, NEG)
    mask[:, 2] = mask[:, 0]
    out["att_mask"] = mask
    out["cum"] = np.stack([same & (i <= j), same & (i >= j)], 1)
    out["rest"] = np.stack([same & (i > j), same & (i < j)], 1)
    out["chunk_ones"] = np.stack([(i // CHUNK == c) & (j >= 0) for c in range(P // CHUNK)], 1)
    level = []
    for k in range(LEVELS):
        block = (i >> (k + 1)) == (j >> (k + 1))
        later, earlier = (i >> k) & 1, (j >> k) & 1
        fwd = block & (later == 1) & (earlier == 0)
        level.append(np.stack([fwd, fwd.T], 1))
    out["level"] = np.stack(level, 1)
    t, c = np.arange(SEQ), np.arange(DND)
    norm = 1.0 / np.sqrt(SEQ * DND)
    at = 2 * np.pi * np.outer(t, t) / SEQ
    ad = 2 * np.pi * np.outer(c, c) / DND
    dft_t = np.stack([np.cos(at), np.sin(at)], 0) * norm
    out["dft_t"] = dft_t.reshape(2, TT, P, SEQ).transpose(2, 0, 1, 3)
    out["dft_d"] = np.stack([np.cos(ad), -np.sin(ad)], 1)
    freq = ROPE_THETA ** (-np.arange(0, ROPE, 2, dtype=np.float32) / np.float32(ROPE))
    out["inv_freq"] = np.broadcast_to(freq, (P, ROPE // 2))
    return {k: np.ascontiguousarray(v, dtype=np.float32) for k, v in out.items()}


LEVELS = CHUNK.bit_length() - 1
ROPE_THETA = np.float32(500000.0)
TWO_PI = (6.28125, 0.0019350051879882812, float(2 * np.pi - 6.28125 - 0.0019350051879882812))
PI_BELOW = 3.1415925
ROUND = 1.5 * 2.0 ** 23
CONSTS = _constants()

SMALL = {
    "x_tok": (P, TT, D), "positions_tok": (P, TT), "p_T": (P, PLE // P, SEQ),
    "w_dt": (P, KT, HEADS), "w_scal": (P, KT, 4 * DNH), "w_proj": (P, PLE // P, D),
    "conv_col": (P, XBC_W // P, CONV1 + 1), "ff_col": (P, N_FF, 2 * FFB // P, CONV_FF + 1),
    "conv2_col": (P, 3 * DNW // P, CONV2), "gains": (len(GAINS), D), "row": (1, N_ROW),
}

U_XBC = 0
U_Z = U_XBC + XBC_W // NC // 2
U_QKV = U_Z + D // NC // 2
U_WOS = U_QKV + QKV_W // NC // 2
U_WOA = U_WOS + D // NC // 2
U_FF = U_WOA + D // NC // 2
U_PLE = U_FF + 3 * N_FF - 2
U_GATE = U_PLE + DC // 2 + 2
U_QKV2 = U_GATE
U_F = U_QKV2 + 3 * DNW // NC // 2
U_Z2 = U_F + DNW // NC // 2
U_MIX = U_Z2 + DNW // NC // 2
U_WO2 = U_MIX + D // NC
U_MLP = U_WO2 + D // NC // 2
V_MIX = 0
V_MLP = V_MIX + D // NC
TR_ATTN, TR_YSSM, TR_YATT, TR_FFN, TR_PLE, TR_MIX2, TR_WO2, TR_MLP = range(8)
NORM_ATTN, NORM_FFN, NORM_PLE, NORM_MIX2, NORM_MLP, NORM_OUT = range(6)
(G_ATTN, G_SSM, G_FFN, G_POST, G_PLE, G_MIX2, G_MLP, G_OUT) = range(8)


class Chain:

    def __init__(self, eng, sem):
        self.eng, self.sem, self.base, self.n = eng, sem, 0, 0

    def __call__(self, instruction):
        instruction.then_inc(self.sem, 1)
        self.n += 1
        self.eng.wait_ge(self.sem, self.base + self.n)

    def enter(self, turn, steps):
        self.before, self.steps = self.base + self.n, steps
        self.base, self.n = self.before + turn * steps, 0

    def leave(self, turns):
        assert self.n == self.steps, (self.n, self.steps)
        self.base, self.n = self.before + turns * self.steps, 0


NORMED = [TT * DC * (k + 1) for k in range(len(GAINS))]


def program(nc, wstream, small, const, out):
    ctx = ExitStack()
    with ctx:
        def sb(name, shape, dt=F32, scope=ctx):
            return scope.enter_context(nc.sbuf_tensor(name, list(shape), dt))

        sems = {}

        def sem(name):
            sems[name] = ctx.enter_context(nc.semaphore(name))
            return sems[name]

        with ExitStack() as rings:
            w_hi = sb("w_hi", [P, QUAD, SLAB_KT * NC], F32R, rings)
            w_lo = sb("w_lo", [P, QUAD, SLAB_KT * NC], F32R, rings)
        delta_b = sb("delta_b", [P, 4 * QUAD, TT * 2 * P])
        w_raw = sb("w_raw", [P, QUAD, SLAB_KT * NC])
        a_hi = sb("a_hi", [P, KT, SEQ], F32R)
        a_lo = sb("a_lo", [P, KT, SEQ], F32R)
        h = sb("h", [P, TT, D])
        gain = sb("gain", [P, D])
        ident = sb("ident_sb", [P, P])
        ones = sb("ones_sb", [P, P])
        row = sb("row_sb", [P, N_ROW])
        neg_half = sb("neg_half", [P, 88])
        stat = sb("stat", [P, TT, DC])
        rstd = sb("rstd", [P, 4])

        with ExitStack() as part:
            def at1(name, shape, dt=F32):
                return sb(name, shape, dt, part)
            qkv = at1("qkv", [P, TT, QKV_W])
            xs = at1("xs", [P, TT, D])
            with ExitStack() as first:
                def at1f(name, shape, dt=F32):
                    return sb(name, shape, dt, first)
                w32_raw = at1f("w32_raw", [P, KT, HEADS])
                w32_hi = at1f("w32_hi", [P, KT, HEADS], F32R)
                w32_lo = at1f("w32_lo", [P, KT, HEADS], F32R)
            z = at1("z", [P, TT, D])
            bcT = at1("bcT", [P, 2, GROUPS, SEQ])
            b_tok = at1("b_tok", [P, GROUPS, P])
            stage = at1("stage", [P, 2, TT, NC])
            cv = at1("cv", [P, 4, SEQ])
            cv_act = at1("cv_act", [P, 4, SEQ])
            work = at1("work", [P, 2 * 1536])
            before = at1("before_sb", [P, P])
            att_mask = at1("att_mask_sb", [P, 3, P])
            inv_freq = at1("inv_freq_sb", [P, ROPE // 2])
            conv_col = at1("conv_col_sb", [P, XBC_W // P, CONV1 + 1])
            pos_i = at1("pos_i", [P, TT], I32)
            pos_f = at1("pos_f", [P, TT])
            ang = at1("ang", [P, 6, TT, ROPE // 2])
            sin = at1("sin", [P, TT, ROPE // 2])
            cos = at1("cos", [P, TT, ROPE // 2])
            qk_ss = at1("qk_ss", [P, TT, 40])
            qk_rs = at1("qk_rs", [P, TT, 40])
            sp = at1("sp", [P, 6, TT * HEADS])
            dt = at1("dt", [P, TT, HEADS])
            adt = at1("adt", [P, TT, HEADS])
            acs = at1("acs", [P, TT, HEADS])
            aneg = at1("aneg", [P, HEADS])
            ds = at1("ds", [P, HEADS])
            ea = at1("ea", [P, HEADS])
            ssm_ss = at1("ssm_ss", [P, TT, GROUPS])
            ssm_rs = at1("ssm_rs", [P, TT, GROUPS])
        with ExitStack() as part:
            def at2(name, shape, dt=F32):
                return sb(name, shape, dt, part)
            xn_f = at2("xn_f", [P, TT, D])
            f_hi = at2("f_hi", [P, FFB // P, SEQ], F32R)
            f_lo = at2("f_lo", [P, FFB // P, SEQ], F32R)
            f_stage = at2("f_stage", [P, TT, 2 * FFB])
            f_cv = at2("f_cv", [P, 2 * FFB // P, SEQ])
            f_silu = at2("f_silu", [P, FFB // P, SEQ])
            f_act = at2("f_act", [P, FFB // P, SEQ])
            ff_col = at2("ff_col_sb", [P, N_FF, 2 * FFB // P, CONV_FF + 1])
            pe_tok = at2("pe_tok", [P, TT, D])
            w_proj = at2("w_proj_sb", [P, PLE // P, D])
            p_T = at2("p_T_sb", [P, PLE // P, SEQ])
            sig = at2("sig", [P, TT, NC])
        with ExitStack() as part:
            def at3(name, shape, dt=F32):
                return sb(name, shape, dt, part)
            qkv2 = at3("qkv2", [P, TT, 3 * DNW])
            qk_T = at3("qk_T", [P, 2, DNH, SEQ])
            z2 = at3("z2", [P, TT, DNW])
            fr = at3("fr", [P, TT, DNW])
            conv2_col = at3("conv2_col_sb", [P, 3 * DNW // P, CONV2])
            sc = at3("sc", [P, TT, 4 * DNH])
            sp2 = at3("sp2", [P, 6, TT * 2 * DNH])
            g2 = at3("g2", [P, TT, 2, DNH])
            aneg2 = at3("aneg2", [P, 2 * DNH])
            beta = at3("beta", [P, TT, 2, DNH])
            gc = at3("gc", [P, TT, 2, DNH])
            be = at3("be", [P, TT, 2, DNH])
            kd = at3("kd", [P, TT, 2, DNH])
            gl = at3("gl", [P, SEQ // CHUNK, 2, DNH])
            dn_ss = at3("dn_ss", [P, TT, 2 * DNH])
            dn_rs = at3("dn_rs", [P, TT, 2 * DNH])
            dft_d = at3("dft_d_sb", [P, 2, DND])
            with ExitStack() as inner:
                def at3a(name, shape, dt_=F32):
                    return sb(name, shape, dt_, inner)
                cum = at3a("cum_sb", [P, 2, P])
                rest = at3a("rest_sb", [P, 2, P])
                chunk_ones = at3a("chunk_ones_sb", [P, P // CHUNK, P])
                level = at3a("level_sb", [P, LEVELS, 2, P])
                with ExitStack() as first:
                    def at3p(name, shape, dt_=F32):
                        return sb(name, shape, dt_, first)
                    s_stage = at3p("s_stage", [P, 2, TT, NC])
                    s_cv = at3p("s_cv", [P, 4, SEQ])
                    s_act = at3p("s_act", [P, 4, SEQ])
                    s_raw = at3p("s_raw", [P, KT, 4 * DNH])
                    s_hi = at3p("s_hi", [P, KT, 4 * DNH], F32R)
                    s_lo = at3p("s_lo", [P, KT, 4 * DNH], F32R)
                delta_a = at3a("delta_a", [P, 4 * QUAD, TT * 2 * P])
            with ExitStack() as inner:
                def at3b(name, shape, dt_=F32):
                    return sb(name, shape, dt_, inner)
                dft_t = at3b("dft_t_sb", [P, 2, TT, SEQ])
                f_half = at3b("f_half", [P, 2, 2, SEQ])
                fr_hi = at3b("fr_hi", [P, DNH, SEQ], F32R)
                fr_lo = at3b("fr_lo", [P, DNH, SEQ], F32R)
                y_hi = at3b("y_hi", [P, DNH, SEQ], F32R)
                y_lo = at3b("y_lo", [P, DNH, SEQ], F32R)
        with ExitStack() as part:
            def at4(name, shape, dt_=F32):
                return sb(name, shape, dt_, part)
            xn_m = at4("xn_m", [P, TT, D])
            m_hi = at4("m_hi", [P, FFB // P, SEQ], F32R)
            m_lo = at4("m_lo", [P, FFB // P, SEQ], F32R)
            m_stage = at4("m_stage", [P, TT, NC])
            m_relu = at4("m_relu", [P, FFB // P, SEQ])
            m_act = at4("m_act", [P, FFB // P, SEQ])
        bank = [ctx.enter_context(nc.psum_tensor(f"bank{i}", [P, NC], F32)) for i in range(8)]
        pair = [bank[2 * i:2 * i + 2] for i in range(4)]

        narrow_T = sp[0:HEADS, 1:5].rearrange("p m n -> p (m n)")
        narrow2_T = s_cv[0:4 * DNH, 0]

        att_q = stage[:, 0].rearrange("p t (a b d) -> p t a b d", a=REP, b=2)
        att_k = stage[:, 1, 0, 0:SEQ].rearrange("p (t d) -> p t d", t=TT)
        att_qT = cv[:].rearrange("p a s -> p (a s)").rearrange("p (t a s) -> p t a s", t=TT, a=REP)
        att_kT = cv_act[:, 0]
        bT, cT, bc_flat = bcT[:, 0], bcT[:, 1], bcT[:].rearrange("p b g s -> p (b g s)")
        att_p = (work[:, 0:1536], bc_flat[:, 0:1536])
        att_pTs = work[:, 1536:3072]
        att_s = sp[:, 1:3].rearrange("p b (m n) -> p b m n", n=TT * REP)

        def qk_square(c):
            return xs[:, :, 0:NC] if c else stage[:, 1]
        ssm_cb = cv_act[:].rearrange("p g (t s) -> p g t s", t=TT)
        ssm_rows = cv[:].rearrange("p a s -> p (a s)").rearrange("p (a s) -> p a s", a=HPG)
        ssm_w = work[:, 0:HPG * P].rearrange("p (a s) -> p a s", a=HPG)
        ssm_xd = work[:, 1024:2048].rearrange("p (t n) -> p t n", t=TT)
        ssm_xds, ssm_state = work[:, 2048:2560], work[:, 2560:3072]
        ssm_dx = stage[:, 0]
        ssm_y, ssm_off = stage[:, 1, 0], stage[:, 1, 1]

        def att_cols(n):
            s0 = n * P if n < REP else REP * P + (n - REP) * 2 * P
            return s0, s0 + (P if n < REP else 2 * P)

        qk_flat = qk_T[:].rearrange("p a h s -> p (a h s)")
        mix = qk_flat.rearrange("p (t n) -> p t n", t=TT)
        qkh = qk_T[:].rearrange("p a h s -> p (a h) s")

        class Head:
            def __init__(self, x):
                self.x, self.bank = x, (bank[4:8], bank[0:4])[x]
                place = [(delta_a, delta_b)[x][:, k] for k in range(4 * QUAD)]
                (self.gs, self.eT, self.eN, self.m, self.mk, self.t, self.r, self.zz, self.vb, self.kb, self.kd, self.u,
                 self.wT, self.qd) = (p.rearrange("p (t d s) -> p t d s", t=TT, d=2) for p in place[:14])
                self.qk = place[14].rearrange("p (a s) -> p a s", a=2)
                self.vn = place[15][:, 0:2 * P].rearrange("p (d s) -> p d s", d=2)
                self.s = place[15][:, 2 * P:].rearrange("p (d s) -> p d s", d=2)

            def at(self, b, n):
                return self.bank[b][:, n * P:(n + 1) * P]

            def units(self, b):
                return self.bank[b][:].rearrange("p (t d s) -> p t d s", t=TT, d=2)

            def of(self, turn, each=1, step=0):
                return 2 * each * turn + 2 * step + self.x + 1
        heads = [Head(0), Head(1)]

        def flat(x):
            return x.rearrange("p t d s -> p (t d s)")

        def rows_of(n, d):
            c = n if d == 0 else SEQ // CHUNK - 1 - n
            r = c % (P // CHUNK) * CHUNK
            return c, c // (P // CHUNK), slice(r, r + CHUNK)

        raw_loaded = [sem(f"raw_loaded{s}") for s in range(QUAD)]
        hi_ready, lo_ready = sem("hi_ready"), sem("lo_ready")
        slab_done = sem("slab_done")
        pair_free = [sem(f"pair_free{p}") for p in range(4)]
        x_loaded = [sem(f"x_loaded{half}") for half in range(2)]
        small1_loaded = sem("small1_loaded")
        w32_hi_ready, w32_lo_ready = sem("w32_hi_ready"), sem("w32_lo_ready")
        gain_loaded = sem("gain_loaded")
        stat_ready, rstd_ready = sem("stat_ready"), sem("rstd_ready")
        normed = sem("normed")
        tr_ready, a_hi_ready, a_lo_ready = sem("tr_ready"), sem("a_hi_ready"), sem("a_lo_ready")
        dve_step, pool_step = sem("dve_step"), sem("pool_step")
        dt_mm, dt_t, narrow_copied = sem("dt_mm"), sem("dt_t"), sem("narrow_copied")
        sp_abs, sp_exp, sp_sum, sp_ln = sem("sp_abs"), sem("sp_exp"), sem("sp_sum"), sem("sp_ln")
        rope_arg, rope_ready = sem("rope_arg"), sem("rope_ready")
        qk_sq, qk_summed, qk_rstd, qk_ready = sem("qk_sq"), sem("qk_summed"), sem("qk_rstd"), sem("qk_ready")
        xbc_t, conv_done, silu_done, xbc_back = sem("xbc_t"), sem("conv_done"), sem("silu_done"), sem("xbc_back")
        back0_evac, back1_evac = sem("back0_evac"), sem("back1_evac")
        att_staged, att_qkT, att_qkT_evac = sem("att_staged"), sem("att_qkT"), sem("att_qkT_evac")
        att_scored, att_masked, att_max, att_exp = (sem(n) for n in ("att_scored", "att_masked", "att_max", "att_exp"))
        att_pT, att_pT_evac, att_pv, att_done = sem("att_pT"), sem("att_pT_evac"), sem("att_pv"), sem("att_done")
        adt_ready, acs_mm, acs_ready, sdecay = sem("adt_ready"), sem("acs_mm"), sem("acs_ready"), sem("sdecay")
        aneg_ready = sem("aneg_ready")
        cb_mm, cb_ready = sem("cb_mm"), sem("cb_ready")
        row_scaled, row_mm, seg_ready, seg_exp, seg_w = (sem(n) for n in (
            "row_scaled", "row_mm", "seg_ready", "seg_exp", "seg_w"))
        xd_ready, xds_ready, state_mm, state_evac = sem("xd_ready"), sem("xds_ready"), sem("state_mm"), sem("state_evac")
        ydiag_mm, yoff_mm, dskip_ready, y_gated, y_squared, ssm_rstd = (sem(n) for n in (
            "ydiag_mm", "yoff_mm", "dskip_ready", "y_gated", "y_squared", "ssm_rstd"))
        small2_loaded, ple_mm = sem("small2_loaded"), sem("ple_mm")
        ff_t, ff_conv, ff_silu, ff_mul, ff_hi, ff_lo = (sem(n) for n in (
            "ff_t", "ff_conv", "ff_silu", "ff_mul", "ff_hi", "ff_lo"))
        sig_ready, gated = sem("sig_ready"), sem("gated")
        small3_loaded, small4_loaded = sem("small3_loaded"), sem("small4_loaded")
        s_hi_ready, s_lo_ready, sc_mm, sc_t = (sem(n) for n in ("s_hi_ready", "s_lo_ready", "sc_mm", "sc_t"))
        qkv2_t, conv2_done, silu2_done, qkv2_back = sem("qkv2_t"), sem("conv2_done"), sem("silu2_done"), sem("qkv2_back")
        back2_evac0, back2_evac1 = sem("back2_evac0"), sem("back2_evac1")
        beta_ready, g2_ready, gc_mm, gc_exp, dn_pre = (sem(n) for n in (
            "beta_ready", "g2_ready", "gc_mm", "gc_exp", "dn_pre"))
        dn_sq, dn_summed, dn_qk_normed, dn_qkT, dn_qkT_evac0, dn_qkT_evac1 = (sem(n) for n in (
            "dn_sq", "dn_summed", "dn_qk_normed", "dn_qkT", "dn_qkT_evac0", "dn_qkT_evac1"))
        z2_scaled, fr_ready = sem("z2_scaled"), sem("fr_ready")
        (dn_free, dn_qk, dn_rows, dn_in, dn_gcb, dn_kk, dn_diff, dn_eT, dn_eN, dn_egb, dn_eTm, dn_qd, dn_m, dn_mk,
         dn_t, dn_rT, dn_r0, dn_r, dn_z, dn_zz, dn_rz, dn_tz, dn_uw, dn_u, dn_wT, dn_qkm, dn_ws, dn_vn, dn_so, dn_s) = (
            sem("dn_" + n) for n in (
                "free", "qk", "rows", "in", "gcb", "kk", "diff", "eT", "eN", "egb", "eTm", "qd", "m", "mk", "t", "rT",
                "r0", "r", "z", "zz", "rz", "tz", "uw", "u", "wT", "qkm", "ws", "vn", "so", "s"))
        o_sq, o_summed, o_rstd, y_ready, y_t, y_hi_ready, y_lo_ready = (sem(n) for n in (
            "o_sq", "o_summed", "o_rstd", "y_ready", "y_t", "y_hi_ready", "y_lo_ready"))
        f_mm, f_half_ready, f_out, fr_hi_ready, fr_lo_ready = (sem(n) for n in (
            "f_mm", "f_half_ready", "f_out", "fr_hi_ready", "fr_lo_ready"))
        mix_ready = sem("mix_ready")
        out_scaled, stored = sem("out_scaled"), sem("stored")

        block = ctx.enter_context(nc.Block())

        @block.sync
        def _(sp_):
            for half in range(2):
                cols = slice(half * D // 2, (half + 1) * D // 2)
                sp_.dma_start(h[:, :, cols], small["x_tok"][:, :, cols]).then_inc(x_loaded[half], 16)
            sp_.dma_start(ident[:], const["ident"]).then_inc(x_loaded[1], 16)
            for s in range(QUAD):
                sp_.dma_start(w_raw[:, s, :], wstream[0, s]).then_inc(raw_loaded[s], 16)
            for dst, src in ((w32_raw, small["w_dt"]), (ones, const["ones"]), (row, small["row"].to_broadcast([P, N_ROW])),
                             (before, const["before"]), (att_mask, const["att_mask"]),
                             (inv_freq, const["inv_freq"]), (conv_col, small["conv_col"]),
                             (pos_i, small["positions_tok"])):
                sp_.dma_start(dst[:], src).then_inc(small1_loaded, 16)
            with sp_.Fori(1, N_QUADS) as q:
                for s in range(QUAD):
                    sp_.wait_ge(lo_ready, QUAD * (q - 1) + s + 1)
                    sp_.dma_start(w_raw[:, s, :], wstream[q, s]).then_inc(raw_loaded[s], 16)

            for c, (done, count) in enumerate(((out_scaled, 1), (out_scaled, 2), (normed, NORMED[G_MLP] + DC), (normed, NORMED[G_MLP] + DC + 1))):
                cols = slice(c * NC, (c + 1) * NC)
                sp_.wait_ge(done, count)
                sp_.dma_start(out[:, :, cols].rearrange("t p n -> p t n"), xn_m[:, :, cols]).then_inc(stored, 16)
            sp_.wait_ge(stored, DC * 16)

        @block.gpsimd
        def _(pool):
            step = Chain(pool, pool_step)

            def load_gain(n):
                if n:
                    pool.wait_ge(normed, NORMED[n - 1])
                pool.dma_start(gain[:], small["gains"][n:n + 1, :].to_broadcast([P, D])).then_inc(gain_loaded, 16)

            def inverse_root(dst, src, width, scale, eps, done):
                step(nc.gpsimd.tensor_scalar(dst, src, scale, eps, ALU.mult, ALU.add))
                nc.gpsimd.tensor_tensor(dst, dst, neg_half[:, 0:width], ALU.pow).then_inc(done, 1)

            def norm_root(n):
                pool.wait_ge(rstd_ready, 2 * n + 1)
                nc.gpsimd.tensor_tensor(rstd[:, 0:TT], rstd[:, 0:TT], neg_half[:, 0:TT], ALU.pow).then_inc(rstd_ready, 1)

            load_gain(G_ATTN)
            for p in range(4):
                nc.gpsimd.memset(neg_half[:, 20 * p:20 * p + 20], -0.5).then_inc(pair_free[p], 2)
            nc.gpsimd.memset(neg_half[:, 80:81], -0.5).then_inc(att_qkT_evac, 3)
            nc.gpsimd.memset(neg_half[:, 81:82], -0.5).then_inc(back0_evac, 1)
            nc.gpsimd.memset(neg_half[:, 82:83], -0.5).then_inc(back1_evac, 1)
            for k, (s, n) in enumerate(((back2_evac0, 1), (back2_evac1, 1), (dn_free, 2))):
                nc.gpsimd.memset(neg_half[:, 83 + k:84 + k], -0.5).then_inc(s, n)
            for s, n in [(pair_free[p], 2) for p in range(4)] + [(att_qkT_evac, 3), (back0_evac, 1), (back1_evac, 1),
                                                                 (back2_evac0, 1), (back2_evac1, 1), (dn_free, 2)]:
                pool.wait_ge(s, n)
            norm_root(0)
            load_gain(G_SSM)

            pool.wait_ge(sdecay, 1)
            pool.wait_ge(small1_loaded, 8 * 16)
            pool.wait_ge(rope_ready, 1)

            def qk_norm(c, t):
                n = TT * c + t
                a0, heads8 = c * NC // HD, NC // HD
                pool.wait_ge(qk_summed, n + 1)
                rs = qk_rs[:, t, a0:a0 + heads8]
                inverse_root(rs, qk_ss[:, t, a0:a0 + heads8], heads8, 1.0 / HD, EPS, qk_rstd)
                pool.wait_ge(qk_rstd, n + 1)
                qk = qkv[:, t, c * NC:(c + 1) * NC].rearrange("p (a d) -> p a d", d=HD)
                step(nc.gpsimd.tensor_tensor(qk, qk, rs.unsqueeze(2).to_broadcast([P, heads8, HD]), ALU.mult))
                r0, r1 = ROW["q_norm_g" if a0 < HEADS else "k_norm_g"]
                step(nc.gpsimd.tensor_tensor(qk, qk, row[:, r0:r1].unsqueeze(1).to_broadcast([P, heads8, HD]), ALU.mult))
                half = ROPE // 2
                t1, t2 = qk[:, :, 0:half], qk[:, :, half:ROPE]
                c8 = cos[:, t, :].unsqueeze(1).to_broadcast([P, heads8, half])
                s8 = sin[:, t, :].unsqueeze(1).to_broadcast([P, heads8, half])
                products = qk_square(c)[:, t, 0:4 * heads8 * half].rearrange("p (m a d) -> p m a d", m=4, d=half)
                for m, (x, y) in enumerate(((t1, c8), (t2, s8), (t2, c8), (t1, s8))):
                    last = nc.gpsimd.tensor_tensor(products[:, m], x, y, ALU.mult)
                step(last)
                nc.gpsimd.tensor_tensor(t1, products[:, 0], products[:, 1], ALU.subtract)
                nc.gpsimd.tensor_tensor(t2, products[:, 2], products[:, 3], ALU.add).then_inc(qk_ready, 1)

            def decay_rows(n):
                if n:
                    pool.wait_ge(row_mm, n)
                w = adt[:, n % TT, n // TT * HPG:(n // TT + 1) * HPG].unsqueeze(2).to_broadcast([P, HPG, P])
                nc.gpsimd.tensor_tensor(ssm_rows, before[:].unsqueeze(1).to_broadcast([P, HPG, P]), w,
                                        ALU.mult).then_inc(row_scaled, 1)
            decay_rows(0)
            for g in range(GROUPS):
                cols = slice(g * NC, (g + 1) * NC)
                hs = slice(g * HPG, (g + 1) * HPG)

                def by_head(x, hd=HD):
                    return x.rearrange("p (a d) -> p a d", d=hd)

                if g:
                    pool.wait_ge(ydiag_mm, TT * g)
                for t in range(TT):
                    w = dt[:, t, hs].unsqueeze(2).to_broadcast([P, HPG, HD])
                    last = nc.gpsimd.tensor_tensor(by_head(ssm_xd[:, t]), by_head(xs[:, t, cols]), w, ALU.mult)
                last.then_inc(xd_ready, 1)
                pool.wait_ge(xd_ready, g + 1)
                w = ds[:, hs].unsqueeze(2).to_broadcast([P, HPG, HD])
                nc.gpsimd.tensor_tensor(by_head(ssm_xds), by_head(ssm_xd[:, 0]), w, ALU.mult).then_inc(xds_ready, 1)
                if g:
                    pool.wait_ge(y_squared, TT * g)
                for t in range(TT):
                    w = row[:, ROW["d_skip"][0] + g * HPG:ROW["d_skip"][0] + (g + 1) * HPG]
                    last = nc.gpsimd.tensor_tensor(by_head(ssm_dx[:, t]), by_head(xs[:, t, cols]),
                                                   w.unsqueeze(2).to_broadcast([P, HPG, HD]), ALU.mult)
                last.then_inc(dskip_ready, 1)
                decay_rows(TT * g + 1)
                for t in range(TT):
                    pool.wait_ge(seg_exp, TT * g + t + 1)
                    cb = ssm_cb[:, g, t, :].unsqueeze(1).to_broadcast([P, HPG, P])
                    nc.gpsimd.tensor_tensor(ssm_w, ssm_w, cb, ALU.mult).then_inc(seg_w, 1)
                    if t and g < GROUPS - 1:
                        decay_rows(TT * (g + 1))
                    qk_norm(g, t)
            pool.wait_ge(y_squared, TT * GROUPS)
            inverse_root(ssm_rs[:].rearrange("p t g -> p (t g)"), ssm_ss[:].rearrange("p t g -> p (t g)"),
                         TT * GROUPS, 1.0 / NC, EPS, ssm_rstd)
            for t in range(TT):
                qk_norm(GROUPS, t)
            pool.wait_ge(qk_ready, TT * (HEADS + KVH) * HD // NC)

            with pool.Fori(0, KVH // 2) as i:
                pool.wait_ge(att_qkT_evac, 3 * i + 3)
                for t in range(TT):
                    for par in range(2):
                        src = qkv[:, t, bass.ds(i * (2 * REP * HD) + par * REP * HD, REP * HD)]
                        nc.gpsimd.tensor_copy(att_q[:, t, :, par, :], src.rearrange("p (a d) -> p a d", d=HD))
                nc.gpsimd.tensor_copy(att_k, qkv[:, :, bass.ds(i * (2 * HD) + HEADS * HD, 2 * HD)]).then_inc(att_staged, 1)

            load_gain(G_FFN)

            norm_root(1)
            pool.wait_ge(pair_free[0], 2 * (U_FF + 1))
            pool.wait_ge(pair_free[1], 2 * (U_FF + 1))
            for dst, src in ((ff_col, "ff_col"), (w_proj, "w_proj"), (p_T, "p_T")):
                pool.dma_start(dst[:], small[src]).then_inc(small2_loaded, 16)
            load_gain(G_POST)
            norm_root(2)
            load_gain(G_PLE)
            norm_root(3)
            load_gain(G_MIX2)

            norm_root(4)
            pool.wait_ge(gated, TT * (D // NC))
            for dst, src in ((s_raw, small["w_scal"]), (conv2_col, small["conv2_col"]), (cum, const["cum"]),
                             (rest, const["rest"]), (chunk_ones, const["chunk_ones"]), (level, const["level"])):
                pool.dma_start(dst[:], src).then_inc(small3_loaded, 16)
            pool.dma_start(dft_d[:], const["dft_d"]).then_inc(small3_loaded, 16)
            load_gain(G_MLP)
            pool.wait_ge(pair_free[0], 2 * (U_F + 1) + 2)
            nc.gpsimd.tensor_copy(fr[:, :, 0:NC], s_stage[:, 0]).then_inc(fr_ready, 1)
            for t in range(TT):
                pool.wait_ge(dn_summed, t + 1)
                step(nc.gpsimd.tensor_scalar(dn_rs[:, t, 0:DNH], dn_ss[:, t, 0:DNH], float(DND), DND * EPS, ALU.mult, ALU.add))
                step(nc.gpsimd.tensor_scalar(dn_rs[:, t, DNH:], dn_ss[:, t, DNH:], EPS, None, ALU.add))
                step(nc.gpsimd.tensor_tensor(dn_rs[:, t], dn_rs[:, t], neg_half[:, 0:2 * DNH], ALU.pow))
                qk = qkv2[:, t, 0:2 * DNW].rearrange("p (a d) -> p a d", d=DND)
                nc.gpsimd.tensor_tensor(qk, qk, dn_rs[:, t].unsqueeze(2).to_broadcast([P, 2 * DNH, DND]),
                                        ALU.mult).then_inc(dn_qk_normed, 1)

            pool.wait_ge(dn_pre, 1)
            pool.wait_ge(dn_qkT_evac0, 4)
            pool.wait_ge(dn_qkT_evac1, 4)
            for p in range(2):
                pool.wait_ge(pair_free[p], 2 * (U_MIX + 1))
            shape = [P, TT, 2, P]
            cums = cum[:].unsqueeze(1).to_broadcast(shape)
            with pool.Fori(0, DNH // 2) as i:
                def of_head(v, x):
                    return v[:, :, :, bass.ds(2 * i + x, 1)].to_broadcast(shape)

                def tokens(col0, x):
                    return qkv2[:, :, bass.ds(i * (2 * DND) + col0 + x * DND, DND)].unsqueeze(2).to_broadcast(shape)
                for hd in heads:
                    nc.gpsimd.tensor_tensor(hd.gs, cums, of_head(g2, hd.x), ALU.mult).then_inc(dn_rows, 1)
                for hd in heads:
                    nc.gpsimd.tensor_copy(hd.qk.unsqueeze(2), qk_T[:, :, bass.ds(2 * i + hd.x, 1), :]).then_inc(dn_qk, 1)
                for k in range(1, LEVELS):
                    for hd in heads:
                        if k == 1:
                            pool.wait_ge(dn_m, hd.of(i))
                        else:
                            pool.wait_ge(dn_z, hd.of(i, LEVELS - 1, k - 2))
                        nc.gpsimd.tensor_tensor(hd.mk, hd.m, level[:, k].unsqueeze(1).to_broadcast(shape),
                                                ALU.mult).then_inc(dn_mk, 1)
                    for hd in heads:
                        if k == 1:
                            pool.wait_ge(dn_eT, hd.of(i))
                            nc.gpsimd.tensor_tensor(hd.eT, hd.eT, cums, ALU.mult).then_inc(dn_eTm, 1)
                            pool.wait_ge(dn_egb, hd.of(i))
                            q_rows = hd.qk[:, 0].rearrange("p (t s) -> p t s", t=TT).unsqueeze(2).to_broadcast(shape)
                            nc.gpsimd.tensor_tensor(hd.qd, hd.qd, q_rows, ALU.mult).then_inc(dn_qd, 1)
                        elif k == 2:
                            nc.gpsimd.tensor_tensor(hd.vb, tokens(2 * DNW, hd.x), of_head(beta, hd.x), ALU.mult)
                        elif k == 3:
                            nc.gpsimd.tensor_tensor(hd.kb, tokens(DNW, hd.x), of_head(be, hd.x), ALU.mult)
                        elif k == 4:
                            nc.gpsimd.tensor_tensor(hd.kd, tokens(DNW, hd.x), of_head(kd, hd.x), ALU.mult).then_inc(dn_in, 1)

            for p in range(2):
                pool.wait_ge(pair_free[p], 2 * (U_MIX + 1))
            g_head = row[:, ROW["g_dn_head_2"][0]:ROW["g_dn_head_2"][1]].unsqueeze(1).to_broadcast([P, DNH, DND])
            for t in range(TT):
                zt = z2[:, t].rearrange("p (a d) -> p a d", d=DND)
                nc.gpsimd.tensor_tensor(zt, zt, g_head, ALU.mult).then_inc(z2_scaled, 1)

            for t in range(TT):
                pool.wait_ge(o_summed, t + 1)
                inverse_root(dn_rs[:, t, 0:DNH], dn_ss[:, t, 0:DNH], DNH, 1.0 / DND, EPS, o_rstd)
            norm_root(5)
            load_gain(G_OUT)
            norm_root(6)
        @block.scalar
        def _(act):
            def split(q, s0=0, s1=QUAD, first=False):
                for s in range(s0, s1):
                    act.wait_ge(raw_loaded[s], 16 * (q + 1))
                    if not first:
                        act.wait_ge(slab_done, QUAD * (q - 1) + s + 1)
                    nc.scalar.copy(w_hi[:, s, :], w_raw[:, s, :]).then_inc(hi_ready, 1)

            def squares(src, junk, c, ready=None, count=0):
                cols = slice(c * NC, (c + 1) * NC)
                for t in range(TT):
                    if ready is not None:
                        act.wait_ge(ready, count - TT + 1 + t)
                    nc.scalar.activation(junk[:, t, cols], src[:, t, cols], ACT.Square, accum_out=stat[:, t, c:c + 1]).then_inc(stat_ready, 1)

            def squares_of_h(junk, use, c):
                squares(h, junk, c, pair_free[c % 2], 2 * (use + c // 2 + 2))

            def projected_squares(q0, use, junk):
                for c in range(DC):
                    split(q0 + 2 * c + 1)
                    if c:
                        squares_of_h(junk, use, c - 1)
                    split(q0 + 2 * c + 2)
                squares_of_h(junk, use, DC - 1)

            def rounded_operand(n, q=None):
                for i in range(KT // 2):
                    act.wait_ge(tr_ready, KT // 2 * n + i + 1)
                    nc.scalar.copy(a_hi[:, 2 * i:2 * i + 2, :].rearrange("p k s -> p (k s)"), bank[4 + i % 4][:]).then_inc(a_hi_ready, 1)
                    if q is not None and i >= 5:
                        split(q, i - 5, i - 4 if i < KT // 2 - 1 else QUAD)

            def softplus_parts(n, buf):
                act.wait_ge(sp_abs, n)
                nc.scalar.activation(buf[:, 2], buf[:, 1], ACT.Exp, scale=-1.0).then_inc(sp_exp, 1)
                act.wait_ge(sp_sum, n)
                nc.scalar.activation(buf[:, 4], buf[:, 3], ACT.Ln).then_inc(sp_ln, 1)

            def pairs_empty(uses):
                act.wait_ge(pair_free[0], 2 * (uses + 1))
                act.wait_ge(pair_free[1], 2 * (uses + 1))

            for half in range(2):
                act.wait_ge(x_loaded[half], 16 * (half + 1))
                for c in range(half * DC // 2, (half + 1) * DC // 2):
                    squares(h, xs, c)
            split(0, first=True)
            rounded_operand(TR_ATTN, Q_XBC + 1)
            act.wait_ge(small1_loaded, 8 * 16)
            nc.scalar.copy(w32_hi[:], w32_raw[:]).then_inc(w32_hi_ready, 1)
            q = Q_XBC
            split(q + 2)
            act.wait_ge(slab_done, QUAD * (q + 2))
            nc.scalar.copy(stage[:, 0, 0, :], pair[0][0][:]).then_inc(pair_free[0], 1)
            act.wait_ge(rope_arg, 1)
            nc.scalar.activation(sin[:], ang[:, 3], ACT.Sin)
            nc.scalar.activation(cos[:], ang[:, 5], ACT.Sin).then_inc(rope_ready, 1)
            act.wait_ge(dt_mm, 1)
            nc.scalar.copy(narrow_T[:], bank[7][0:HEADS, 0:SEQ]).then_inc(narrow_copied, 1)
            softplus_parts(1, sp)
            a0, a1 = ROW["a_log"]
            nc.scalar.activation(aneg[:], row[:, a0:a1], ACT.Exp).then_inc(aneg_ready, 1)
            with act.Fori(0, 2) as i:
                for k in range(2):
                    c, par = 2 * i + k, (1 + k) % 2
                    q = Q_XBC + 2 * (2 * i + 1 + k)
                    split(q + 1)
                    split(q + 2, 0, 2)
                    act.wait_ge(conv_done, 2 * c + 2)
                    nc.scalar.activation(cv_act[:], cv[:], ACT.Silu).then_inc(silu_done, 1)
                    split(q + 2, 2, 4)
                    act.wait_ge(slab_done, QUAD * (q + 2))
                    nc.scalar.copy(stage[:, par, 0, :], pair[par][0][:]).then_inc(pair_free[par], 1)
                    act.wait_ge(xbc_back, c + 1)
                    nc.scalar.copy(xs[:, 0, bass.ds(c * NC, NC)], bank[6][:]).then_inc(back0_evac, 1)
            q = Q_XBC + 10
            split(q + 1)
            act.wait_ge(conv_done, 10)
            nc.scalar.activation(bT, cv[:], ACT.Silu).then_inc(silu_done, 1)
            split(q + 2)
            act.wait_ge(slab_done, QUAD * (q + 2))
            nc.scalar.copy(stage[:, 1, 0, :], pair[1][0][:]).then_inc(pair_free[1], 1)
            act.wait_ge(xbc_back, 5)
            nc.scalar.copy(b_tok[:].rearrange("p g n -> p (g n)"), bank[6][:]).then_inc(back0_evac, 1)
            act.wait_ge(conv_done, 12)
            nc.scalar.activation(cT, cv[:], ACT.Silu).then_inc(silu_done, 1)

            with act.Fori(0, D // NC // 2) as i:
                for par in range(2):
                    q = Q_Z + 4 * i + 2 * par
                    split(q + 1)
                    split(q + 2)
                    act.wait_ge(slab_done, QUAD * (q + 2))
                    for t in range(TT):
                        nc.scalar.activation(z[:, t, bass.ds(i * (2 * NC) + par * NC, NC)], pair[par][t][:], ACT.Silu).then_inc(pair_free[par], 1)

            def qkv_evac(c):
                act.wait_ge(slab_done, QUAD * (Q_QKV + 2 * c + 2))
                nc.scalar.copy(qkv[:, 0, c * NC:(c + 1) * NC], pair[c % 2][0][:]).then_inc(pair_free[c % 2], 1)
            split(Q_QKV + 1)
            act.wait_ge(acs_ready, 1)
            nc.scalar.activation(ds[:], sp[:, 0, 0:HEADS], ACT.Exp)
            nc.scalar.activation(ea[:], acs[:, 1, :], ACT.Exp).then_inc(sdecay, 1)
            split(Q_QKV + 2)
            qkv_evac(0)

            def qk_squares(c, t):
                n = TT * c + t
                if c > 1:
                    act.wait_ge(qk_ready, n - 1)
                elif c == 1:
                    act.wait_ge(dskip_ready, 1)
                act.wait_ge(pair_free[c % 2], 2 * (U_QKV + c // 2 + 2))
                nc.scalar.activation(qk_square(c)[:, t], qkv[:, t, c * NC:(c + 1) * NC], ACT.Square).then_inc(qk_sq, 1)
            for g in range(GROUPS):
                q = Q_QKV + 2 * (g + 1)

                def decays(t):
                    act.wait_ge(seg_ready, TT * g + t + 1)
                    nc.scalar.activation(ssm_w, ssm_w, ACT.Exp).then_inc(seg_exp, 1)

                def square(t):
                    act.wait_ge(y_gated, TT * g + t + 1)
                    nc.scalar.activation(ssm_dx[:, t], z[:, t, g * NC:(g + 1) * NC], ACT.Square,
                                         accum_out=ssm_ss[:, t, g:g + 1]).then_inc(y_squared, 1)
                decays(0)
                split(q + 1, 0, 1)
                for t in range(TT):
                    qk_squares(g, t)
                split(q + 1, 1, 2)
                act.wait_ge(state_mm, g + 1)
                nc.scalar.copy(ssm_state, bank[6][:]).then_inc(state_evac, 1)
                split(q + 1, 2, 3)
                decays(1)
                split(q + 1, 3, 4)
                square(0)
                split(q + 2)
                square(1)
                qkv_evac(g + 1)
            q = Q_QKV + 10
            split(q + 1)
            for t in range(TT):
                qk_squares(GROUPS, t)
            split(q + 2)
            qkv_evac(5)
            rounded_operand(TR_YSSM)

            with act.Fori(0, D // NC // 2) as i2:
                for k in range(2):
                    i, q = 2 * i2 + k, Q_WOS + 4 * i2 + 2 * k
                    act.wait_ge(att_qkT, i + 1)
                    nc.scalar.copy(att_qT[:, 0].rearrange("p a s -> p (a s)"), bank[4][:]).then_inc(att_qkT_evac, 1)
                    nc.scalar.copy(att_kT, bank[6][:, 0:SEQ]).then_inc(att_qkT_evac, 1)

                    def exponentials(par):
                        act.wait_ge(att_max, 2 * i + par + 1)
                        for n in range(TT * REP):
                            s0, s1 = att_cols(n)
                            nc.scalar.activation(att_p[par][:, s0:s1], att_p[par][:, s0:s1], ACT.Exp, bias=att_s[:, par, 2, n:n + 1],
                                                 accum_out=att_s[:, par, 4, n:n + 1])
                        nc.scalar.activation(att_s[:, par, 5, :], att_s[:, par, 3, :], ACT.Exp).then_inc(att_exp, 1)

                    def probs_evac(par):
                        act.wait_ge(att_pT, 2 * i + par + 1)
                        nc.scalar.copy(att_pTs[:, 0:NC], bank[4][:]).then_inc(att_pT_evac, 1)
                    split(q + 1, 0, 2)
                    exponentials(0)
                    split(q + 1, 2, 4)
                    split(q + 2, 0, 1)
                    probs_evac(0)
                    exponentials(1)
                    split(q + 2, 1, 2)
                    probs_evac(1)
                    split(q + 2, 2, 4)
            rounded_operand(TR_YATT)
            projected_squares(Q_WOA, U_WOA, xn_f)

            rounded_operand(TR_FFN, Q_FF + 1)

            def ff_evac(par, q):
                act.wait_ge(slab_done, QUAD * (q + 2))
                nc.scalar.copy(f_stage[:, 0, par * FFB:(par + 1) * FFB], pair[par][0][:]).then_inc(pair_free[par], 1)

            def ff_gated_silu(j):
                act.wait_ge(ff_conv, 2 * j + 1)
                nc.scalar.activation(f_silu[:], f_cv[:, 0:4], ACT.Silu).then_inc(ff_silu, 1)

            def ff_gated_hi(j):
                act.wait_ge(ff_mul, j + 1)
                nc.scalar.copy(f_hi[:], f_act[:]).then_inc(ff_hi, 1)

            q = Q_FF
            split(q + 2)
            ff_evac(0, q)
            split(q + 3)
            split(q + 4)
            ff_evac(1, q + 2)
            with act.Fori(0, N_FF - 1) as j:
                q = Q_FF + 4 + 6 * j
                split(q + 1, 0, 2)
                ff_gated_silu(j)
                split(q + 1, 2, 4)
                split(q + 2)
                ff_gated_hi(j)
                ff_evac(0, q)
                split(q + 3)
                split(q + 4)
                ff_evac(1, q + 2)
                split(q + 5)
                split(q + 6)
            def embedding(n):
                act.wait_ge(ple_mm, n + 1)
                for t in range(TT):
                    nc.scalar.copy(pe_tok[:, t, n * NC:(n + 1) * NC], pair[n % 2][t][:]).then_inc(pair_free[n % 2], 1)
                act.wait_ge(pair_free[n % 2], 2 * (U_PLE + n // 2 + 2))
                squares(pe_tok, xn_f, n)
            embedding(0)
            embedding(1)
            ff_gated_silu(N_FF - 1)
            embedding(2)
            embedding(3)
            ff_gated_hi(N_FF - 1)
            split(Q_GATE - 1)
            for n in range(DC):
                if n == 2:
                    split(Q_GATE, 0, 3)
                if n == 3:
                    split(Q_GATE, 3)
                squares_of_h(xn_f, U_GATE - 2, n)

            rounded_operand(TR_PLE, Q_GATE + 1)
            for n in range(D // NC):
                q = Q_GATE + 2 * n
                if n:
                    split(q + 1)
                if n:
                    squares(h, qkv2, n - 1, gated, TT * n)
                split(q + 2, 0, QUAD - 1)
                act.wait_ge(slab_done, QUAD * (q + 2))
                for t in range(TT):
                    nc.scalar.activation(sig[:, t], pair[n % 2][t][:], ACT.Sigmoid).then_inc(sig_ready, 1)
                split(q + 2, QUAD - 1)

            squares(h, qkv2, DC - 1, gated, TT * DC)
            rounded_operand(TR_MIX2, Q_QKV2 + 1)
            act.wait_ge(small3_loaded, 7 * 16)
            nc.scalar.copy(s_hi[:], s_raw[:]).then_inc(s_hi_ready, 1)
            q = Q_QKV2
            split(q + 2)
            act.wait_ge(slab_done, QUAD * (q + 2))
            nc.scalar.copy(s_stage[:, 0, 0, :], pair[0][0][:]).then_inc(pair_free[0], 1)
            with act.Fori(0, 3) as i:
                for k in range(2):
                    c, par = 2 * i + k, (1 + k) % 2
                    q = Q_QKV2 + 2 * (2 * i + 1 + k)
                    split(q + 1)
                    split(q + 2, 0, 2)
                    act.wait_ge(conv2_done, 2 * c + 2)
                    nc.scalar.activation(s_act[:], s_cv[:], ACT.Silu).then_inc(silu2_done, 1)
                    split(q + 2, 2, 4)
                    act.wait_ge(slab_done, QUAD * (q + 2))
                    nc.scalar.copy(s_stage[:, par, 0, :], pair[par][0][:]).then_inc(pair_free[par], 1)
                    act.wait_ge(qkv2_back, c + 1)
                    nc.scalar.copy(qkv2[:, 0, bass.ds(c * NC, NC)], bank[6][:]).then_inc(back2_evac0, 1)
            act.wait_ge(sc_mm, 1)
            nc.scalar.copy(narrow2_T[:], bank[5][0:4 * DNH, 0:SEQ]).then_inc(narrow_copied, 1)
            q = Q_F + 2
            split(q + 1)
            act.wait_ge(sc_t, 1)
            act.wait_ge(sp_abs, 2)
            sc_view = bank[5][:, SEQ:SEQ + TT * 4 * DNH].rearrange("p (t a) -> p t a", t=TT)
            nc.scalar.activation(beta[:].rearrange("p t d a -> p t (d a)"), sc_view[:, :, 0:2 * DNH], ACT.Sigmoid).then_inc(beta_ready, 1)
            nc.scalar.activation(aneg2[:], row[:, ROW["a_log_fwd_2"][0]:ROW["a_log_bwd_2"][1]], ACT.Exp).then_inc(aneg_ready, 1)
            softplus_parts(2, sp2)
            split(q + 2)
            act.wait_ge(slab_done, QUAD * (q + 2))
            nc.scalar.copy(fr[:, 0, NC:], pair[1][0][:]).then_inc(pair_free[1], 1)

            def z_evac(par):
                act.wait_ge(slab_done, QUAD * (Q_Z2 + 2 * par + 2))
                for t in range(TT):
                    nc.scalar.activation(z2[:, t, par * NC:(par + 1) * NC], pair[par][t][:], ACT.Silu).then_inc(pair_free[par], 1)
            act.wait_ge(back2_evac1, 7)
            q = Q_Z2
            nc.scalar.activation(mix[:, 0], qkv2[:, 0, 0:2 * DNW], ACT.Square).then_inc(dn_sq, 1)
            split(q + 1)
            nc.scalar.activation(mix[:, 1], qkv2[:, 1, 0:2 * DNW], ACT.Square).then_inc(dn_sq, 1)
            split(q + 2)
            z_evac(0)
            split(q + 3)
            act.wait_ge(gc_mm, 1)
            for x, c0 in zip([x[:].rearrange("p a d h -> p (a d h)") for x in (be, kd, gl)], (0, 32, 64)):
                last = nc.scalar.activation(x, bank[4][:, c0:c0 + x.shape[1]], ACT.Exp)
            last.then_inc(gc_exp, 1)
            z_evac(1)
            for n in range(0, 8, 2):
                act.wait_ge(dn_qkT, n + 1)
                nc.scalar.copy(qkh[:, 2 * n:2 * n + 2].rearrange("p a s -> p (a s)"), bank[4 + n % 4][:]).then_inc(dn_qkT_evac0, 1)

            with act.Fori(0, DNH // 2) as i:
                for hd in heads:
                    act.wait_ge(dn_diff, hd.of(i, 2, 0))
                    nc.scalar.activation(hd.eN, hd.eN, ACT.Exp, scale=-1.0).then_inc(dn_eN, 1)
                for hd in heads:
                    act.wait_ge(dn_rT, hd.of(i))
                    nc.scalar.copy(flat(hd.r), hd.bank[2][:]).then_inc(dn_r0, 1)
                    act.wait_ge(dn_diff, hd.of(i, 2, 1))
                    nc.scalar.activation(hd.eT, hd.eT, ACT.Exp).then_inc(dn_eT, 1)
                    nc.scalar.activation(flat(hd.qd), hd.bank[0][:], ACT.Exp).then_inc(dn_egb, 1)
                for k in range(1, LEVELS):
                    for hd in heads:
                        act.wait_ge(dn_z, hd.of(i, LEVELS - 1, k - 1))
                        nc.scalar.copy(flat(hd.zz), hd.bank[3][:]).then_inc(dn_zz, 1)
                for hd in heads:
                    act.wait_ge(dn_uw, hd.of(i))
                    nc.scalar.copy(flat(hd.wT), hd.bank[2][:]).then_inc(dn_wT, 1)
            act.wait_ge(dn_free, DNH + 2)
            act.dma_start(dft_t[:], const["dft_t"]).then_inc(small4_loaded, 16)
            split(Q_MIX)
            for t in range(TT):
                act.wait_ge(dn_free, DNH + 2)
                nc.scalar.activation(mix[:, t, 0:DNW], qkv2[:, t, 0:DNW], ACT.Square).then_inc(o_sq, 1)
            for g in range(DNH):
                act.wait_ge(f_mm, g + 1)
                nc.scalar.copy(f_half[:, g % 2].rearrange("p c s -> p (c s)"), bank[4 + g % 2][:]).then_inc(f_half_ready, 1)
                act.wait_ge(f_out, g + 1)
                nc.scalar.copy(fr_hi[:, g], bank[6 + g % 2][:, 0:SEQ]).then_inc(fr_hi_ready, 1)

            for n in range(4):
                act.wait_ge(y_t, n + 1)
                nc.scalar.copy(y_hi[:, 2 * n:2 * n + 2].rearrange("p k s -> p (k s)"), bank[4 + n][:]).then_inc(y_hi_ready, 1)


            with act.Fori(0, D // NC) as n:
                q = Q_MIX + 6 * n
                for k, p in enumerate((0, 1)):
                    split(q + 2 * k + 1)
                    split(q + 2 * k + 2)
                    act.wait_ge(slab_done, QUAD * (q + 2 * k + 2))
                    act.wait_ge(pair_free[2 + p], 2 * (V_MIX + n + 1))
                    for t in range(TT):
                        nc.scalar.activation(z2[:, t, p * NC:(p + 1) * NC], pair[p][t][:], ACT.Sigmoid).then_inc(pair_free[p], 1)
                split(q + 5)
                split(q + 6)
            rounded_operand(TR_WO2)
            projected_squares(Q_WO2, U_WO2, xn_m)

            rounded_operand(TR_MLP, Q_MLP + 1)

            def mlp_evac(q, p):
                act.wait_ge(slab_done, QUAD * (q + 2))
                nc.scalar.copy(m_stage[:, 0], pair[p][0][:]).then_inc(pair_free[p], 1)

            def mlp_relu(j):
                act.wait_ge(ff_t, N_FF + j + 1)
                for b in range(2):
                    nc.scalar.activation(m_relu[:, 2 * b:2 * b + 2].rearrange("p k s -> p (k s)"), bank[6 + b][:], ACT.Relu).then_inc(ff_silu, 1)
                for b in range(2):
                    act.wait_ge(ff_silu, N_FF + 2 * j + b + 1)
                    nc.scalar.activation(m_hi[:, 2 * b:2 * b + 2], m_relu[:, 2 * b:2 * b + 2], ACT.Square).then_inc(ff_hi, 1)

            q = Q_MLP
            split(q + 2)
            mlp_evac(q, 0)
            with act.Fori(0, N_FF2 - 1) as j:
                q = Q_MLP + 2 + 4 * j
                split(q + 1, 0, 1)
                mlp_relu(j)
                split(q + 1, 1)
                split(q + 2)
                mlp_evac(q, 2)
                split(q + 3)
                split(q + 4)
            mlp_relu(N_FF2 - 1)
            split(N_QUADS - 1)
            for n in range(DC):
                squares_of_h(xn_m, U_MLP + 2 * (N_FF2 - 1) + 1 - n % 2, n)
            act.wait_ge(normed, NORMED[G_MLP] + DC - 1)
            act.wait_ge(rstd_ready, 2 * 7)
            for c in range(DC // 2):
                cols = slice(c * NC, (c + 1) * NC)
                for t in range(TT):
                    last = nc.scalar.activation(xn_m[:, t, cols], h[:, t, cols], ACT.Copy, scale=rstd[:, t:t + 1])
                last.then_inc(out_scaled, 1)

        @block.vector
        def _(dve):
            step = Chain(dve, dve_step)
            V = nc.vector

            def split(q, s0=0, s1=QUAD):
                for s in range(s0, s1):
                    dve.wait_ge(hi_ready, QUAD * q + s + 1)
                    V.tensor_tensor(w_lo[:, s, :], w_raw[:, s, :], w_hi[:, s, :].bitcast(F32), ALU.subtract).then_inc(lo_ready, 1)

            def rest_of_operand(n, i0=0, i1=KT // 2):
                for i in range(i0, i1):
                    dve.wait_ge(a_hi_ready, KT // 2 * n + i + 1)
                    V.tensor_tensor(a_lo[:, 2 * i:2 * i + 2, :].rearrange("p k s -> p (k s)"), bank[4 + i % 4][:],
                                    a_hi[:, 2 * i:2 * i + 2, :].rearrange("p k s -> p (k s)").bitcast(F32),
                                    ALU.subtract).then_inc(a_lo_ready, 1)

            def mean_square(n):
                dve.wait_ge(stat_ready, TT * DC * (n + 1))
                step(V.tensor_reduce(rstd[:, TT:2 * TT], stat[:], AX.X, ALU.add))
                V.tensor_scalar(rstd[:, 0:TT], rstd[:, TT:2 * TT], 1.0 / D, EPS, ALU.mult, ALU.add).then_inc(rstd_ready, 1)

            def normalize(dst, src, n, g, c0=0, c1=DC):
                if c0 == 0:
                    mean_square(n)
                    dve.wait_ge(rstd_ready, 2 * (n + 1))
                    dve.wait_ge(gain_loaded, 16 * (g + 1))
                for c in range(c0, c1):
                    cols = slice(c * NC, (c + 1) * NC)
                    for t in range(TT):
                        V.scalar_tensor_tensor(dst[:, t, cols], src[:, t, cols], rstd[:, t:t + 1], gain[:, cols],
                                               ALU.mult, ALU.mult).then_inc(normed, 1)

            def last_of_operand(n, i0, q):
                for i in range(i0, KT // 2):
                    rest_of_operand(n, i, i + 1)
                    if i >= 5:
                        split(q, i - 5, i - 4 if i < KT // 2 - 1 else QUAD)

            def normalized_operand(dst, n, g, tr, q):
                normalize(dst, h, n, g, 0, 2)
                rest_of_operand(tr, 0, 1)
                normalize(dst, h, n, g, 2, 3)
                rest_of_operand(tr, 1, 3)
                normalize(dst, h, n, g, 3, 4)
                last_of_operand(tr, 3, q)

            def softplus(n, buf, out):
                V.scalar_tensor_tensor(buf[:, 1], buf[:, 0], -1.0, buf[:, 0], ALU.mult, ALU.max).then_inc(sp_abs, 1)
                dve.wait_ge(sp_exp, n)
                V.tensor_scalar(buf[:, 3], buf[:, 2], 1.0, None, ALU.add).then_inc(sp_sum, 1)
                dve.wait_ge(sp_sum, n)
                step(V.tensor_scalar(buf[:, 5], buf[:, 3], -1.0, None, ALU.add))
                step(V.tensor_tensor(buf[:, 5], buf[:, 2], buf[:, 5], ALU.subtract))
                step(V.reciprocal(buf[:, 1], buf[:, 3]))
                step(V.tensor_tensor(buf[:, 5], buf[:, 5], buf[:, 1], ALU.mult))
                dve.wait_ge(sp_ln, n)
                step(V.tensor_tensor(buf[:, 5], buf[:, 5], buf[:, 4], ALU.add))
                step(V.scalar_tensor_tensor(out, buf[:, 0], 0.0, buf[:, 5], ALU.max, ALU.add))

            def add_to_h(p, col):
                for t in range(TT):
                    V.tensor_tensor(h[:, t, col], h[:, t, col], pair[p][t][:], ALU.add).then_inc(pair_free[p], 1)

            def project_into_h(q0):
                with dve.Fori(0, D // NC // 2) as i:
                    for par in range(2):
                        q = q0 + 4 * i + 2 * par
                        split(q + 1)
                        split(q + 2, 0, QUAD - 1)
                        dve.wait_ge(slab_done, QUAD * (q + 2))
                        add_to_h(par, bass.ds(i * (2 * NC) + par * NC, NC))
                        split(q + 2, QUAD - 1)

            def convolve(dst, src, col, taps, back, done, bias):
                tiles = dst.shape[1]
                for n, j in enumerate([back] + [j for j in range(taps) if j != back]):
                    d = j - back
                    for ct in range(tiles):
                        w = col(ct, j)
                        if n == 0 and bias:
                            last = V.tensor_scalar(dst[:, ct], src(ct), w, col(ct, taps), ALU.mult, ALU.add)
                        elif n == 0:
                            last = V.tensor_scalar(dst[:, ct], src(ct), w, None, ALU.mult)
                        else:
                            o = slice(max(0, -d), SEQ - max(0, d))
                            s = slice(max(0, d), SEQ - max(0, -d))
                            last = V.scalar_tensor_tensor(dst[:, ct, o], src(ct)[:, s], w, dst[:, ct, o], ALU.mult, ALU.add)
                    if n < taps - 1:
                        step(last)
                last.then_inc(done, 1)

            def tile_in_bank(first):
                return lambda ct: bank[first + ct // 2][:, (ct % 2) * SEQ:(ct % 2 + 1) * SEQ]

            normalize(xs, h, 0, G_ATTN, 0, 2)
            split(0, 0, 1)
            rest_of_operand(TR_ATTN, 0, 1)
            normalize(xs, h, 0, G_ATTN, 2, 3)
            split(0, 1, 2)
            rest_of_operand(TR_ATTN, 1, 3)
            normalize(xs, h, 0, G_ATTN, 3, 4)
            split(0, 2, 3)
            rest_of_operand(TR_ATTN, 3, 4)
            split(0, 3, 4)
            last_of_operand(TR_ATTN, 4, Q_XBC + 1)
            dve.wait_ge(w32_hi_ready, 1)
            V.tensor_tensor(w32_lo[:], w32_raw[:], w32_hi[:].bitcast(F32), ALU.subtract).then_inc(w32_lo_ready, 1)
            dve.wait_ge(small1_loaded, 8 * 16)
            step(V.tensor_copy(pos_f[:], pos_i[:]))
            for t in range(TT):
                last = V.tensor_scalar(ang[:, 0, t], inv_freq[:], pos_f[:, t:t + 1], None, ALU.mult)
            step(last)
            step(V.tensor_scalar(ang[:, 1], ang[:, 0], float(1 / (2 * np.pi)), ROUND, ALU.mult, ALU.add))
            step(V.tensor_scalar(ang[:, 1], ang[:, 1], -ROUND, None, ALU.add))
            src = ang[:, 0]
            for part_2pi in TWO_PI:
                step(V.scalar_tensor_tensor(ang[:, 2], ang[:, 1], -part_2pi, src, ALU.mult, ALU.add))
                src = ang[:, 2]
            step(V.tensor_scalar(ang[:, 3], ang[:, 2], PI_BELOW, -PI_BELOW, ALU.min, ALU.max))
            step(V.scalar_tensor_tensor(ang[:, 4], ang[:, 3], -1.0, ang[:, 3], ALU.mult, ALU.max))
            V.tensor_scalar(ang[:, 5], ang[:, 4], -1.0, float(np.pi / 2), ALU.mult, ALU.add).then_inc(rope_arg, 1)
            def xbc_convolve(c, half):
                dve.wait_ge(xbc_t, c + 1)
                convolve(cv[:, 2 * half:2 * half + 2], tile_in_bank(4 + half),
                         lambda ct, j: conv_col[:, bass.ds(c * 4 + 2 * half + ct, 1), j], CONV1, CONV1 - 1, conv_done, True)

            q = Q_XBC
            split(q + 2)
            dve.wait_ge(slab_done, QUAD * (q + 2))
            V.tensor_copy(stage[:, 0, 1, :], pair[0][1][:]).then_inc(pair_free[0], 1)
            dve.wait_ge(dt_t, 1)
            for t in range(TT):
                last = V.tensor_tensor(sp[:, 0, t * HEADS:(t + 1) * HEADS], bank[7][:, SEQ + t * HEADS:SEQ + (t + 1) * HEADS],
                                       row[:, ROW["dt_bias"][0]:ROW["dt_bias"][1]], ALU.add)
            step(last)
            softplus(1, sp, dt[:].rearrange("p t a -> p (t a)"))
            dve.wait_ge(aneg_ready, 1)
            for t in range(TT):
                last = V.scalar_tensor_tensor(adt[:, t], dt[:, t], -1.0, aneg[:], ALU.mult, ALU.mult)
            last.then_inc(adt_ready, 1)
            with dve.Fori(0, 2) as i:
                step.enter(i, 2 * 2 * (CONV1 - 1))
                for k in range(2):
                    c, par = 2 * i + k, (1 + k) % 2
                    q = Q_XBC + 2 * (2 * i + 1 + k)
                    split(q + 1, 0, 2)
                    xbc_convolve(c, 0)
                    split(q + 1, 2, 4)
                    xbc_convolve(c, 1)
                    split(q + 2)
                    dve.wait_ge(slab_done, QUAD * (q + 2))
                    V.tensor_copy(stage[:, par, 1, :], pair[par][1][:]).then_inc(pair_free[par], 1)
                    dve.wait_ge(xbc_back, c + 1)
                    V.tensor_copy(xs[:, 1, bass.ds(c * NC, NC)], bank[7][:]).then_inc(back1_evac, 1)
                step.leave(2)
            q = Q_XBC + 10
            split(q + 1, 0, 2)
            xbc_convolve(4, 0)
            split(q + 1, 2, 4)
            xbc_convolve(4, 1)
            split(q + 2)
            dve.wait_ge(slab_done, QUAD * (q + 2))
            V.tensor_copy(stage[:, 1, 1, :], pair[1][1][:]).then_inc(pair_free[1], 1)
            dve.wait_ge(silu_done, 5)
            xbc_convolve(5, 0)
            xbc_convolve(5, 1)

            with dve.Fori(0, D // NC) as i:
                split(Q_Z + 2 * i + 1)
                split(Q_Z + 2 * i + 2)

            dve.wait_ge(acs_mm, 1)
            step(V.tensor_copy(acs[:].rearrange("p t a -> p (t a)"), bank[4][:, 0:TT * HEADS]))
            V.tensor_tensor(sp[:, 0, 0:HEADS], bank[4][:, TT * HEADS:(TT + 1) * HEADS], acs[:, 0], ALU.subtract).then_inc(acs_ready, 1)
            split(Q_QKV + 1)
            dve.wait_ge(cb_mm, 1)
            for b in range(2):
                last = V.tensor_tensor(ssm_cb[:, 2 * b:2 * b + 2].rearrange("p g t s -> p (g t) s"),
                                       bank[5 + b][:].rearrange("p (g s) -> p g s", s=P),
                                       before[:].unsqueeze(1).to_broadcast([P, 4, P]), ALU.mult)
            last.then_inc(cb_ready, 1)
            split(Q_QKV + 2)

            def qkv_evac(c):
                dve.wait_ge(slab_done, QUAD * (Q_QKV + 2 * c + 2))
                V.tensor_copy(qkv[:, 1, c * NC:(c + 1) * NC], pair[c % 2][1][:]).then_inc(pair_free[c % 2], 1)
            qkv_evac(0)

            def qk_sums(c, t):
                dve.wait_ge(qk_sq, TT * c + t + 1)
                heads8 = slice(c * NC // HD, (c + 1) * NC // HD)
                V.tensor_reduce(qk_ss[:, t, heads8], qk_square(c)[:, t].rearrange("p (a d) -> p a d", d=HD), AX.X, ALU.add).then_inc(qk_summed, 1)
            for g in range(GROUPS):
                cols = slice(g * NC, (g + 1) * NC)
                q = Q_QKV + 2 * (g + 1)

                def decays(t):
                    n = TT * g + t
                    dve.wait_ge(row_mm, n + 1)
                    if n:
                        dve.wait_ge(ydiag_mm, n)
                    for a in range(HPG):
                        last = V.tensor_scalar(ssm_w[:, a], bank[4 + a // 4][:, (a % 4) * P:(a % 4 + 1) * P],
                                               acs[:, t, g * HPG + a:g * HPG + a + 1], 0.0, ALU.subtract, ALU.min)
                    last.then_inc(seg_ready, 1)

                def gated_output(t):
                    dve.wait_ge(ydiag_mm, TT * g + t + 1)
                    dve.wait_ge(dskip_ready, g + 1)
                    if g == 0:
                        dve.wait_ge(qk_ready, t + 1)
                    step(V.tensor_tensor(ssm_y, bank[7][:], ssm_dx[:, t], ALU.add))
                    if t == 1:
                        dve.wait_ge(yoff_mm, g + 1)
                        w = ea[:, g * HPG:(g + 1) * HPG].unsqueeze(2).to_broadcast([P, HPG, HD])
                        step(V.tensor_tensor(ssm_off.rearrange("p (a d) -> p a d", d=HD),
                                             bank[6][:].rearrange("p (a d) -> p a d", d=HD), w, ALU.mult))
                        step(V.tensor_tensor(ssm_y, ssm_y, ssm_off, ALU.add))
                    V.tensor_tensor(z[:, t, cols], z[:, t, cols], ssm_y, ALU.mult).then_inc(y_gated, 1)
                decays(0)
                split(q + 1, 0, 1)
                for t in range(TT):
                    qk_sums(g, t)
                split(q + 1, 1, 3)
                decays(1)
                gated_output(0)
                split(q + 1, 3, 4)
                split(q + 2, 0, 2)
                gated_output(1)
                split(q + 2, 2, 4)
                qkv_evac(g + 1)
            q = Q_QKV + 10
            split(q + 1)
            dve.wait_ge(ssm_rstd, 1)
            dve.wait_ge(gain_loaded, 16 * (G_SSM + 1))
            for half in range(2):
                qk_sums(GROUPS, half)
                for g in range(2 * half, 2 * half + 2):
                    cols = slice(g * NC, (g + 1) * NC)
                    for t in range(TT):
                        V.scalar_tensor_tensor(z[:, t, cols], z[:, t, cols], ssm_rs[:, t, g:g + 1], gain[:, cols],
                                               ALU.mult, ALU.mult).then_inc(normed, 1)
                if half == 0:
                    split(q + 2, 0, 2)
            rest_of_operand(TR_YSSM, 0, KT // 4)
            qkv_evac(5)
            rest_of_operand(TR_YSSM, KT // 4)
            split(q + 2, 2, 4)

            scale = float(HD ** -0.5)
            s_max, s_m, s_neg, s_sink, s_sum, s_esink, s_tot, s_inv = range(8)
            with dve.Fori(0, D // NC // 2) as i2:
                step.enter(i2, 2 * 2 * 5)
                for k in range(2):
                    i, q = 2 * i2 + k, Q_WOS + 4 * i2 + 2 * k

                    def masked(par):
                        p = att_p[par]
                        dve.wait_ge(att_scored, 2 * i + par + 1)
                        V.scalar_tensor_tensor(p[:, 0:NC].rearrange("p (a k) -> p a k", a=REP),
                                               bank[4][:].rearrange("p (a k) -> p a k", a=REP), scale,
                                               att_mask[:, 0].unsqueeze(1).to_broadcast([P, REP, P]), ALU.mult, ALU.add)
                        for b in range(2):
                            last = V.scalar_tensor_tensor(
                                p[:, (b + 1) * NC:(b + 2) * NC].rearrange("p (a k) -> p a k", a=2),
                                bank[5 + b][:].rearrange("p (a k) -> p a k", a=2), scale,
                                att_mask[:, 1:3].rearrange("p b k -> p (b k)").unsqueeze(1).to_broadcast([P, 2, 2 * P]),
                                ALU.mult, ALU.add)
                        last.then_inc(att_masked, 1)

                    def by_tile(par, n):
                        return att_s[:, par, n, :].rearrange("p (t a) -> p t a", t=TT)

                    def maximum(par):
                        p, s = att_p[par], att_s[:, par]
                        dve.wait_ge(att_masked, 2 * i + par + 1)
                        V.tensor_reduce(s[:, s_max, 0:REP], p[:, 0:NC].rearrange("p (a k) -> p a k", a=REP), AX.X, ALU.max)
                        step(V.tensor_reduce(s[:, s_max, REP:2 * REP], p[:, NC:3 * NC].rearrange("p (a k) -> p a k", a=REP), AX.X, ALU.max))
                        sink = row[:, bass.ds(i2 * (4 * REP) + ROW["sinks"][0] + (2 * k + par) * REP, REP)].unsqueeze(1).to_broadcast([P, TT, REP])
                        step(V.tensor_tensor(by_tile(par, s_m), by_tile(par, s_max), sink, ALU.max))
                        step(V.tensor_scalar(s[:, s_neg], s[:, s_m], -1.0, None, ALU.mult))
                        V.tensor_tensor(by_tile(par, s_sink), by_tile(par, s_neg), sink, ALU.add).then_inc(att_max, 1)

                    def probs_evac(par):
                        s = att_s[:, par]
                        dve.wait_ge(att_exp, 2 * i + par + 1)
                        step(V.tensor_tensor(s[:, s_tot], s[:, s_sum], s[:, s_esink], ALU.add))
                        step(V.reciprocal(s[:, s_inv], s[:, s_tot]))
                        dve.wait_ge(att_pT, 2 * i + par + 1)
                        for b in range(2):
                            V.tensor_copy(att_pTs[:, (b + 1) * NC:(b + 2) * NC], bank[5 + b][:]).then_inc(att_pT_evac, 1)

                    def output(par):
                        dve.wait_ge(att_pv, 2 * i + par + 1)
                        for t in range(TT):
                            inv = att_s[:, par, s_inv, t * REP:(t + 1) * REP].unsqueeze(2).to_broadcast([P, REP, HD])
                            last = V.tensor_tensor(
                                qkv[:, t, bass.ds(i2 * (4 * REP * HD) + (2 * k + par) * REP * HD, REP * HD)].rearrange("p (a d) -> p a d", d=HD),
                                bank[7][:, t * REP * HD:(t + 1) * REP * HD].rearrange("p (a d) -> p a d", d=HD), inv, ALU.mult)
                        last.then_inc(att_done, 1)

                    dve.wait_ge(att_qkT, i + 1)
                    V.tensor_copy(att_qT[:, 1].rearrange("p a s -> p (a s)"), bank[5][:]).then_inc(att_qkT_evac, 1)
                    split(q + 1, 0, 1)
                    masked(0)
                    split(q + 1, 1, 2)
                    maximum(0)
                    masked(1)
                    split(q + 1, 2, 4)
                    probs_evac(0)
                    maximum(1)
                    split(q + 2, 0, 2)
                    output(0)
                    probs_evac(1)
                    split(q + 2, 2, 3)
                    output(1)
                    split(q + 2, 3, 4)
                    dve.wait_ge(slab_done, QUAD * (q + 2))
                    add_to_h(k, bass.ds(i2 * (2 * NC) + k * NC, NC))
                step.leave(D // NC // 2)
            rest_of_operand(TR_YATT)
            project_into_h(Q_WOA)

            normalized_operand(xn_f, 1, G_FFN, TR_FFN, Q_FF + 1)

            def ff_evac(par, q):
                dve.wait_ge(slab_done, QUAD * (q + 2))
                V.tensor_copy(f_stage[:, 1, par * FFB:(par + 1) * FFB], pair[par][1][:]).then_inc(pair_free[par], 1)

            def ff_convolve(j, half):
                if half == 0:
                    dve.wait_ge(ff_t, j + 1)
                k0 = half * (FFB // P)
                convolve(f_cv[:, k0:k0 + FFB // P], tile_in_bank(4 + 2 * half), lambda ct, k: ff_col[:, bass.ds(j, 1), k0 + ct, k],
                         CONV_FF, CONV_FF - 1, ff_conv, True)

            def ff_gated(j):
                dve.wait_ge(ff_conv, 2 * j + 2)
                dve.wait_ge(ff_silu, j + 1)
                V.tensor_tensor(f_act[:], f_silu[:], f_cv[:, 4:8], ALU.mult).then_inc(ff_mul, 1)

            def ff_gated_lo(j):
                dve.wait_ge(ff_hi, j + 1)
                V.tensor_tensor(f_lo[:], f_act[:], f_hi[:].bitcast(F32), ALU.subtract).then_inc(ff_lo, 1)

            def ff_down(q):
                for n in range(D // NC):
                    split(q + 1 + n // 2, 2 * (n % 2), 2 * (n % 2) + 1)
                    dve.wait_ge(slab_done, QUAD * q + 2 * (n + 1))
                    add_to_h(n % 2, slice(n * NC, (n + 1) * NC))
                    split(q + 1 + n // 2, 2 * (n % 2) + 1, 2 * (n % 2) + 2)

            q = Q_FF
            split(q + 2)
            ff_evac(0, q)
            split(q + 3)
            split(q + 4)
            ff_evac(1, q + 2)
            dve.wait_ge(small2_loaded, 3 * 16)
            with dve.Fori(0, N_FF - 1) as j:
                step.enter(j, 2 * (CONV_FF - 1))
                q = Q_FF + 4 + 6 * j
                ff_convolve(j, 0)
                split(q + 1)
                ff_convolve(j, 1)
                split(q + 2, 0, 2)
                ff_gated(j)
                split(q + 2, 2, 4)
                ff_gated_lo(j)
                ff_evac(0, q)
                split(q + 3)
                split(q + 4)
                ff_evac(1, q + 2)
                ff_down(q + 4)
                step.leave(N_FF - 1)
            ff_convolve(N_FF - 1, 0)
            ff_convolve(N_FF - 1, 1)
            ff_gated(N_FF - 1)
            ff_gated_lo(N_FF - 1)
            normalize(pe_tok, pe_tok, 2, G_POST)
            ff_down(Q_GATE - 2)

            normalized_operand(xn_f, 3, G_PLE, TR_PLE, Q_GATE + 1)
            for n in range(D // NC):
                q = Q_GATE + 2 * n
                if n:
                    split(q + 1)
                split(q + 2, 0, QUAD - 1)
                cols = slice(n * NC, (n + 1) * NC)
                for t in range(TT):
                    dve.wait_ge(sig_ready, TT * n + t + 1)
                    last = V.tensor_tensor(sig[:, t], sig[:, t], pe_tok[:, t, cols], ALU.mult)
                step(last)
                for t in range(TT):
                    V.tensor_tensor(h[:, t, cols], h[:, t, cols], sig[:, t], ALU.add).then_inc(gated, 1)
                split(q + 2, QUAD - 1)

            normalized_operand(qkv2[:, :, 0:D], 4, G_MIX2, TR_MIX2, Q_QKV2 + 1)
            dve.wait_ge(s_hi_ready, 1)
            V.tensor_tensor(s_lo[:], s_raw[:], s_hi[:].bitcast(F32), ALU.subtract).then_inc(s_lo_ready, 1)
            q = Q_QKV2
            split(q + 2)
            dve.wait_ge(slab_done, QUAD * (q + 2))
            V.tensor_copy(s_stage[:, 0, 1, :], pair[0][1][:]).then_inc(pair_free[0], 1)
            dve.wait_ge(small3_loaded, 7 * 16)
            with dve.Fori(0, 3) as i:
                step.enter(i, 2 * 2 * (CONV2 - 1))
                for k in range(2):
                    c, par = 2 * i + k, (1 + k) % 2
                    q = Q_QKV2 + 2 * (2 * i + 1 + k)
                    for half in range(2):
                        split(q + 1, 2 * half, 2 * half + 2)
                        dve.wait_ge(qkv2_t, c + 1)
                        convolve(s_cv[:, 2 * half:2 * half + 2], tile_in_bank(4 + half),
                                 lambda ct, j: conv2_col[:, bass.ds(c * 4 + 2 * half + ct, 1), j], CONV2, CONV2 // 2, conv2_done, False)
                    split(q + 2)
                    dve.wait_ge(slab_done, QUAD * (q + 2))
                    V.tensor_copy(s_stage[:, par, 1, :], pair[par][1][:]).then_inc(pair_free[par], 1)
                    dve.wait_ge(qkv2_back, c + 1)
                    V.tensor_copy(qkv2[:, 1, bass.ds(c * NC, NC)], bank[7][:]).then_inc(back2_evac1, 1)
                step.leave(3)
            q = Q_F + 2
            split(q + 1)
            dve.wait_ge(sc_t, 1)
            sc_view = bank[5][:, SEQ:SEQ + TT * 4 * DNH].rearrange("p (t a) -> p t a", t=TT)
            bias = row[:, ROW["dt_bias_fwd_2"][0]:ROW["dt_bias_bwd_2"][1]].unsqueeze(1).to_broadcast([P, TT, 2 * DNH])
            step(V.tensor_tensor(sp2[:, 0].rearrange("p (t a) -> p t a", t=TT), sc_view[:, :, 2 * DNH:], bias, ALU.add))
            g2_tok = g2[:].rearrange("p t d a -> p t (d a)")
            softplus(2, sp2, g2[:].rearrange("p t d a -> p (t d a)"))
            dve.wait_ge(aneg_ready, 2)
            dve.wait_ge(beta_ready, 1)
            V.scalar_tensor_tensor(g2_tok, g2_tok, -1.0, aneg2[:].unsqueeze(1).to_broadcast([P, TT, 2 * DNH]),
                                   ALU.mult, ALU.mult).then_inc(g2_ready, 1)
            split(q + 2)
            dve.wait_ge(slab_done, QUAD * (q + 2))
            V.tensor_copy(fr[:, 1, NC:], pair[1][1][:]).then_inc(pair_free[1], 1)
            for t in range(TT):
                split(Q_Z2 + 1 + t)
                dve.wait_ge(dn_sq, t + 1)
                V.tensor_reduce(dn_ss[:, t], mix[:, t].rearrange("p (a d) -> p a d", d=DND), AX.X, ALU.add).then_inc(dn_summed, 1)
            split(Q_Z2 + 3)
            dve.wait_ge(gc_exp, 1)
            V.tensor_copy(gc[:].rearrange("p t d a -> p (t d a)"), bank[4][:, 0:32])
            V.tensor_tensor(be[:].rearrange("p t d a -> p (t d a)"), be[:].rearrange("p t d a -> p (t d a)"),
                            beta[:].rearrange("p t d a -> p (t d a)"), ALU.mult).then_inc(dn_pre, 1)
            for n in range(1, 8, 2):
                dve.wait_ge(dn_qkT, n + 1)
                V.tensor_copy(qkh[:, 2 * n:2 * n + 2].rearrange("p a s -> p (a s)"), bank[4 + n % 4][:]).then_inc(dn_qkT_evac1, 1)

            steps = SEQ // CHUNK
            unit = [(t, d) for t in range(TT) for d in range(2)]
            with dve.Fori(0, DNH // 2) as i:
                step.enter(i, 2)

                def col(v, t, d, hd):
                    return v[:, t, d, bass.ds(2 * i + hd.x, 1)]
                def differences(hd, dst, bound):
                    for t, d in unit:
                        last = V.tensor_scalar(dst[:, t, d], hd.units(0)[:, t, d], col(gc, t, d, hd), 0.0, ALU.subtract, bound)
                    last.then_inc(dn_diff, 1)
                for hd in heads:
                    dve.wait_ge(dn_gcb, hd.of(i))
                    differences(hd, hd.eN, ALU.max)
                for hd in heads:
                    dve.wait_ge(dn_kk, hd.of(i))
                    dve.wait_ge(dn_eN, hd.of(i))
                    for t, d in unit:
                        last = V.scalar_tensor_tensor(hd.m[:, t, d], hd.at(1, t), col(beta, t, d, hd), hd.eN[:, t, d], ALU.mult, ALU.mult)
                    last.then_inc(dn_m, 1)
                    dve.wait_ge(dn_m, hd.of(i))
                    step(V.tensor_tensor(hd.gs, hd.m, level[:, 0].unsqueeze(1).to_broadcast([P, TT, 2, P]), ALU.mult))
                    V.tensor_tensor(hd.t.rearrange("p t d s -> p (t d) s"), ident[:].unsqueeze(1).to_broadcast([P, 2 * TT, P]),
                                    hd.gs.rearrange("p t d s -> p (t d) s"), ALU.subtract).then_inc(dn_t, 1)
                for hd in heads:
                    differences(hd, hd.eT, ALU.min)
                for k in range(1, LEVELS):
                    for hd in heads:
                        dve.wait_ge(dn_rz, hd.of(i, LEVELS - 1, k - 1))
                        V.tensor_tensor(hd.r, hd.r, hd.units(2), ALU.subtract).then_inc(dn_r, 1)
                        if k < LEVELS - 1:
                            dve.wait_ge(dn_tz, hd.of(i, LEVELS - 2, k - 1))
                            V.tensor_tensor(hd.t, hd.t, hd.units(0), ALU.subtract).then_inc(dn_t, 1)
                    if k == 2:
                        for hd in heads:
                            dve.wait_ge(dn_eTm, hd.of(i))
                            for t in range(TT):
                                qk = hd.at(1, TT + t).unsqueeze(1).to_broadcast([P, 2, P])
                                last = V.tensor_tensor(hd.eT[:, t], qk, hd.eT[:, t], ALU.mult)
                            last.then_inc(dn_qkm, 1)
                for hd in heads:
                    dve.wait_ge(dn_uw, hd.of(i))
                    V.tensor_copy(flat(hd.u), hd.bank[3][:]).then_inc(dn_u, 1)
                for n in range(steps):
                    for hd in heads:
                        if n:
                            dve.wait_ge(dn_ws, hd.of(i, steps - 1, n - 1))
                            for d in range(2):
                                c, t, r = rows_of(n, d)
                                last = V.tensor_tensor(hd.vn[r, d], hd.u[r, t, d], hd.bank[0][r, d * P:(d + 1) * P], ALU.subtract)
                            last.then_inc(dn_vn, 1)
                    for hd in heads:
                        dve.wait_ge(dn_so, hd.of(i, steps, n))
                        if n < steps - 1:
                            for d in range(2):
                                c, t, r = rows_of(n, d)
                                if n == 0:
                                    last = V.tensor_copy(hd.s[:, d], hd.at(2 + d, 0))
                                else:
                                    last = V.scalar_tensor_tensor(hd.s[:, d], hd.s[:, d], gl[:, c, d, bass.ds(2 * i + hd.x, 1)],
                                                                  hd.at(2 + d, 0), ALU.mult, ALU.add)
                            last.then_inc(dn_s, 1)
                        for d in range(2):
                            c, t, r = rows_of(n, d)
                            o = qkv2[r, t, bass.ds(i * (2 * DND) + hd.x * DND, DND)]
                            b = hd.bank[1][r, d * P:(d + 1) * P]
                            if n < steps // 2:
                                last = V.tensor_copy(o, b)
                            else:
                                last = V.tensor_tensor(o, o, b, ALU.add)
                        if n == steps - 1:
                            last.then_inc(dn_free, 1)
                step.leave(DNH // 2)
            split(Q_MIX)

            def fourier_lo(g):
                dve.wait_ge(fr_hi_ready, g + 1)
                V.tensor_tensor(fr_lo[:, g], bank[6 + g % 2][:, 0:SEQ], fr_hi[:, g].bitcast(F32), ALU.subtract).then_inc(fr_lo_ready, 1)
            for t in range(TT):
                dve.wait_ge(o_sq, t + 1)
                V.tensor_reduce(dn_ss[:, t, 0:DNH], mix[:, t, 0:DNW].rearrange("p (a d) -> p a d", d=DND), AX.X, ALU.add).then_inc(o_summed, 1)
            for g in range(DNH // 2):
                fourier_lo(g)
            for t in range(TT):
                dve.wait_ge(o_rstd, t + 1)
                o = qkv2[:, t, 0:DNW].rearrange("p (a d) -> p a d", d=DND)
                step(V.tensor_tensor(o, o, dn_rs[:, t, 0:DNH].unsqueeze(2).to_broadcast([P, DNH, DND]), ALU.mult))
                dve.wait_ge(z2_scaled, t + 1)
                V.tensor_tensor(qkv2[:, t, 0:DNW], qkv2[:, t, 0:DNW], z2[:, t], ALU.mult).then_inc(y_ready, 1)
                fourier_lo(DNH // 2 + t)
            for g in range(DNH // 2 + TT, DNH):
                fourier_lo(g)
            for n in range(4):
                dve.wait_ge(y_hi_ready, n + 1)
                V.tensor_tensor(y_lo[:, 2 * n:2 * n + 2].rearrange("p k s -> p (k s)"), bank[4 + n][:],
                                y_hi[:, 2 * n:2 * n + 2].rearrange("p k s -> p (k s)").bitcast(F32), ALU.subtract).then_inc(y_lo_ready, 1)

            with dve.Fori(0, D // NC) as n:
                step.enter(n, 1)
                q = Q_MIX + 6 * n
                for k in range(1, 5):
                    split(q + k)
                for k, p in enumerate((2, 3)):
                    split(q + 5 + k, 0, QUAD - 1)
                    dve.wait_ge(slab_done, QUAD * (q + 5 + k))
                    dve.wait_ge(pair_free[p - 2], 2 * (U_MIX + n + 1) + 2)
                    for t in range(TT):
                        last = V.tensor_tensor(fr[:, t, k * NC:(k + 1) * NC], z2[:, t, k * NC:(k + 1) * NC], pair[p][t][:],
                                               ALU.mult).then_inc(pair_free[p], 1)
                    split(q + 5 + k, QUAD - 1)
                dve.wait_ge(pair_free[3], 2 * (V_MIX + n + 1) + 2)
                dve.wait_ge(pair_free[2], 2 * (V_MIX + n + 1) + 2)
                step(V.tensor_tensor(mix[:, 0, bass.ds(n * NC, NC)], fr[:, 0, 0:NC], fr[:, 0, NC:], ALU.add))
                V.tensor_tensor(mix[:, 1, bass.ds(n * NC, NC)], fr[:, 1, 0:NC], fr[:, 1, NC:], ALU.add).then_inc(mix_ready, 1)
                step.leave(D // NC)
            rest_of_operand(TR_WO2)
            project_into_h(Q_WO2)

            normalized_operand(xn_m, 5, G_MLP, TR_MLP, Q_MLP + 1)

            def mlp_evac(q, p):
                dve.wait_ge(slab_done, QUAD * (q + 2))
                V.tensor_copy(m_stage[:, 1], pair[p][1][:]).then_inc(pair_free[p], 1)

            def mlp_gated(j):
                for b in range(2):
                    half = slice(2 * b, 2 * b + 2)
                    dve.wait_ge(ff_silu, N_FF + 2 * j + b + 1)
                    V.tensor_tensor(m_act[:, half].rearrange("p k s -> p (k s)"), m_relu[:, half].rearrange("p k s -> p (k s)"),
                                    bank[6 + b][:], ALU.mult).then_inc(ff_mul, 1)
                for b in range(2):
                    half = slice(2 * b, 2 * b + 2)
                    dve.wait_ge(ff_mul, N_FF + 2 * j + b + 1)
                    dve.wait_ge(ff_hi, N_FF + 2 * j + b + 1)
                    V.tensor_tensor(m_lo[:, half], m_act[:, half], m_hi[:, half].bitcast(F32), ALU.subtract).then_inc(ff_lo, 1)

            def mlp_down(q, quads, last=False):
                for n in range(D // NC):
                    if n // 2 < quads:
                        split(q + 1 + n // 2, 2 * (n % 2), 2 * (n % 2) + 2)
                    if last and n:
                        dve.wait_ge(gain_loaded, 16 * (G_OUT + 1))
                        dve.wait_ge(stat_ready, TT * DC * 6 + TT * n)
                        cols = slice((n - 1) * NC, n * NC)
                        V.tensor_tensor(h[:, :, cols], h[:, :, cols], gain[:, cols].unsqueeze(1).to_broadcast([P, TT, NC]),
                                        ALU.mult).then_inc(normed, 1)
                    dve.wait_ge(slab_done, QUAD * q + 2 * (n + 1))
                    add_to_h(n % 2, slice(n * NC, (n + 1) * NC))

            q = Q_MLP
            split(q + 2)
            mlp_evac(q, 0)
            with dve.Fori(0, N_FF2 - 1) as j:
                q = Q_MLP + 2 + 4 * j
                mlp_gated(j)
                split(q + 1)
                split(q + 2)
                mlp_evac(q, 2)
                mlp_down(q + 2, 2)
            mlp_gated(N_FF2 - 1)
            mlp_down(N_QUADS - 2, 1, last=True)
            mean_square(6)
            dve.wait_ge(rstd_ready, 2 * 7)
            for c in range(DC // 2, DC):
                cols = slice(c * NC, (c + 1) * NC)
                for t in range(TT):
                    if c < DC - 1:
                        last = V.tensor_scalar(xn_m[:, t, cols], h[:, t, cols], rstd[:, t:t + 1], None, ALU.mult)
                    else:
                        last = V.scalar_tensor_tensor(xn_m[:, t, cols], h[:, t, cols], rstd[:, t:t + 1], gain[:, cols], ALU.mult, ALU.mult)
                last.then_inc(normed, 1)
        @block.tensor
        def _(pe):
            T = nc.tensor

            def slab(q, s, products, psum, start, stop):
                pe.wait_ge(lo_ready, QUAD * q + s + 1)
                for j, (left_hi, left_lo) in enumerate(products):
                    wh = w_hi[:, s, j * NC:(j + 1) * NC]
                    wl = w_lo[:, s, j * NC:(j + 1) * NC]
                    for t in range(TT):
                        ts = slice(t * P, (t + 1) * P)
                        first = start and j == 0
                        final = stop and j == SLAB_KT - 1
                        T.matmul(psum[t][:], left_hi[:, ts], wh, start=first, stop=False)
                        T.matmul(psum[t][:], left_hi[:, ts], wl, start=False, stop=False)
                        last = T.matmul(psum[t][:], left_lo[:, ts], wh, start=False, stop=final)
                last.then_inc(slab_done, 1)

            def chunk(q, p, use, left_hi, left_lo, k_tiles=KT, between=None):
                pe.wait_ge(pair_free[p], 2 * (use + 1))
                for n in range(k_tiles // SLAB_KT):
                    if between and n in between:
                        between[n]()
                    k = n * SLAB_KT
                    slab(q + n // QUAD, n % QUAD, [(left_hi[:, k + j], left_lo[:, k + j]) for j in range(SLAB_KT)],
                         pair[p], n == 0, n == k_tiles // SLAB_KT - 1)

            def operand_tiles(n, src, ready, i):
                if i % 2 == 0:
                    ready(i // 2)
                if i >= 4:
                    pe.wait_ge(a_lo_ready, KT // 2 * n + i - 3)
                for k in range(2):
                    for t in range(TT):
                        last = T.transpose(bank[4 + i % 4][:, k * SEQ + t * P:k * SEQ + (t + 1) * P],
                                           src[:, t, (2 * i + k) * P:(2 * i + k + 1) * P], ident[:])
                last.then_inc(tr_ready, 1)

            def transpose_operand(n, src, ready):
                for i in range(KT // 2):
                    operand_tiles(n, src, ready, i)
                pe.wait_ge(a_lo_ready, KT // 2 * (n + 1))

            def first_chunk(n, src, ready, q, p, use, complete=False):
                for i in range(4 if complete else 3):
                    operand_tiles(n, src, ready, i)

                def tiles_of(s):
                    if complete and s + 4 < KT // 2:
                        operand_tiles(n, src, ready, s + 4)
                    if not complete and 1 <= s < KT // 2 - 2:
                        operand_tiles(n, src, ready, s + 2)
                    pe.wait_ge(a_lo_ready, KT // 2 * n + s + 1)
                chunk(q, p, use, a_hi, a_lo, between={s: lambda s=s: tiles_of(s) for s in range(KT // SLAB_KT)})

            def norm_chunk(g):
                return lambda c: pe.wait_ge(normed, NORMED[g] - TT * (DC - 1 - c))

            def narrow(psum, hi, lo, width, done, token_major, transposed):
                o = psum[0:width, 0:SEQ]
                for k in range(KT):
                    T.matmul(o, hi[:, k], a_hi[:, k], start=k == 0, stop=False)
                    T.matmul(o, lo[:, k], a_hi[:, k], start=False, stop=False)
                    last = T.matmul(o, hi[:, k], a_lo[:, k], start=False, stop=k == KT - 1)
                last.then_inc(done, 1)
                pe.wait_ge(narrow_copied, transposed)
                for t in range(TT):
                    last = T.transpose(psum[:, SEQ + t * width:SEQ + (t + 1) * width], token_major[:, t * P:(t + 1) * P],
                                       ident[0:width, 0:width])
                return last

            def project_into_h(q0, use, n, src, ready):
                first_chunk(n, src, ready, q0, 0, use, complete=True)
                for c in range(1, DC):
                    chunk(q0 + 2 * c, c % 2, use + c // 2, a_hi, a_lo)

            def project(q0, use, chunks):
                with pe.Fori(0, chunks // 2) as i:
                    for par in range(2):
                        chunk(q0 + 4 * i + 2 * par, par, use + i, a_hi, a_lo)

            def to_channels(src, col0, first):
                for ct in range(4):
                    for t in range(TT):
                        last = T.transpose(bank[first + ct // 2][:, (ct % 2) * SEQ + t * P:(ct % 2) * SEQ + (t + 1) * P],
                                           src[:, t, col0 + ct * P:col0 + (ct + 1) * P], ident[:])
                return last

            def to_tokens(src, tiles):
                for t in range(tiles):
                    for ct in range(4):
                        last = T.transpose(bank[6 + t][:, ct * P:(ct + 1) * P], src[:, ct, t * P:(t + 1) * P], ident[:])
                return last

            first_chunk(TR_ATTN, xs, norm_chunk(G_ATTN), Q_XBC, 0, U_XBC)
            pe.wait_ge(w32_lo_ready, 1)
            narrow(bank[7], w32_hi, w32_lo, HEADS, dt_mm, narrow_T, 1).then_inc(dt_t, 1)
            with pe.Fori(0, 2) as i:
                for k in range(2):
                    c, par = 2 * i + k, (1 + k) % 2

                    def channels():
                        pe.wait_ge(pair_free[1 - par], 2 * (U_XBC + i + 1) + 2)
                        to_channels(stage[:, 1 - par], 0, 4).then_inc(xbc_t, 1)
                    chunk(Q_XBC + 2 * (2 * i + 1 + k), par, U_XBC + i + k, a_hi, a_lo, between={2: channels})
                    pe.wait_ge(silu_done, c + 1)
                    pe.wait_ge(back0_evac, c + 1)
                    pe.wait_ge(back1_evac, c + 1)
                    pe.wait_ge(adt_ready, 1)
                    to_tokens(cv_act, TT).then_inc(xbc_back, 1)

            def channels_of_b():
                pe.wait_ge(pair_free[0], 2 * (U_Z) + 2)
                to_channels(stage[:, 0], 0, 4).then_inc(xbc_t, 1)
            chunk(Q_XBC + 10, 1, U_XBC + 2, a_hi, a_lo, between={2: channels_of_b})
            pe.wait_ge(silu_done, 5)
            pe.wait_ge(back0_evac, 4 + 1)
            pe.wait_ge(back1_evac, 4 + 1)
            to_tokens(bT, 1).then_inc(xbc_back, 1)
            pe.wait_ge(pair_free[1], 2 * (U_Z) + 2)
            to_channels(stage[:, 1], 0, 4).then_inc(xbc_t, 1)

            project(Q_Z, U_Z, D // NC)

            pe.wait_ge(silu_done, 6)
            for t in range(TT):
                T.matmul(bank[4][:, t * HEADS:(t + 1) * HEADS], before[:], adt[:, t], start=True, stop=True)
            T.matmul(bank[4][:, TT * HEADS:(TT + 1) * HEADS], ones[:], adt[:, 0], start=True, stop=True).then_inc(acs_mm, 1)
            for g in range(GROUPS):
                for t in range(TT):
                    ts = slice(t * P, (t + 1) * P)
                    c = (TT * g + t) * P
                    last = T.matmul(bank[5 + c // NC][:, c % NC:c % NC + P], bT[:, g, ts], cT[:, g, ts], start=True, stop=True)
            last.then_inc(cb_mm, 1)
            chunk(Q_QKV, 0, U_QKV, a_hi, a_lo)
            pe.wait_ge(cb_ready, 1)
            for g in range(GROUPS):
                def decay_rows(t):
                    n = TT * g + t
                    pe.wait_ge(row_scaled, n + 1)
                    if n:
                        pe.wait_ge(seg_ready, n)
                    for b in range(2):
                        last = T.matmul(bank[4 + b][:], ones[:], ssm_rows[:, 4 * b:4 * b + 4].rearrange("p a s -> p (a s)"),
                                        start=True, stop=True)
                    last.then_inc(row_mm, 1)

                def within(t):
                    n = TT * g + t
                    pe.wait_ge(seg_w, n + 1)
                    if n:
                        pe.wait_ge(y_gated, n)
                    for a in range(HPG):
                        cols = slice(a * HD, (a + 1) * HD)
                        last = T.matmul(bank[7][:, cols], ssm_w[:, a], ssm_xd[:, t, cols], start=True, stop=True)
                    last.then_inc(ydiag_mm, 1)

                def state():
                    pe.wait_ge(xds_ready, g + 1)
                    if g:
                        pe.wait_ge(y_gated, TT * g)
                    T.matmul(bank[6][:], b_tok[:, g], ssm_xds, start=True, stop=True).then_inc(state_mm, 1)

                def of_state():
                    pe.wait_ge(state_evac, g + 1)
                    T.matmul(bank[6][:], cT[:, g, P:2 * P], ssm_state, start=True, stop=True).then_inc(yoff_mm, 1)

                def second_tile():
                    within(0)
                    decay_rows(1)
                c = g + 1
                chunk(Q_QKV + 2 * c, c % 2, U_QKV + c // 2, a_hi, a_lo,
                      between={0: lambda: decay_rows(0), 1: state, 3: second_tile, 4: of_state, 6: lambda: within(1)})
            chunk(Q_QKV + 10, 1, U_QKV + 2, a_hi, a_lo)
            transpose_operand(TR_YSSM, z, norm_chunk(G_SSM))
            pe.wait_ge(pair_free[1], 2 * (U_WOS + 1))

            with pe.Fori(0, D // NC // 2) as i2:
                for k in range(2):
                    i = 2 * i2 + k

                    def qk_transposed():
                        pe.wait_ge(att_staged, i + 1)
                        for t in range(TT):
                            for a in range(REP):
                                T.transpose(bank[4 + t][:, a * P:(a + 1) * P], att_q[:, t, a].rearrange("p b d -> p (b d)"), ident[:])
                        for t in range(TT):
                            last = T.transpose(bank[6][:, t * P:(t + 1) * P], att_k[:, t], ident[:])
                        last.then_inc(att_qkT, 1)

                    def scores(par):
                        rows = slice(par * HD, (par + 1) * HD)
                        if par == 0:
                            pe.wait_ge(att_qkT_evac, 3 * i + 6)
                        else:
                            pe.wait_ge(att_masked, 2 * i + 1)
                        for a in range(REP):
                            T.matmul(bank[4][:, a * P:(a + 1) * P], att_qT[rows, 0, a], att_kT[rows, 0:P], start=True, stop=True)
                        for a in range(REP):
                            last = T.matmul(bank[5 + a // 2][:, (a % 2) * SEQ:(a % 2 + 1) * SEQ], att_qT[rows, 1, a],
                                            att_kT[rows, 0:SEQ], start=True, stop=True)
                        last.then_inc(att_scored, 1)

                    def probs_transposed(par):
                        p = att_p[par]
                        pe.wait_ge(att_masked, 2 * i + 2)
                        pe.wait_ge(att_exp, 2 * i + par + 1)
                        for a in range(REP):
                            T.transpose(bank[4][:, a * P:(a + 1) * P], p[:, a * P:(a + 1) * P], ident[:])
                        for a in range(REP):
                            for b in range(2):
                                c = (2 * a + b) * P
                                last = T.transpose(bank[5 + c // NC][:, c % NC:c % NC + P], p[:, NC + c:NC + c + P], ident[:])
                        last.then_inc(att_pT, 1)

                    def values(par):
                        pe.wait_ge(att_pT_evac, 6 * i + 3 * par + 3)
                        if par:
                            pe.wait_ge(att_done, 2 * i + 1)
                        for a in range(REP):
                            v = [qkv[:, t, bass.ds(i2 * (4 * HD) + (HEADS + KVH) * HD + (2 * k + par) * HD, HD)] for t in range(TT)]
                            T.matmul(bank[7][:, a * HD:(a + 1) * HD], att_pTs[:, a * P:(a + 1) * P], v[0], start=True, stop=True)
                            o = bank[7][:, (REP + a) * HD:(REP + a + 1) * HD]
                            for b in range(TT):
                                c = NC + (2 * a + b) * P
                                last = T.matmul(o, att_pTs[:, c:c + P], v[b], start=b == 0, stop=b == TT - 1)
                        last.then_inc(att_pv, 1)
                    chunk(Q_WOS + 4 * i2 + 2 * k, k, U_WOS + i2, a_hi, a_lo,
                          between={1: qk_transposed, 2: lambda: scores(0), 3: lambda: scores(1), 5: lambda: probs_transposed(0),
                                   6: lambda: values(0), 7: lambda: probs_transposed(1)})
                    values(1)
            pe.wait_ge(att_done, KVH)
            project_into_h(Q_WOA, U_WOA, TR_YATT, qkv, lambda c: None)

            def ff_down(q, use, between=None):
                for n in range(D // NC):
                    if between and n == 1:
                        between()
                    pe.wait_ge(pair_free[n % 2], 2 * (use + n // 2 + 1))
                    for s in range(2):
                        slab(q + n // 2, 2 * (n % 2) + s, [(f_hi[:, 2 * s + k], f_lo[:, 2 * s + k]) for k in range(SLAB_KT)],
                             pair[n % 2], s == 0, s == 1)

            def ff_channels(use):
                for p in range(2):
                    pe.wait_ge(pair_free[p], 2 * (use + 1))
                to_channels(f_stage, 0, 4)
                to_channels(f_stage, FFB, 6).then_inc(ff_t, 1)

            first_chunk(TR_FFN, xn_f, norm_chunk(G_FFN), Q_FF, 0, U_FF)
            chunk(Q_FF + 2, 1, U_FF, a_hi, a_lo)
            ff_channels(U_FF + 1)
            with pe.Fori(0, N_FF - 1) as j:
                q, use = Q_FF + 4 + 6 * j, U_FF + 1 + 3 * j
                chunk(q, 0, use, a_hi, a_lo)
                chunk(q + 2, 1, use, a_hi, a_lo)
                pe.wait_ge(ff_lo, j + 1)
                ff_down(q + 4, use + 1, between=lambda: ff_channels(use + 1))
            pe.wait_ge(small2_loaded, 3 * 16)
            for n in range(DC):
                pe.wait_ge(pair_free[n % 2], 2 * (U_PLE + n // 2 + 1))
                for t in range(TT):
                    for k in range(PLE // P):
                        last = T.matmul(pair[n % 2][t][:], p_T[:, k, t * P:(t + 1) * P], w_proj[:, k, n * NC:(n + 1) * NC],
                                        start=k == 0, stop=k == PLE // P - 1)
                last.then_inc(ple_mm, 1)
            pe.wait_ge(ff_lo, N_FF)
            ff_down(Q_GATE - 2, U_GATE - 2)

            first_chunk(TR_PLE, xn_f, norm_chunk(G_PLE), Q_GATE, 0, U_GATE)
            for n in range(1, DC):
                if n >= 2:
                    pe.wait_ge(sig_ready, TT * (n - 1))
                chunk(Q_GATE + 2 * n, n % 2, U_GATE, a_hi, a_lo)

            pe.wait_ge(sig_ready, TT * DC)
            first_chunk(TR_MIX2, qkv2, norm_chunk(G_MIX2), Q_QKV2, 0, U_QKV2)
            with pe.Fori(0, 3) as i:
                for k in range(2):
                    c, par = 2 * i + k, (1 + k) % 2

                    def channels2():
                        pe.wait_ge(pair_free[1 - par], 2 * (U_QKV2 + i + 1) + 2)
                        to_channels(s_stage[:, 1 - par], 0, 4).then_inc(qkv2_t, 1)
                    chunk(Q_QKV2 + 2 * (2 * i + 1 + k), par, U_QKV2 + i + k, a_hi, a_lo, between={2: channels2})
                    pe.wait_ge(silu2_done, c + 1)
                    pe.wait_ge(back2_evac0, c + 1)
                    pe.wait_ge(back2_evac1, c + 1)
                    to_tokens(s_act, TT).then_inc(qkv2_back, 1)
            pe.wait_ge(s_lo_ready, 1)
            narrow(bank[5], s_hi, s_lo, 4 * DNH, sc_mm, narrow2_T, 2).then_inc(sc_t, 1)
            chunk(Q_F + 2, 1, U_F, a_hi, a_lo)
            chunk(Q_Z2, 0, U_Z2, a_hi, a_lo)
            pe.wait_ge(g2_ready, 1)
            for t in range(TT):
                for d in range(2):
                    c = (2 * t + d) * DNH
                    T.matmul(bank[4][:, c:c + DNH], cum[:, d], g2[:, t, d], start=True, stop=True)
                    T.matmul(bank[4][:, 32 + c:32 + c + DNH], rest[:, d], g2[:, t, d], start=True, stop=True)
                for b in range(P // CHUNK):
                    c = 64 + (2 * t + b) * 2 * DNH
                    last = T.matmul(bank[4][:, c:c + 2 * DNH], chunk_ones[:, b], g2[:, t].rearrange("p d a -> p (d a)"),
                                    start=True, stop=True)
            last.then_inc(gc_mm, 1)
            chunk(Q_Z2 + 2, 1, U_Z2, a_hi, a_lo)
            pe.wait_ge(dn_qk_normed, TT)
            pe.wait_ge(dn_pre, 1)
            for n in range(8):
                if n >= 4:
                    pe.wait_ge((dn_qkT_evac0, dn_qkT_evac1)[n % 2], n // 2 - 1)
                for a in range(2):
                    for t in range(TT):
                        last = T.transpose(bank[4 + n % 4][:, a * SEQ + t * P:a * SEQ + (t + 1) * P],
                                           qkv2[:, t, (2 * n + a) * P:(2 * n + a + 1) * P], ident[:])
                last.then_inc(dn_qkT, 1)

            steps = SEQ // CHUNK
            unit = [(t, d) for t in range(TT) for d in range(2)]
            pe.wait_ge(dn_qkT_evac0, 4)
            pe.wait_ge(dn_qkT_evac1, 4)
            with pe.Fori(0, DNH // 2) as i:
                for hd in heads:
                    pe.wait_ge(dn_rows, hd.of(i))
                    T.matmul(hd.bank[0][:], ones[:], flat(hd.gs), start=True, stop=True).then_inc(dn_gcb, 1)
                for hd in heads:
                    pe.wait_ge(dn_qk, hd.of(i))
                    pe.wait_ge(dn_free, hd.of(i))
                    for a in (1, 0):
                        for t in range(TT):
                            ts = slice(t * P, (t + 1) * P)
                            last = T.matmul(hd.at(1, TT * (1 - a) + t), hd.qk[:, 1, ts], hd.qk[:, a, ts], start=True, stop=True)
                    last.then_inc(dn_kk, 1)
                for hd in heads:
                    pe.wait_ge(dn_t, hd.of(i, LEVELS - 1, 0))
                    for n, (t, d) in enumerate(unit):
                        last = T.transpose(hd.at(2, n), hd.t[:, t, d], ident[:])
                    last.then_inc(dn_rT, 1)
                for k in range(1, LEVELS):
                    for hd in heads:
                        pe.wait_ge(dn_mk, hd.of(i, LEVELS - 1, k - 1))
                        if k == 1:
                            pe.wait_ge(dn_r0, hd.of(i))
                        else:
                            pe.wait_ge(dn_r, hd.of(i, LEVELS - 1, k - 2))
                        for n, (t, d) in enumerate(unit):
                            last = T.matmul(hd.at(3, n), hd.mk[:, t, d], hd.r[:, t, d], start=True, stop=True)
                        last.then_inc(dn_z, 1)
                    for hd in heads:
                        pe.wait_ge(dn_zz, hd.of(i, LEVELS - 1, k - 1))
                        pe.wait_ge(dn_t, hd.of(i, LEVELS - 1, k - 1))
                        for n, (t, d) in enumerate(unit):
                            last = T.matmul(hd.at(2, n), hd.t[:, t, d], hd.zz[:, t, d], start=True, stop=True)
                        last.then_inc(dn_rz, 1)
                        if k == 1:
                            pe.wait_ge(dn_egb, hd.of(i))
                        if k < LEVELS - 1:
                            for n, (t, d) in enumerate(unit):
                                last = T.matmul(hd.at(0, n), hd.zz[:, t, d], hd.t[:, t, d], start=True, stop=True)
                            last.then_inc(dn_tz, 1)
                for hd in heads:
                    pe.wait_ge(dn_in, hd.of(i))
                    pe.wait_ge(dn_r, hd.of(i, LEVELS - 1, LEVELS - 2))
                    for n, (t, d) in enumerate(unit):
                        T.matmul(hd.at(3, n), hd.r[:, t, d], hd.vb[:, t, d], start=True, stop=True)
                        last = T.matmul(hd.at(2, n), hd.kb[:, t, d], hd.r[:, t, d], start=True, stop=True)
                    last.then_inc(dn_uw, 1)
                for n in range(steps):
                    for hd in heads:
                        if n:
                            pe.wait_ge(dn_s, hd.of(i, steps - 1, n - 1))
                            for d in range(2):
                                c, t, r = rows_of(n, d)
                                last = T.matmul(hd.bank[0][r, d * P:(d + 1) * P], hd.wT[:, t, d, r], hd.s[:, d], start=True, stop=True)
                            last.then_inc(dn_ws, 1)
                    for hd in heads:
                        if n:
                            pe.wait_ge(dn_vn, hd.of(i, steps - 1, n - 1))
                        else:
                            for place in (dn_u, dn_wT, dn_qkm, dn_qd):
                                pe.wait_ge(place, hd.of(i))
                        for d in range(2):
                            c, t, r = rows_of(n, d)
                            v = hd.vn[r, d] if n else hd.u[r, t, d]
                            if n < steps - 1:
                                T.matmul(hd.at(2 + d, 0), hd.kd[r, t, d], v, start=True, stop=True)
                            o = hd.bank[1][r, d * P:(d + 1) * P]
                            if n:
                                T.matmul(o, hd.qd[:, t, d, r], hd.s[:, d], start=True, stop=False)
                            last = T.matmul(o, hd.eT[r, t, d, r], v, start=n == 0, stop=True)
                        last.then_inc(dn_so, 1)
            pe.wait_ge(small4_loaded, 16)
            pe.wait_ge(fr_ready, 1)
            for g in range(DNH + 1):
                if g < DNH:
                    for c in range(2):
                        for t in range(TT):
                            last = T.matmul(bank[4 + g % 2][:, c * SEQ:(c + 1) * SEQ], fr[:, t, g * P:(g + 1) * P], dft_t[:, c, t],
                                            start=t == 0, stop=t == TT - 1)
                    last.then_inc(f_mm, 1)
                if g:
                    pe.wait_ge(f_half_ready, g)
                    if g >= 3:
                        pe.wait_ge(fr_lo_ready, g - 2)
                    for c in range(2):
                        last = T.matmul(bank[6 + (g - 1) % 2][:, 0:SEQ], dft_d[:, c], f_half[:, (g - 1) % 2, c], start=c == 0, stop=c == 1)
                    last.then_inc(f_out, 1)

            pe.wait_ge(fr_lo_ready, DNH)
            pe.wait_ge(y_ready, TT)
            for n in range(4):
                for a in range(2):
                    for t in range(TT):
                        last = T.transpose(bank[4 + n][:, a * SEQ + t * P:a * SEQ + (t + 1) * P],
                                           qkv2[:, t, (2 * n + a) * P:(2 * n + a + 1) * P], ident[:])
                last.then_inc(y_t, 1)
            pe.wait_ge(y_lo_ready, 4)


            with pe.Fori(0, D // NC) as n:
                q = Q_MIX + 6 * n
                chunk(q, 0, U_MIX + n, a_hi, a_lo)
                chunk(q + 2, 1, U_MIX + n, a_hi, a_lo)
                chunk(q + 4, 2, V_MIX + n, fr_hi, fr_lo, DNH)
                chunk(q + 5, 3, V_MIX + n, y_hi, y_lo, DNH)
            for p in (2, 3):
                pe.wait_ge(pair_free[p], 2 * (V_MIX + DC + 1))
            project_into_h(Q_WO2, U_WO2, TR_WO2, mix, lambda c: pe.wait_ge(mix_ready, c + 1))

            first_chunk(TR_MLP, xn_m, norm_chunk(G_MLP), Q_MLP, 0, U_MLP)

            def mlp_down(q, use):
                for n in range(D // NC):
                    pe.wait_ge(pair_free[n % 2], 2 * (use + n // 2 + 2 - n % 2))
                    for s in range(2):
                        slab(q + n // 2, 2 * (n % 2) + s, [(m_hi[:, 2 * s + k], m_lo[:, 2 * s + k]) for k in range(SLAB_KT)],
                             pair[n % 2], s == 0, s == 1)

            def mlp_channels():
                to_channels(m_stage, 0, 6).then_inc(ff_t, 1)

            pe.wait_ge(pair_free[0], 2 * (U_MLP + 2))
            mlp_channels()
            with pe.Fori(0, N_FF2 - 1) as j:
                q = Q_MLP + 2 + 4 * j
                chunk(q, 2, V_MLP + j, a_hi, a_lo)
                pe.wait_ge(ff_lo, N_FF + 2 * j + 2)
                mlp_down(q + 2, U_MLP + 2 * j)
                pe.wait_ge(pair_free[2], 2 * (V_MLP + j + 2))
                mlp_channels()
            pe.wait_ge(ff_lo, N_FF + 2 * N_FF2)
            mlp_down(N_QUADS - 2, U_MLP + 2 * (N_FF2 - 1))


def _slabs(w, k_major=False):
    k, n = w.shape
    s = w.reshape(k // (SLAB_KT * P), SLAB_KT, P, n // NC, NC).transpose(3, 0, 2, 1, 4)
    return s.reshape(-1, P, SLAB_KT * NC)


def _stream(a):
    w_in, w_out, w_up, w_down = a["w_in"][0], a["w_out"][0], a["w_up"][0], a["w_down"][0]
    w_in2, up2, down2 = a["w_in_2"][0], a["w_mlp_up_2"][0], a["w_mlp_down_2"][0]
    o_xbc, o_dt = D, D + XBC_W
    o_q = o_dt + HEADS
    parts = [_slabs(w_in[:, o_xbc:o_dt]), _slabs(w_in[:, :D]), _slabs(w_in[:, o_q:]),
             _slabs(w_out[:D]), _slabs(w_out[D:])]
    for j in range(N_FF + 1):
        if j < N_FF:
            parts += [_slabs(w_up[:, j * FFB:(j + 1) * FFB]), _slabs(w_up[:, D_FF + j * FFB:D_FF + (j + 1) * FFB])]
        if j:
            parts.append(_slabs(w_down[(j - 1) * FFB:j * FFB]))
    parts.append(_slabs(a["w_ple_gate"][0]))
    o_z, o_f = 3 * DNW, 4 * DNW
    o_sc = o_f + DNW
    o_ga = o_sc + 4 * DNH
    o_gf = o_ga + D
    parts += [_slabs(w_in2[:, :o_z]), _slabs(w_in2[:, o_f:o_sc]), _slabs(w_in2[:, o_z:o_f])]
    for n in range(D // NC):
        c = slice(n * NC, (n + 1) * NC)
        parts += [_slabs(w_in2[:, o_gf:][:, c]), _slabs(w_in2[:, o_ga:o_gf][:, c]),
                  _slabs(a["w_fourier_2"][0][:, c]), _slabs(a["w_dn_up_2"][0][:, c])]
    parts.append(_slabs(a["w_o_2"][0]))
    for j in range(N_FF2 + 1):
        if j < N_FF2:
            parts.append(_slabs(up2[:, j * NC:(j + 1) * NC]))
        if j:
            parts.append(_slabs(down2[(j - 1) * NC:j * NC]))
    return np.concatenate(parts).reshape(N_QUADS, QUAD, P, SLAB_KT * NC)


def _small(a):
    def tiles(x):
        return np.ascontiguousarray(x.reshape(-1, P, x.shape[-1]).transpose(1, 0, 2))

    def columns(*rows):
        return tiles(np.concatenate(rows, 0).T)
    o_dt = D + XBC_W
    o_sc = 5 * DNW
    ff = columns(a["ffn_conv_w"][0], a["ffn_conv_b"])
    ff = ff.reshape(P, 2, N_FF, FFB // P, CONV_FF + 1).transpose(0, 2, 1, 3, 4).reshape(P, N_FF, -1, CONV_FF + 1)
    out = {
        "x_tok": tiles(a["x"][0]), "positions_tok": a["positions"].reshape(TT, P).T,
        "p_T": tiles(a["p"][0, 0].T), "w_dt": tiles(a["w_in"][0][:, o_dt:o_dt + HEADS]),
        "w_scal": tiles(a["w_in_2"][0][:, o_sc:o_sc + 4 * DNH]), "w_proj": tiles(a["w_ple_proj"][0]),
        "conv_col": columns(a["conv_w"][0], a["conv_b"]), "ff_col": ff, "conv2_col": columns(a["conv_w_2"][0]),
        "gains": np.stack([np.asarray(a[g]).reshape(D) for g in GAINS]),
        "row": np.concatenate([a[n].reshape(1, -1) for n in ROW], 1),
    }
    return {k: np.ascontiguousarray(v) for k, v in out.items()}


def build(nc):
    def dram(name, shape, dt=F32, kind="ExternalInput"):
        return nc.dram_tensor(name, tuple(shape), dt, kind=kind).ap()
    wstream = dram("weights", (N_QUADS, QUAD, P, SLAB_KT * NC))
    small = {n: dram(n, s, I32 if n == "positions_tok" else F32) for n, s in SMALL.items()}
    const = {n: dram("c_" + n, v.shape) for n, v in CONSTS.items()}
    out = dram("out", (TT, P, D), kind="ExternalOutput")
    program(nc, wstream, small, const, out)


def kernel(**inputs):
    import concourse.bacc as bacc
    from concourse.bass_utils import run_bass_kernel_spmd

    a = {k: np.asarray(v) for k, v in inputs.items()}
    nc = bacc.Bacc("TRN2", target_bir_lowering=False, num_devices=1)
    build(nc)
    arrays = {"weights": _stream(a), **_small(a), **{"c_" + n: v for n, v in CONSTS.items()}}
    r = run_bass_kernel_spmd(nc, [arrays], core_ids=[0])
    return r.results[0]["out"].reshape(1, SEQ, D)
```
